# Optimizing a Trainium2 kernel written in Bass

```python
import math
import jax, jax.numpy as jnp
from jax import lax
import numpy as np

D_MODEL = 1024
BATCH = 1
SEQ = 256
DEPTH = 2

GRID_W = 64
CTX_LEN = 256
N_MIXERS = 2
N_ATTN_LAYERS = (DEPTH + 1) // 2
N_HGRN_LAYERS = DEPTH // 2
EPS = 1e-6

HEAD_DIM = 64
N_HEADS = D_MODEL // HEAD_DIM
N_KV_HEADS = 4
GROUP = N_HEADS // N_KV_HEADS
WINDOW = 128
BLOCK = 128
ROPE_THETA = 10000.0
ATTN_IN_W = (N_HEADS + 2 * N_KV_HEADS) * HEAD_DIM

HG_EXPAND = 128
HG_HEADS = D_MODEL // HG_EXPAND
HG_DK = HG_EXPAND
HG_DV = D_MODEL // HG_HEADS
HG_DF = HG_HEADS * HG_DK
HG_CHUNK = 32
HG_SPLITS = [HG_DF, 2 * HG_DF, 3 * HG_DF, 3 * HG_DF + D_MODEL]
HG_IN_W = 3 * HG_DF + 2 * D_MODEL

D_FF = 2816
CONV_W = 3


def rms_norm(x, gain):
    xf = x.astype(jnp.float32)
    y = xf * lax.rsqrt(jnp.mean(xf * xf, axis=-1, keepdims=True) + EPS)
    return (y * gain.astype(jnp.float32)).astype(x.dtype)

def axial_angles(rows):
    row = jnp.repeat(jnp.arange(rows, dtype=jnp.float32), GRID_W)
    col = jnp.tile(jnp.arange(GRID_W, dtype=jnp.float32), rows)
    n_pairs = HEAD_DIM // 4
    inv = ROPE_THETA ** (-jnp.arange(n_pairs, dtype=jnp.float32) / n_pairs)
    return row[:, None] * inv, col[:, None] * inv

def rope_rotate(x, ang):
    x1, x2 = jnp.split(x, 2, axis=-1)
    cos = jnp.cos(ang)[None, :, None, :].astype(x.dtype)
    sin = jnp.sin(ang)[None, :, None, :].astype(x.dtype)
    return jnp.concatenate([x1 * cos - x2 * sin, x1 * sin + x2 * cos], axis=-1)

def apply_axial_rope(x, ang_r, ang_c):
    xr, xc = jnp.split(x, 2, axis=-1)
    return jnp.concatenate([rope_rotate(xr, ang_r), rope_rotate(xc, ang_c)], axis=-1)

def sink_softmax(scores, sink_g):
    s_sink = jnp.broadcast_to(sink_g[None, :, :, None, None].astype(jnp.float32), scores.shape[:-1] + (1,))
    p = jax.nn.softmax(jnp.concatenate([scores, s_sink], axis=-1), axis=-1)
    return p[..., :-1]

def attn_project(h, w_in, q_gain, k_gain):
    b, t, _ = h.shape
    q, k, v = jnp.split(h @ w_in, [N_HEADS * HEAD_DIM, (N_HEADS + N_KV_HEADS) * HEAD_DIM], axis=-1)
    q = rms_norm(q.reshape(b, t, N_HEADS, HEAD_DIM), q_gain)
    k = rms_norm(k.reshape(b, t, N_KV_HEADS, HEAD_DIM), k_gain)
    v = v.reshape(b, t, N_KV_HEADS, HEAD_DIM)
    return q, k, v

def windowed_gqa(hx, hc, w_in, w_out, q_gain, k_gain, sink, ang_r, ang_c, need_ctx_out):
    B, L, _ = hx.shape
    nb = L // BLOCK
    scale = HEAD_DIM ** -0.5
    qx, kx, vx = attn_project(hx, w_in, q_gain, k_gain)
    qc, kc, vc = attn_project(hc, w_in, q_gain, k_gain)
    qx = apply_axial_rope(qx, ang_r, ang_c)
    kx = apply_axial_rope(kx, ang_r, ang_c)
    kc_t = kc.transpose(0, 2, 1, 3)
    vc_t = vc.transpose(0, 2, 1, 3)
    pad = ((0, 0), (0, 0), (BLOCK, BLOCK), (0, 0))
    kx_p = jnp.pad(kx.transpose(0, 2, 1, 3), pad)
    vx_p = jnp.pad(vx.transpose(0, 2, 1, 3), pad)
    q_blocks = qx.reshape(B, nb, BLOCK, N_KV_HEADS, GROUP, HEAD_DIM).transpose(1, 0, 3, 4, 2, 5)
    sink_g = sink.reshape(N_KV_HEADS, GROUP)
    q_off = jnp.arange(BLOCK, dtype=jnp.int32)
    k_off = jnp.arange(3 * BLOCK, dtype=jnp.int32) - BLOCK

    def block(args):
        n, qb = args
        start = n * BLOCK
        kb = lax.dynamic_slice_in_dim(kx_p, start, 3 * BLOCK, axis=2)
        vb = lax.dynamic_slice_in_dim(vx_p, start, 3 * BLOCK, axis=2)
        qi = start + q_off
        kj = start + k_off
        valid = ((kj >= 0) & (kj < L))[None, :] & (jnp.abs(qi[:, None] - kj[None, :]) <= WINDOW)
        s_win = jnp.einsum('bkgqd,bkjd->bkgqj', qb, kb).astype(jnp.float32) * scale
        s_win = jnp.where(valid, s_win, -jnp.inf)
        s_ctx = jnp.einsum('bkgqd,bkcd->bkgqc', qb, kc_t).astype(jnp.float32) * scale
        p = sink_softmax(jnp.concatenate([s_win, s_ctx], axis=-1), sink_g).astype(vb.dtype)
        return (jnp.einsum('bkgqj,bkjd->bkgqd', p[..., :3 * BLOCK], vb)
                + jnp.einsum('bkgqc,bkcd->bkgqd', p[..., 3 * BLOCK:], vc_t))

    o = lax.map(block, (jnp.arange(nb, dtype=jnp.int32), q_blocks))
    ox = o.transpose(1, 0, 4, 2, 3, 5).reshape(B, L, N_HEADS * HEAD_DIM)
    yc = None
    if need_ctx_out:
        C = hc.shape[1]
        qcg = qc.reshape(B, C, N_KV_HEADS, GROUP, HEAD_DIM).transpose(0, 2, 3, 1, 4)
        s = jnp.einsum('bkgqd,bkcd->bkgqc', qcg, kc_t).astype(jnp.float32) * scale
        p = sink_softmax(s, sink_g).astype(vc.dtype)
        oc = jnp.einsum('bkgqc,bkcd->bkgqd', p, vc_t).transpose(0, 3, 1, 2, 4).reshape(B, C, N_HEADS * HEAD_DIM)
        yc = oc @ w_out
    return ox @ w_out, yc

def chunk_scan(q, k, g, v, s0, need_out):
    B, T, H, dk = q.shape
    dv = v.shape[-1]
    n = T // HG_CHUNK

    def to_chunks(a):
        return a.reshape(B, n, HG_CHUNK, H, a.shape[-1]).transpose(1, 0, 3, 2, 4).astype(jnp.float32)

    tri = jnp.tril(jnp.ones((HG_CHUNK, HG_CHUNK), dtype=bool))

    def step(S, inp):
        qc, kc, gc, vc = inp
        b = jnp.cumsum(gc, axis=2)
        b_last = b[:, :, -1:, :]
        k_dec = kc * jnp.exp(b_last - b)
        S_new = jnp.exp(b_last[:, :, 0, :])[..., None] * S + jnp.einsum('bhck,bhcv->bhkv', k_dec, vc)
        if not need_out:
            return S_new, None
        o_inter = jnp.einsum('bhck,bhkv->bhcv', qc * jnp.exp(b), S)
        diff = jnp.where(tri[:, :, None], b[:, :, :, None, :] - b[:, :, None, :, :], -jnp.inf)
        a = jnp.einsum('bhtk,bhsk,bhtsk->bhts', qc, kc, jnp.exp(diff))
        return S_new, o_inter + jnp.einsum('bhts,bhsv->bhtv', a, vc)

    S_fin, o = lax.scan(step, s0, (to_chunks(q), to_chunks(k), to_chunks(g), to_chunks(v)))
    if need_out:
        o = o.transpose(1, 0, 3, 2, 4).reshape(B, T, H, dv)
    return o, S_fin

def hgrn2_bidir(hx, hc, w_in, w_out, o_gain, lb, need_ctx_out):
    def project(h):
        b, t, _ = h.shape
        q, f_fw, f_bw, inp, gate = jnp.split(h @ w_in, HG_SPLITS, axis=-1)
        q = jax.nn.silu(q).reshape(b, t, HG_HEADS, HG_DK)
        inp = inp.reshape(b, t, HG_HEADS, HG_DV)

        def forget(fl):
            f = lb + (1.0 - lb) * jax.nn.sigmoid(fl.astype(jnp.float32))
            return (1.0 - f).reshape(b, t, HG_HEADS, HG_DK), jnp.log(f).reshape(b, t, HG_HEADS, HG_DK)

        return q, forget(f_fw), forget(f_bw), inp, gate

    flip = lambda a: jnp.flip(a, axis=1)
    qx, (kxf, gxf), (kxb, gxb), vx, gx = project(hx)
    qc, (kcf, gcf), (kcb, gcb), vc, gc = project(hc)
    s0 = jnp.zeros((hc.shape[0], HG_HEADS, HG_DK, HG_DV), jnp.float32)
    oc_f, sc_f = chunk_scan(qc, kcf, gcf, vc, s0, need_ctx_out)
    oc_b, sc_b = chunk_scan(flip(qc), flip(kcb), flip(gcb), flip(vc), s0, need_ctx_out)
    ox_f, _ = chunk_scan(qx, kxf, gxf, vx, sc_f, True)
    ox_b, _ = chunk_scan(flip(qx), flip(kxb), flip(gxb), flip(vx), sc_b, True)

    def readout(o, gate, h):
        o = rms_norm(o, o_gain).astype(h.dtype) * jax.nn.silu(gate).reshape(o.shape)
        return o.reshape(h.shape[0], h.shape[1], D_MODEL) @ w_out

    yx = readout(ox_f + flip(ox_b), gx, hx)
    yc = readout(oc_f + flip(oc_b), gc, hc) if need_ctx_out else None
    return yx, yc

def dwconv3(u, w, b):
    up = jnp.pad(u, ((0, 0), (1, 1), (0, 0)))
    return up[:, :-2] * w[0] + up[:, 1:-1] * w[1] + up[:, 2:] * w[2] + b

def conv_glu(h, w_up, conv_w, conv_b, w_down):
    gate, val = jnp.split(h @ w_up, 2, axis=-1)
    return (jax.nn.silu(dwconv3(gate, conv_w, conv_b)) * val) @ w_down

def first_inputs(seed: int = 0) -> dict:
    key = jax.random.key(seed)
    ks = jax.random.split(key, 21)
    D = D_MODEL

    def nrm(k, shape, scale):
        return jax.random.normal(k, shape, jnp.float32) * scale

    def gain(k, shape):
        return 1.0 + 0.05 * jax.random.normal(k, shape, jnp.float32)

    return {
        'x': nrm(ks[0], (BATCH, SEQ, D), 1.0),
        'c': nrm(ks[1], (BATCH, D), 1.0),
        'ctx': nrm(ks[2], (BATCH, CTX_LEN, D), 1.0),
        'c_ctx': nrm(ks[3], (D,), 1.0),
        'ada_w': nrm(ks[4], (DEPTH, D, 6 * D), 0.5 * D ** -0.5),
        'ada_b': nrm(ks[5], (DEPTH, 6 * D), 0.02),
        'norm1_g': gain(ks[6], (DEPTH, D)),
        'norm2_g': gain(ks[7], (DEPTH, D)),
        'attn_w_in': nrm(ks[8], (N_ATTN_LAYERS, D, ATTN_IN_W), D ** -0.5),
        'attn_w_out': nrm(ks[9], (N_ATTN_LAYERS, N_HEADS * HEAD_DIM, D), (N_HEADS * HEAD_DIM) ** -0.5),
        'attn_q_gain': gain(ks[10], (N_ATTN_LAYERS, HEAD_DIM)),
        'attn_k_gain': gain(ks[11], (N_ATTN_LAYERS, HEAD_DIM)),
        'attn_sink': nrm(ks[12], (N_ATTN_LAYERS, N_HEADS), 0.5),
        'hgrn_w_in': nrm(ks[13], (N_HGRN_LAYERS, D, HG_IN_W), D ** -0.5),
        'hgrn_w_out': nrm(ks[14], (N_HGRN_LAYERS, D, D), D ** -0.5),
        'hgrn_o_gain': gain(ks[15], (N_HGRN_LAYERS, HG_DV)),
        'hgrn_lb_logits': nrm(ks[16], (DEPTH, HG_DF), 0.5),
        'ffn_w_up': nrm(ks[17], (DEPTH, D, 2 * D_FF), D ** -0.5),
        'ffn_conv_w': nrm(ks[18], (DEPTH, CONV_W, D_FF), CONV_W ** -0.5),
        'ffn_conv_b': nrm(ks[19], (DEPTH, D_FF), 0.02),
        'ffn_w_down': nrm(ks[20], (DEPTH, D_FF, D), D_FF ** -0.5),
    }

def first_block(x, c, ctx, c_ctx, ada_w, ada_b, norm1_g, norm2_g, attn_w_in, attn_w_out, attn_q_gain,
              attn_k_gain, attn_sink, hgrn_w_in, hgrn_w_out, hgrn_o_gain, hgrn_lb_logits, ffn_w_up,
              ffn_conv_w, ffn_conv_b, ffn_w_down):
    L = x.shape[1]
    rows = L // GRID_W
    ang_r, ang_c = axial_angles(rows)
    lb_prob = jax.nn.softmax(hgrn_lb_logits.astype(jnp.float32), axis=0)
    lb_sched = jnp.cumsum(lb_prob, axis=0) - lb_prob[0]
    for layer in range(DEPTH):
        last = layer == DEPTH - 1
        j = layer // N_MIXERS
        mod = jax.nn.silu(c) @ ada_w[layer] + ada_b[layer]
        mod_c = jax.nn.silu(c_ctx) @ ada_w[layer] + ada_b[layer]
        sh1, sc1, g1, sh2, sc2, g2 = jnp.split(mod[:, None, :], 6, axis=-1)
        csh1, csc1, cg1, csh2, csc2, cg2 = jnp.split(mod_c, 6)
        hx = rms_norm(x, norm1_g[layer]) * (1.0 + sc1) + sh1
        hc = rms_norm(ctx, norm1_g[layer]) * (1.0 + csc1) + csh1
        if layer % N_MIXERS == 0:
            yx, yc = windowed_gqa(hx, hc, attn_w_in[j], attn_w_out[j], attn_q_gain[j], attn_k_gain[j],
                                  attn_sink[j], ang_r, ang_c, not last)
        else:
            yx, yc = hgrn2_bidir(hx, hc, hgrn_w_in[j], hgrn_w_out[j], hgrn_o_gain[j], lb_sched[layer], not last)
        x = x + g1 * yx
        hx2 = rms_norm(x, norm2_g[layer]) * (1.0 + sc2) + sh2
        x = x + g2 * conv_glu(hx2, ffn_w_up[layer], ffn_conv_w[layer], ffn_conv_b[layer], ffn_w_down[layer])
        if not last:
            ctx = ctx + cg1 * yc
            hc2 = rms_norm(ctx, norm2_g[layer]) * (1.0 + csc2) + csh2
            ctx = ctx + cg2 * conv_glu(hc2, ffn_w_up[layer], ffn_conv_w[layer], ffn_conv_b[layer], ffn_w_down[layer])
    return x


DEPTH_2 = 1

DIL_GROUPS = ((128, 1), (512, 4), (2048, 16))
DIL_HEADS = 4
DIL_WIDTH = len(DIL_GROUPS) * DIL_HEADS * HEAD_DIM
DIL_OUT = DIL_HEADS * HEAD_DIM
SWA_Q_HEADS = 16
SWA_KV_HEADS = 2
SWA_REP = SWA_Q_HEADS // SWA_KV_HEADS
SWA_WINDOW = 128
SWA_Q_WIDTH = SWA_Q_HEADS * HEAD_DIM
SWA_KV_WIDTH = SWA_KV_HEADS * HEAD_DIM
N_ALIBI_HEADS = SWA_Q_HEADS + len(DIL_GROUPS) * DIL_HEADS
ATTN_BLOCK = 128
SPLIT_SIZES = (DIL_WIDTH, DIL_WIDTH, DIL_WIDTH, SWA_Q_WIDTH, SWA_KV_WIDTH, SWA_KV_WIDTH, D_MODEL, D_MODEL)
SPLIT_POINTS = tuple(sum(SPLIT_SIZES[:i + 1]) for i in range(len(SPLIT_SIZES) - 1))
IN_COLS = sum(SPLIT_SIZES)
N_EXPERTS = 32
TOP_K = 4
D_FF_2 = 1024
SWIGLU_LIMIT = 7.0
SWIGLU_ALPHA = 1.702
MOE_BLOCK = 128
LN_EPS = 1e-5
DEEPNORM_ALPHA = (2 * DEPTH_2) ** 0.25
DEEPNORM_BETA = (8 * DEPTH_2) ** -0.25
NEG_INF = -1e30


def layer_norm(x, g, b):
    xf = x.astype(jnp.float32)
    mu = jnp.mean(xf, axis=-1, keepdims=True)
    var = jnp.mean(jnp.square(xf - mu), axis=-1, keepdims=True)
    y = (xf - mu) * lax.rsqrt(var + LN_EPS) * g.astype(jnp.float32) + b.astype(jnp.float32)
    return y.astype(x.dtype)

def alibi_slopes():
    h = jnp.arange(1, N_ALIBI_HEADS + 1, dtype=jnp.float32)
    return jnp.exp2(-8.0 * h / N_ALIBI_HEADS)

def banded_attention(q, k, v, slopes, max_diff, dist_scale, sinks):
    n, g, r, L, hd = q.shape
    nb = -(-L // ATTN_BLOCK)
    pad = nb * ATTN_BLOCK - L
    q = jnp.pad(q, ((0, 0), (0, 0), (0, 0), (0, pad), (0, 0)))
    k = jnp.pad(k, ((0, 0), (0, 0), (ATTN_BLOCK, pad), (0, 0)))
    v = jnp.pad(v, ((0, 0), (0, 0), (ATTN_BLOCK, pad), (0, 0)))
    qb = q.reshape(n, g, r, nb, ATTN_BLOCK, hd)
    kb = k.reshape(n, g, nb + 1, ATTN_BLOCK, hd)
    vb = v.reshape(n, g, nb + 1, ATTN_BLOCK, hd)
    kw = jnp.concatenate([kb[:, :, :-1], kb[:, :, 1:]], axis=3)
    vw = jnp.concatenate([vb[:, :, :-1], vb[:, :, 1:]], axis=3)
    s = jnp.einsum('ngrbqd,ngbkd->ngrbqk', qb, kw, preferred_element_type=jnp.float32) * (hd ** -0.5)
    qi = jnp.arange(ATTN_BLOCK)[:, None]
    kj = jnp.arange(2 * ATTN_BLOCK)[None, :]
    diff = qi - kj + ATTN_BLOCK
    kpos = jnp.arange(nb)[:, None, None] * ATTN_BLOCK - ATTN_BLOCK + kj[None]
    valid = (diff >= 0) & (diff <= max_diff) & (kpos >= 0)
    bias = -slopes.astype(jnp.float32)[:, :, None, None, None] * (dist_scale * diff).astype(jnp.float32)
    s = jnp.where(valid, s + bias, NEG_INF)
    m = jnp.max(s, axis=-1)
    if sinks is not None:
        sink = sinks.astype(jnp.float32)[:, :, None, None]
        m = jnp.maximum(m, sink)
    p = jnp.exp(s - m[..., None])
    denom = jnp.sum(p, axis=-1)
    if sinks is not None:
        denom = denom + jnp.exp(sink - m)
    o = jnp.einsum('ngrbqk,ngbkd->ngrbqd', p.astype(v.dtype), vw, preferred_element_type=jnp.float32)
    o = o / denom[..., None]
    lse = m + jnp.log(denom)
    o = o.reshape(n, g, r, nb * ATTN_BLOCK, hd)[:, :, :, :L]
    lse = lse.reshape(n, g, r, nb * ATTN_BLOCK)[:, :, :, :L]
    return o.astype(q.dtype), lse

def dilated_attention(q, k, v, slopes_a):
    b, S, _ = q.shape
    q = q.reshape(b, S, len(DIL_GROUPS), DIL_HEADS, HEAD_DIM)
    k = k.reshape(b, S, len(DIL_GROUPS), DIL_HEADS, HEAD_DIM)
    v = v.reshape(b, S, len(DIL_GROUPS), DIL_HEADS, HEAD_DIM)
    outs, lses = [], []
    for gi, (window, dil) in enumerate(DIL_GROUPS):
        L = S // dil

        def to_sub(t):
            t = t[:, :, gi].reshape(b, L, dil, DIL_HEADS, HEAD_DIM)
            return t.transpose(0, 2, 3, 1, 4).reshape(b * dil, DIL_HEADS, L, HEAD_DIM)

        qs, ks, vs = to_sub(q), to_sub(k), to_sub(v)
        o, lse = banded_attention(qs[:, :, None], ks, vs, slopes_a[gi][:, None],
                                  max_diff=window // dil, dist_scale=dil, sinks=None)
        o = o[:, :, 0].reshape(b, dil, DIL_HEADS, L, HEAD_DIM).transpose(0, 3, 1, 2, 4).reshape(b, S, DIL_HEADS, HEAD_DIM)
        lse = lse[:, :, 0].reshape(b, dil, DIL_HEADS, L).transpose(0, 3, 1, 2).reshape(b, S, DIL_HEADS)
        outs.append(o)
        lses.append(lse)
    w = jax.nn.softmax(jnp.stack(lses, axis=0), axis=0)
    o = jnp.einsum('gbsh,gbshd->bshd', w, jnp.stack(outs, axis=0).astype(jnp.float32))
    return o.reshape(b, S, DIL_OUT).astype(q.dtype)

def swa_sink_attention(q, k, v, slopes_b, sinks):
    b, S, _ = q.shape
    q = q.reshape(b, S, SWA_KV_HEADS, SWA_REP, HEAD_DIM).transpose(0, 2, 3, 1, 4)
    k = k.reshape(b, S, SWA_KV_HEADS, HEAD_DIM).transpose(0, 2, 1, 3)
    v = v.reshape(b, S, SWA_KV_HEADS, HEAD_DIM).transpose(0, 2, 1, 3)
    o, _ = banded_attention(q, k, v, slopes_b, max_diff=SWA_WINDOW - 1, dist_scale=1, sinks=sinks)
    return o.transpose(0, 3, 1, 2, 4).reshape(b, S, SWA_Q_WIDTH)

def token_mixer(x, w_in, sinks, w_proj_a, w_proj_b, w_out, slopes):
    h = jnp.einsum('bsd,dc->bsc', x, w_in)
    a_q, a_k, a_v, b_q, b_k, b_v, g_a, g_b = jnp.split(h, SPLIT_POINTS, axis=-1)
    slopes_b = slopes[:SWA_Q_HEADS].reshape(SWA_KV_HEADS, SWA_REP)
    slopes_a = slopes[SWA_Q_HEADS:].reshape(len(DIL_GROUPS), DIL_HEADS)
    out_a = dilated_attention(a_q, a_k, a_v, slopes_a)
    out_b = swa_sink_attention(b_q, b_k, b_v, slopes_b, sinks.reshape(SWA_KV_HEADS, SWA_REP))
    merged = (jax.nn.sigmoid(g_a) * jnp.einsum('bsc,cd->bsd', out_a, w_proj_a)
              + jax.nn.sigmoid(g_b) * jnp.einsum('bsc,cd->bsd', out_b, w_proj_b))
    return jnp.einsum('bsd,de->bse', merged, w_out)

def moe_ffn(y, router_w, router_b, w_gate, b_gate, w_up, b_up, w_down, b_down):
    b, S, D = y.shape
    n_tok = b * S
    yf = y.reshape(n_tok, D)
    logits = (yf @ router_w + router_b).astype(jnp.float32)
    top_val, top_idx = lax.top_k(logits, TOP_K)
    gates = jax.nn.softmax(top_val, axis=-1)
    n_assign = n_tok * TOP_K
    flat_e = top_idx.reshape(-1)
    order = jnp.argsort(flat_e)
    sorted_e = flat_e[order]
    tok = order // TOP_K
    counts = jnp.zeros((N_EXPERTS,), jnp.int32).at[flat_e].add(1)
    padded = (counts + MOE_BLOCK - 1) // MOE_BLOCK * MOE_BLOCK
    p_end = jnp.cumsum(padded)
    p_start = p_end - padded
    u_start = jnp.cumsum(counts) - counts
    dest = p_start[sorted_e] + jnp.arange(n_assign, dtype=jnp.int32) - u_start[sorted_e]
    n_blocks = -(-n_assign // MOE_BLOCK) + N_EXPERTS
    rows = n_blocks * MOE_BLOCK
    xs = jnp.zeros((rows, D), y.dtype).at[dest].set(yf[tok])
    block_e = jnp.minimum(jnp.searchsorted(p_end, jnp.arange(n_blocks, dtype=jnp.int32) * MOE_BLOCK, side='right'),
                          N_EXPERTS - 1).astype(jnp.int32)

    def expert_block(args):
        xb, e = args
        gt = xb @ w_gate[e] + b_gate[e]
        up = xb @ w_up[e] + b_up[e]
        gt = jnp.minimum(gt, SWIGLU_LIMIT)
        up = jnp.clip(up, -SWIGLU_LIMIT, SWIGLU_LIMIT)
        hdn = gt * jax.nn.sigmoid(SWIGLU_ALPHA * gt) * (up + 1.0)
        return hdn @ w_down[e] + b_down[e]

    ys = lax.map(expert_block, (xs.reshape(n_blocks, MOE_BLOCK, D), block_e)).reshape(rows, D)
    contrib = ys[dest] * gates.reshape(-1)[order][:, None].astype(ys.dtype)
    out = jax.ops.segment_sum(contrib, tok, num_segments=n_tok)
    return out.reshape(b, S, D)

def second_inputs(seed: int = 0) -> dict:
    key = jax.random.key(seed)
    ks = jax.random.split(key, 20)
    f32 = jnp.float32
    beta = DEEPNORM_BETA
    col_scale = jnp.concatenate([
        jnp.ones((2 * DIL_WIDTH,), f32), jnp.full((DIL_WIDTH,), beta, f32),
        jnp.ones((SWA_Q_WIDTH + SWA_KV_WIDTH,), f32), jnp.full((SWA_KV_WIDTH,), beta, f32),
        jnp.ones((2 * D_MODEL,), f32)])
    nrm = lambda k, shape: jax.random.normal(k, shape, f32)
    return {
        "x": nrm(ks[0], (BATCH, SEQ, D_MODEL)),
        "w_in": nrm(ks[1], (DEPTH_2, D_MODEL, IN_COLS)) * (D_MODEL ** -0.5) * col_scale,
        "sinks": 0.5 * nrm(ks[2], (DEPTH_2, SWA_Q_HEADS)),
        "w_proj_a": nrm(ks[3], (DEPTH_2, DIL_OUT, D_MODEL)) * (DIL_OUT ** -0.5),
        "w_proj_b": nrm(ks[4], (DEPTH_2, SWA_Q_WIDTH, D_MODEL)) * (SWA_Q_WIDTH ** -0.5),
        "w_out": nrm(ks[5], (DEPTH_2, D_MODEL, D_MODEL)) * (D_MODEL ** -0.5) * beta,
        "ln1_g": 1.0 + 0.05 * nrm(ks[6], (DEPTH_2, D_MODEL)),
        "ln1_b": 0.02 * nrm(ks[7], (DEPTH_2, D_MODEL)),
        "router_w": nrm(ks[8], (DEPTH_2, D_MODEL, N_EXPERTS)) * (D_MODEL ** -0.5),
        "router_b": 0.01 * nrm(ks[9], (DEPTH_2, N_EXPERTS)),
        "w_gate": nrm(ks[10], (DEPTH_2, N_EXPERTS, D_MODEL, D_FF_2)) * (D_MODEL ** -0.5),
        "b_gate": 0.02 * nrm(ks[11], (DEPTH_2, N_EXPERTS, D_FF_2)),
        "w_up": nrm(ks[12], (DEPTH_2, N_EXPERTS, D_MODEL, D_FF_2)) * (D_MODEL ** -0.5),
        "b_up": 0.02 * nrm(ks[13], (DEPTH_2, N_EXPERTS, D_FF_2)),
        "w_down": nrm(ks[14], (DEPTH_2, N_EXPERTS, D_FF_2, D_MODEL)) * (D_FF_2 ** -0.5) * beta,
        "b_down": 0.02 * nrm(ks[15], (DEPTH_2, N_EXPERTS, D_MODEL)),
        "ln2_g": 1.0 + 0.05 * nrm(ks[16], (DEPTH_2, D_MODEL)),
        "ln2_b": 0.02 * nrm(ks[17], (DEPTH_2, D_MODEL)),
    }

def second_block(x, w_in, sinks, w_proj_a, w_proj_b, w_out, ln1_g, ln1_b, router_w, router_b,
              w_gate, b_gate, w_up, b_up, w_down, b_down, ln2_g, ln2_b):
    slopes = alibi_slopes()
    for l in range(DEPTH_2):
        mix = token_mixer(x, w_in[l], sinks[l], w_proj_a[l], w_proj_b[l], w_out[l], slopes)
        x = layer_norm(DEEPNORM_ALPHA * x + mix, ln1_g[l], ln1_b[l])
        ffn = moe_ffn(x, router_w[l], router_b[l], w_gate[l], b_gate[l], w_up[l], b_up[l], w_down[l], b_down[l])
        x = layer_norm(DEEPNORM_ALPHA * x + ffn, ln2_g[l], ln2_b[l])
    return x


def setup_inputs(seed=0):
    out = dict(first_inputs(seed))
    for name, value in second_inputs(seed + 1).items():
        if name != "x":
            out[name + "_2"] = value
    return out


def reference(
    x, c, ctx, c_ctx, ada_w, ada_b, norm1_g, norm2_g, attn_w_in, attn_w_out, attn_q_gain,
    attn_k_gain, attn_sink, hgrn_w_in, hgrn_w_out, hgrn_o_gain, hgrn_lb_logits, ffn_w_up,
    ffn_conv_w, ffn_conv_b, ffn_w_down, w_in_2, sinks_2, w_proj_a_2, w_proj_b_2, w_out_2,
    ln1_g_2, ln1_b_2, router_w_2, router_b_2, w_gate_2, b_gate_2, w_up_2, b_up_2, w_down_2,
    b_down_2, ln2_g_2, ln2_b_2,
):
    x = first_block(
        x, c, ctx, c_ctx, ada_w, ada_b, norm1_g, norm2_g, attn_w_in, attn_w_out, attn_q_gain,
        attn_k_gain, attn_sink, hgrn_w_in, hgrn_w_out, hgrn_o_gain, hgrn_lb_logits, ffn_w_up,
        ffn_conv_w, ffn_conv_b, ffn_w_down,
    )
    return second_block(
        x, w_in_2, sinks_2, w_proj_a_2, w_proj_b_2, w_out_2, ln1_g_2, ln1_b_2, router_w_2,
        router_b_2, w_gate_2, b_gate_2, w_up_2, b_up_2, w_down_2, b_down_2, ln2_g_2, ln2_b_2,
    )


_drawn_inputs = setup_inputs


def setup_inputs(seed=0):
    import zlib

    import numpy as np

    out = dict(_drawn_inputs(seed))
    spreads = {}
    factors = {'attn_q_gain': 8.0,
     'attn_k_gain': 6.031,
     'attn_sink': 8.0,
     'ffn_conv_b': 3.255,
     'sinks_2': 4.396,
     'b_gate_2': 8.0,
     'b_up_2': 8.0,
     'b_down_2': 6.51,
     'ln2_b_2': 2.842,
     'hgrn_o_gain': 2.685,
     'hgrn_lb_logits': 2.745,
     'router_b_2': 3.153}
    for name, (base, spread) in spreads.items():
        noise = np.random.default_rng([zlib.crc32(name.encode()), seed]).standard_normal(out[name].shape)
        drawn = base * np.exp(spread * noise) if base else spread * noise
        out[name] = __import__('jax').numpy.asarray(drawn.astype(out[name].dtype))
    for name, factor in factors.items():
        out[name] = (out[name] * factor).astype(out[name].dtype)
    return out
```

```python
from contextlib import ExitStack

import numpy as np
import concourse.bass as bass
from concourse import mybir

ALU = mybir.AluOpType
ACT = mybir.ActivationFunctionType
AX = mybir.AxisListType.X
F32 = mybir.dt.float32
F32R = mybir.dt.float32r
I32 = mybir.dt.int32
U8 = mybir.dt.uint8

P = 128
D = 1024
KC = D // P
SEQ, CTX = 256, 256
TOK = SEQ + CTX
NT, XT = TOK // P, SEQ // P
HD = 64
FF = 2816
FC = FF // P
NH, NKV = 16, 4
HG = 8
LEVELS = [64, 32, 16, 8, 4, 2, 1]
E = 32
SLOTS = 64
UNIT = 4096
RING = 3
PASSES = -(-SEQ // SLOTS)
ITEMS = E * (PASSES - 1)
ALPHA = 2.0 ** 0.25
BANKS = 8

CONST = {}


def _lay():
    at = 0
    for name, n in (("ident", 128), ("cos", 64), ("sin", 64), ("mask0", 1024), ("diff", 1024), ("sel2", 2),
                    ("selb", 256), ("before", 128), ("slot", 128), ("ones", 128), ("eps6", 1), ("eps5", 1),
                    ("item", ITEMS + 2)):
        CONST[name] = (at, n)
        at += n
    return at


NCONST = _lay()

COLS = {"n1": (0, 16), "n2": (16, 16), "adab": (32, 96), "cw": (128, 132), "cb": (260, 44), "lb": (304, 16),
        "c": (320, 16)}
NCOLS = 336
ROWS = {"qg": (0, 64), "kg": (64, 64), "sink": (128, 16), "og": (144, 128), "sink2": (272, 16), "rb": (288, 32)}
NROWS = 320


def slopes():
    h = np.arange(1, 29, dtype=np.float32)
    return [float(v) for v in np.exp2(np.float32(-8.0) * h / np.float32(28))]


def constants():
    c = np.zeros((P, NCONST), np.float32)

    def put(name, v):
        at, n = CONST[name]
        c[:, at:at + n] = np.asarray(v, np.float32).reshape(-1, n) if np.ndim(v) else v

    p = np.arange(P)
    put("ident", np.eye(P))
    inv = (np.float32(10000.0) ** (-np.arange(16, dtype=np.float32) / np.float32(16))).astype(np.float32)
    t = np.arange(SEQ)
    ang = np.stack([(t // 64).astype(np.float32)[:, None] * inv, (t % 64).astype(np.float32)[:, None] * inv], 1)
    for name, f in (("cos", np.cos), ("sin", np.sin)):
        put(name, f(ang.astype(np.float32)).reshape(2, P, 32).transpose(1, 0, 2).reshape(P, 64))
    m = np.zeros((P, 2, 512), np.float32)
    for i in range(2):
        m[:, i, :SEQ] = np.where(np.abs((i * P + p)[:, None] - np.arange(SEQ)) <= 128, 0.0, -1e30)
    put("mask0", m.reshape(P, 1024))
    diff = P + p[:, None] - np.arange(SEQ)
    far = np.float32(1e33)
    d = np.stack([np.where((diff >= 0) & (diff <= lim) & (diff % dil == 0), diff, far)
                  for lim, dil in ((127, 1), (128, 1), (512, 4), (2048, 16))], 1)
    put("diff", d.reshape(P, 1024))
    q, v = p % 32, np.arange(2)
    put("sel2", (q[:, None] == v).astype(np.float32))
    put("selb", np.repeat((q[:, None] == v).astype(np.float32), P, axis=1))
    put("before", (p[:, None] < p).astype(np.float32))
    put("slot", np.tile(np.arange(SLOTS, dtype=np.float32), (P, 2)))
    put("ones", np.ones((P, P)))
    put("eps6", 1e-6)
    put("eps5", 1e-5)
    put("item", np.tile(np.arange(ITEMS + 2, dtype=np.float32), (P, 1)))
    masks = np.zeros((P, 2, len(LEVELS), P), np.float32)
    s, tt = p[:, None], p[None, :]
    for n, h in enumerate(LEVELS):
        fw = (s // (2 * h) == tt // (2 * h)) & (s % (2 * h) < h) & (tt % (2 * h) >= h)
        masks[:, 0, n], masks[:, 1, n] = fw, fw.T
    return c, masks.reshape(P, -1)


def program(nc, a, out, dbg=None, stop=None):
    with ExitStack() as ctx:
        def sb(name, shape, dt=F32):
            return ctx.enter_context(nc.sbuf_tensor(name, shape, dt))

        def sem(name):
            return ctx.enter_context(nc.semaphore(name))

        PS = [ctx.enter_context(nc.psum_tensor(f"bank{i}", [P, 512], F32)) for i in range(BANKS)]
        ring_at = -(-nc.sbuf_base // 32) * 32
        ring = sb("ring", [P, RING, UNIT])
        arena_at = -(-nc.sbuf_base // 32) * 32
        arena = sb("arena", [P, 80 * 256])
        xr = sb("xr", [P, NT, D])
        hT_at = -(-nc.sbuf_base // 32) * 32
        hT = sb("hT", [P, KC, TOK])
        gb = sb("gb", [P, 4, D])
        modp = sb("modp", [P, 2, 512])
        xn = sb("xn", [P, 2, D])
        const = sb("const", [P, NCONST])
        mask_in = xn[:, :, :].rearrange("p a b -> p (a b)")[:, 0:2 * len(LEVELS) * P]
        masks = sb("masks", [P, 2 * len(LEVELS) * P], U8)
        cols = sb("cols", [P, NCOLS])
        rows = sb("rows", [P, NROWS])
        cT = sb("cT", [P, KC, 32])
        modT = sb("modT", [P, 2, 48, 2])
        coef = sb("coef", [P, 2, 2, KC, 2])
        stat = sb("stat", [P, 256])

        def C(name, lo=0, n=None):
            at, w = CONST[name]
            return const[:, at + lo:at + lo + (w if n is None else n)]

        def COL(name, lo=0, n=None):
            at, w = COLS[name]
            return cols[:, at + lo:at + lo + (w if n is None else n)]

        def ROW(name, lo=0, n=None):
            at, w = ROWS[name]
            return rows[:, at + lo:at + lo + (w if n is None else n)]

        ident = C("ident")

        def region(at, *shape):
            n = int(np.prod(shape))
            assert at + n <= 80 * 256, (at, n)
            v = arena[:, at:at + n]
            if len(shape) == 1:
                return v
            names = "abcd"[:len(shape)]
            return v.rearrange(f"p ({' '.join(names)}) -> p {' '.join(names)}",
                               **{k: s for k, s in zip(names, shape)})

        qkv = region(0, NT, 1536)
        qT = region(6144, 8, TOK)
        kT = region(10240, 8, TOK)
        SB = region(14336, 2, 2048)
        PT = region(18432, 2, 512)
        hid = region(0, FC, TOK)
        ft = xn[:, :, :].rearrange("p a (b n) -> p (a b) n", n=512)
        def high_low(name, shape, at):
            return nc.alloc_sbuf_tensor_at(name, shape, F32R, offset=at)

        hT_high = high_low("hT_high", [P, KC, TOK], hT_at)
        hT_low = high_low("hT_low", [P, KC, TOK], arena_at + 4 * FC * TOK)
        w_split = [high_low("w_split0", [P, 2, KC, 2, P], arena_at + 4 * (FC * TOK + KC * TOK)),
                   high_low("w_split1", [P, 2, KC, 2, P], ring_at + 4 * UNIT * (RING - 1))]
        rq = region(0, HG, SEQ)
        rv = region(2048, NT, D)
        rg = region(6144, XT, D)
        rk = region(8192, 4, TOK)
        rb = region(10240, 4, TOK)
        rE = region(12288, 4, SEQ)
        rQ = region(13312, 4, SEQ)
        rK = region(14336, 4, SEQ)
        rA = region(15360, 2, 4, P)
        rC = region(16384, 4, P)
        rS = region(16896, 4, P)
        rD = region(17408, 2, 2, P)
        ro = region(17920, XT, D)
        aT = region(0, 6, SEQ)
        aK = region(1536, 12, SEQ)
        bT = region(4608, 8, SEQ)
        bK = region(6656, 4, SEQ)
        av = region(7680, XT, 768)
        bv = region(9216, XT, P)
        ga = region(9472, XT, D)
        gb2 = region(11520, XT, D)
        oA = region(13568, XT, 256)
        oB = xn
        moe_slot = [ring[:, i, :] for i in range(RING)] + [region(i * UNIT, UNIT) for i in range(6 - RING)]
        M0 = (6 - RING) * UNIT
        xg = region(M0, KC, SLOTS)
        hm = region(M0 + 512, 512)
        um = region(M0 + 1024, 512)
        sg = region(M0 + 1536, 512)
        hh = region(M0 + 2048, 512)
        hhT = region(M0 + 2560, 4, P)
        yg = region(M0 + 3072, 512)
        bias = region(M0 + 3584, D)
        rw = region(M0 + 4608, KC, E)
        sel = region(M0 + 4864, 2, P)
        selg = region(M0 + 5120, 2, P)
        selgT = region(M0 + 5376, 2, P)
        table = region(M0 + 5632, E + 2, 6)
        cur = region(M0 + 5900, 8)
        lgx = region(M0 + 5908, 2, 40)
        top = region(M0 + 5988, 2, 8)
        pick = region(M0 + 6004, 2, 40)
        gate = region(M0 + 6084, 2, E)
        chosen = region(M0 + 6148, 2, E)
        rank = region(M0 + 6212, 3, E)
        extra = region(M0 + 6308, 2, E)
        far = region(M0 + 6372, 2, ITEMS + 2)
        fari = region(M0 + 6572, ITEMS + 2).bitcast(I32)
        nfar = region(M0 + 6670, 1).bitcast(I32)
        tst = region(M0 + 6672, 16)
        wide = hT[:, :, :].rearrange("p k t -> p (k t)")[:, 0:(ITEMS + 2) * E].rearrange("p (j e) -> p j e", e=E)
        acc = xr[:, XT:NT, :]

        NL = len(LEVELS)

        group, reader, nth = {}, [], []
        seen = {"act": 0, "dve": 0}

        def add(key, who):
            assert key not in group, key
            group[key] = len(reader)
            reader.append(who)
            seen[who] += 1
            nth.append(seen[who])

        units, unit_no = [], {}

        def stream(key, *pieces):
            unit_no[key] = len(units)
            units.append(pieces)

        def colblock(w, lo, n):
            return w.rearrange("(k p) n -> p k n", p=P)[:, :, lo:lo + n]

        def ring_col(s, lo, n):
            return ring[:, s, :].rearrange("p (k n) -> p k n", k=KC)[:, :, lo:lo + n]

        def ring_row(s, n):
            return ring[:, s, 0:n * D].rearrange("p (k n) -> p k n", k=n)

        def col_unit(key, w, lo, n=512):
            stream(key, (lambda s: ring_col(s, 0, n), colblock(w, lo, n)))

        def row_units(key, w, chunks):
            for j, k0 in enumerate(range(0, chunks, 4)):
                n = min(4, chunks - k0)
                stream((*key, j), (lambda s, n=n: ring_row(s, n),
                                   w[k0 * P:(k0 + n) * P, :].rearrange("(k p) n -> p k n", p=P)))

        G_BLOCKS = {4: (0, 0), 5: (0, 1), 10: (1, 0), 11: (1, 1)}

        def gate_slots(l, blk):
            if blk not in G_BLOCKS:
                return []
            g = G_BLOCKS[blk][0]
            return [(2 * g, 0), (2 * g + 1, 1)] if l == 0 else [(g, 0)]

        GATE = {(0, 0): (0, 1), (0, 1): (2, 3), (1, 0): (0,), (1, 1): (1,)}

        ada_turn = {}

        def plan_ada(l, blk):
            ada_turn[l, blk] = len(ada_turn) % 2
            col_unit(("ada", l, blk), a["ada_w"][l], blk * 512)
            add(("adap", l, blk), "act")
            add(("adat", l, blk), "dve")
            for row, v in gate_slots(l, blk):
                add(("adag", l, blk, row), "dve")

        def plan_turn(tag, tiles):
            for t in tiles:
                for h in range(2):
                    add(("turn", tag, t, h), "act")

        ALL, XS = range(NT), range(XT)
        for blk in range(4):
            plan_ada(0, blk)
        plan_turn("a0", ALL)
        for b in range(3):
            col_unit(("qkv", b), a["attn_w_in"][0], b * 512)
            for t in ALL:
                add(("qkv", b, t), "act")
        for t in ALL:
            for j in range(3):
                add(("qkt", t, j), "act")

        def att_units0():
            for t in ALL:
                for g in range(NKV):
                    w = TOK if t < XT else CTX
                    lo = 0 if t < XT else SEQ

                    def qa(r, t=t, g=g):
                        return qT[:, 2 * g + r // 2, t * P:(t + 1) * P]

                    def ka(r, g=g, lo=lo, w=w):
                        return kT[:, 2 * g + r % 2, lo:lo + w]

                    def va(r, c, g=g, t=t):
                        return qkv[:, c if t < XT else c + XT, 1280 + g * HD:1280 + (g + 1) * HD]

                    yield dict(tag=("x0", t, g), n=w, q=qa, k=ka, v=va, heads=4,
                               mask=C("mask0", t * 512, 512) if t < XT else None, slope=None,
                               sink=ROW("sink", 4 * g, 4), out=qkv[:, t, g * 256:(g + 1) * 256])

        def att_units2():
            sl = slopes()
            for t in XS:
                n = (t + 1) * P
                for g in range(4):
                    def qa(r, t=t, g=g):
                        return bT[:, 2 * g + r // 2, t * P:(t + 1) * P]

                    def ka(r, g=g, n=n):
                        return bK[:, 2 * (g // 2) + r % 2, 0:n]

                    def va(r, c, g=g):
                        return bv[:, c, (g // 2) * HD:(g // 2 + 1) * HD]

                    yield dict(tag=("b2", t, g), n=n, q=qa, k=ka, v=va, heads=4, mask=None,
                               slope=[(sl[4 * g + r], C("diff", SEQ - n, n)) for r in range(4)],
                               sink=ROW("sink2", 4 * g, 4), out=oB[:, t, g * 256:(g + 1) * 256])
            for t in XS:
                n = (t + 1) * P
                for h in range(4):
                    def qa(r, t=t, h=h):
                        return aT[:, 2 * r + h // 2, t * P:(t + 1) * P]

                    def ka(r, h=h, n=n):
                        return aK[:, 4 * r + h, 0:n]

                    def va(r, c, h=h):
                        return av[:, c, (r * 4 + h) * HD:(r * 4 + h + 1) * HD]

                    yield dict(tag=("a2", t, h), n=n, q=qa, k=ka, v=va, heads=1, mask=None,
                               slope=[(sl[16 + 4 * r + h], C("diff", (r + 1) * SEQ + SEQ - n, n)) for r in range(3)],
                               sink=None, out=oA[:, t, h * HD:(h + 1) * HD])

        rk2 = gb[:, 2:4, :].rearrange("p a b -> p (a b)").rearrange("p (i t) -> p i t", i=4)
        rks = (rk, rk2)
        rlog = region(12288, 4, TOK)
        EL = [rE, xn[:, 0, :].rearrange("p (h t) -> p h t", h=4)]
        QL = [rQ, xn[:, 1, :].rearrange("p (h t) -> p h t", h=4)]
        KL = [rK, modp[:, :, :].rearrange("p a b -> p (a b)").rearrange("p (h t) -> p h t", h=4)]

        def late_early(v, h, d):
            v = v.rearrange("p i (n z c) -> p i n z c", z=2, c=h)
            return v[:, :, :, 1 - d, :], v[:, :, :, d, :]

        def nrows(u):
            return 4 if u["heads"] == 4 else 3

        def plan_att(us, between):
            for i in range(len(us) + 1):
                if i < len(us):
                    for r in range(nrows(us[i])):
                        add(("score", us[i]["tag"], r), "dve")
                if i:
                    for r in range(nrows(us[i - 1])):
                        add(("probt", us[i - 1]["tag"], r), "act")
                    add(("pv", us[i - 1]["tag"]), "dve")
                    between(i - 1)

        ATT0, ATT2 = list(att_units0()), list(att_units2())
        ADA_BETWEEN = [(0, 4 + i // 2) if i % 2 == 0 else (1, (0, 1, 2, 3, 6, 7, 8, 9)[i // 2]) for i in range(16)]
        ADA_LATE = [4, 5, 10, 11]
        plan_att(ATT0, lambda i: plan_ada(*ADA_BETWEEN[i]))
        plan_turn("o0", ALL)
        for b in range(2):
            col_unit(("wo0", b), a["attn_w_out"][0], b * 512)
            for t in ALL:
                add(("wo0", b, t), "dve")

        def plan_ffn(l, T):
            plan_turn(("f", l), range(T))
            w = a["ffn_w_up"][l]
            for j in range(FC // 2):
                stream(("up", l, j), (lambda s: ring_col(s, 0, 256), colblock(w, j * 256, 256)),
                       (lambda s: ring_col(s, 256, 256), colblock(w, FF + j * 256, 256)))
                for i in range(2):
                    add(("gate", l, 2 * j + i), "act")
                    add(("val", l, 2 * j + i), "dve")
                if l == 0 and j < 4:
                    plan_ada(1, ADA_LATE[j])
            row_units(("down", l), a["ffn_w_down"][l], FC)
            for t in range(T):
                for h in range(2):
                    add(("down", l, t, h), "dve")

        plan_ffn(0, NT)
        plan_turn("h1", ALL)
        w = a["hgrn_w_in"][0]
        for b in range(2):
            col_unit(("hq", b), w, b * 512)
            for i in range(4):
                add(("hq", 4 * b + i), "act")
        for b in range(2):
            col_unit(("hv", b), w, 3072 + b * 512)
            for t in ALL:
                add(("hv", b, t), "act")
        for b in range(2):
            col_unit(("hg", b), w, 4096 + b * 512)
            for t in XS:
                add(("hg", b, t), "act")
        def after(d, b):
            return (d, 1) if b == 0 else (1, 0) if d == 0 else None

        def plan_hf(d, b, i):
            if i == 0:
                col_unit(("hf", d, b), w, 1024 + d * 1024 + b * 512)
            add(("hf", d, b, i), "act")

        for i in range(4):
            plan_hf(0, 0, i)
        for d in range(2):
            for b in range(2):
                for i in range(4):
                    add(("kt", d, b, i), "act")
                    add(("st", d, b, i), "act")
                for n in range(-1, NL + 1):
                    if n == NL:
                        add(("lev", d, b, n, 0), "dve")
                    else:
                        for t in XS:
                            add(("lev", d, b, n, t), "dve")
                    if n >= 0 and n % 2 == 0 and after(d, b):
                        plan_hf(*after(d, b), n // 2)
                for t in XS:
                    add(("ro", d, b, t), "dve")
        plan_turn("o1", XS)
        for b in range(2):
            col_unit(("wo1", b), a["hgrn_w_out"][0], b * 512)
            for t in XS:
                add(("wo1", b, t), "dve")
        plan_ffn(1, XT)
        plan_turn("x2", XS)
        w = a["w_in_2"][0]
        W2 = []
        for c in range(12):
            W2.append((c * 128 // 512, "T", c * 128 % 512, ("aT", c)))
        W2 += [(3, "N", (0, 512), ("av", 0)), (4, "N", (0, 256), ("av", 512))]
        for c in range(8):
            at = 2304 + c * 128
            W2.append((at // 512, "T", at % 512, ("bT", c)))
        for g in range(2):
            W2.append((6, "K", 256 + 64 * g, ("bT", 8 + g)))
        W2.append((6, "N", (384, 128), ("bv", 0)))
        for j in range(4):
            W2.append((7 + j, "N", (0, 512), ("g", j)))
        for b in range(11):
            col_unit(("w2", b), w, b * 512)
        for u, kind, c, dst in W2:
            if kind == "N":
                for t in XS:
                    add(("w2", dst, t), "act")
            else:
                add(("w2", dst), "act")
        plan_att(ATT2, lambda i: None)
        for t in XS:
            add(("turn", "oa2", t, 0), "act")
        plan_turn("ob2", XS)
        row_units(("pa",), a["w_proj_a_2"][0], 2)
        for b in range(2):
            col_unit(("pb", b), a["w_proj_b_2"][0], b * 512)
        for b in range(2):
            for t in XS:
                add(("pa", b, t), "dve")
                add(("pb", b, t), "dve")
        plan_turn("m2", XS)
        for b in range(2):
            col_unit(("wo2", b), a["w_out_2"][0], b * 512)
            for t in XS:
                add(("wo2", b, t), "dve")
        plan_turn("y2", XS)
        add(("route",), "dve")
        add(("rank",), "dve")
        N_DENSE = len(reader)

        unit_end = {}
        for key in unit_no:
            if key[0] == "ada":
                unit_end[key] = ("adap", *key[1:])
            elif key[0] == "up":
                unit_end[key] = ("val", key[1], 2 * key[2] + 1)
            elif key[0] == "down":
                last = key[2] == (FC + 3) // 4 - 1
                unit_end[key] = ("down", key[1], NT - 1 if key[1] == 0 else XT - 1, 1) if last else None
            elif key[0] in ("qkv", "wo0", "hv"):
                unit_end[key] = (*key, NT - 1)
            elif key[0] == "hq":
                unit_end[key] = ("hq", 4 * key[1] + 3)
            elif key[0] == "hf":
                unit_end[key] = (*key, 3)
            elif key[0] == "pa":
                unit_end[key] = ("pa", 1, XT - 1)
            elif key[0] == "w2":
                dst, kind = [(d, k) for u, k, _, d in W2 if u == key[1]][-1]
                unit_end[key] = ("w2", dst, XT - 1) if kind == "N" else ("w2", dst)
            else:
                unit_end[key] = (*key, XT - 1)
        mid_units = 0
        splits = 0
        unit_done = []
        for key, n in unit_no.items():
            if key[0] == "up":
                splits += 2
                unit_done.append(("w_low", splits))
            elif unit_end[key] is None:
                mid_units += 1
                unit_done.append(("units_used", mid_units))
            else:
                unit_done.append(("psum_ready", group[unit_end[key]] + 1))

        slot_of, before_load, landed = [], [], []
        cnt, owner, order = [0] * RING, [None] * RING, list(range(RING))
        names = list(unit_no)
        for n, (key, pieces) in enumerate(zip(names, units)):
            narrow = key[0] == "up" or (key[0] == "ada" and names[n - 1][0] == "up")
            s = [x for x in order if x < RING - 1 or not narrow][0]
            order.remove(s)
            order.append(s)
            slot_of.append(s)
            before_load.append(owner[s])
            owner[s] = unit_done[n]
            if key[0] == "up":
                owner[RING - 1] = ("psum_ready", group[unit_end[key]] + 1)
            cnt[s] += 16 * len(pieces)
            landed.append((s, cnt[s]))
        unit_landed = [sem(f"unit_landed{i}") for i in range(RING)]
        units_used = sem("units_used")
        psum_ready = sem("psum_ready")
        w_high, w_low, w_low_v = sem("weights_high"), sem("weights_low_gate"), sem("weights_low_value")
        x_high, x_low = sem("input_high"), sem("input_low")
        SEM = {"psum_ready": psum_ready, "units_used": units_used, "w_low": w_low_v}
        freed = {"act": sem("freed_by_act"), "dve": sem("freed_by_dve")}
        params_landed = sem("params_landed")
        rows_landed = sem("gate_bias_landed")
        zeros_ready, silu_c = sem("zeros_ready"), sem("silu_c_ready")
        modp_ready = sem("modp_ready")
        coef_ready = sem("coef_ready")
        ss_ready, std_ready, xn_ready = sem("square_sum_ready"), sem("std_ready"), sem("normed_ready")
        hT_ready = sem("hT_ready")
        qkv_ready, qk_ready, qT_ready = sem("qkv_ready"), sem("qk_normed"), sem("qT_ready")
        max_ready, p_ready, sum_ready, pt_ready = sem("max_ready"), sem("p_ready"), sem("sum_ready"), sem("pt_ready")
        o_ready = sem("o_ready")
        state_k, kdec_ready, diff_ready, exp_ready, qk_scaled = (
            sem("gate_logs"), sem("kdec_ready"), sem("diff_ready"), sem("exp_ready"), sem("qk_scaled"))
        sig_ready, forget_ready, kd_turned, lb_ready, exp_lb = (
            sem("sigmoid_ready"), sem("forget_ready"), sem("kdec_turned"), sem("lb_ready"), sem("lb_exp"))
        x2_ready, merged_ready, y_ready, route_ready, rank_ready = (
            sem("x2_ready"), sem("merged_ready"), sem("y_ready"), sem("chosen_ready"), sem("table_ready"))
        out_ready, route_max, gate_exp = sem("out_ready"), sem("route_max_ready"), sem("gate_exp_ready")
        ln_landed, rw_landed = sem("ln_landed"), sem("router_landed")
        gate_landed, up_landed, down_landed = sem("moe_gate_landed"), sem("moe_up_landed"), sem("moe_down_landed")
        sel_ready, gx_ready, xg_ready, gt_ready, selgT_ready = (
            sem("sel_ready"), sem("gather_closed"), sem("xg_ready"), sem("selt_closed"), sem("selgT_ready"))
        gg_ready, gu_ready, hm_ready, sg_ready, hh_ready = (
            sem("gate_closed"), sem("up_closed"), sem("hm_ready"), sem("sg_ready"), sem("hidden_ready"))
        ht_ready, hhT_ready, gd_ready, yg_ready, c_ready, c_added = (
            sem("hiddent_closed"), sem("hhT_ready"), sem("down_closed"), sem("yg_ready"), sem("combine_closed"),
            sem("combine_added"))
        gates_read = sem("gates_read")
        conv1, conv2, silu_ready, hid_ready = sem("gate_scaled"), sem("conv_done"), sem("silu_ready"), sem("hid_ready")
        res_ready = sem("residual_ready")
        act_step, dve_step, dve_link = sem("act_step"), sem("dve_step"), sem("dve_link")
        stored = sem("stored")

        def helpers(eng, own, name):
            count, got, last = {}, {}, [-1]

            def do(ins, s=own, n=1):
                count[s.name] = count.get(s.name, 0) + n
                ins.then_inc(s, n)
                eng.wait_ge(s, count[s.name])

            def signal(s):
                count[s.name] = count.get(s.name, 0) + 1
                eng.sem_inc(s, 1)

            def await_next(s, n=1):
                got[s.name] = got.get(s.name, 0) + n
                eng.wait_ge(s, got[s.name])

            def take(key):
                g = group[key]
                assert reader[g] == name and g > last[0], key
                last[0] = g
                eng.wait_ge(psum_ready, g + 1)
                return PS[g % BANKS]

            def pe_past(key):
                eng.wait_ge(psum_ready, group[key] + 1)

            return do, signal, await_next, take, pe_past

        block = ctx.enter_context(nc.Block())

        def expert_units(sp, e, i, first=False):
            def rows_of(w, e, j):
                return w[0][bass.ds(e, 1)].rearrange("e (k p) n -> p (e k) n", p=P)[:, 4 * j:4 * j + 4, :]

            def cols_of(w, e, j):
                return w[0][bass.ds(e, 1)].rearrange("e (k p) n -> p (e k) n", p=P)[:, :, 512 * j:512 * j + 512]

            def slot_free(n):
                if first and n < RING:
                    sp.wait_ge(SEM[owner[n][0]], owner[n][1])
                if first and n == RING:
                    sp.wait_ge(psum_ready, group[("turn", "m2", 1, 1)] + 1)

            b_src = lambda name: a[name][0][bass.ds(e, 1)]
            if not first:
                sp.wait_ge(gg_ready, i)
            for j in range(2):
                slot_free(j)
                sp.dma_start(moe_slot[j].rearrange("p (k n) -> p k n", k=KC), cols_of(a["w_gate_2"], e, j))\
                    .then_inc(gate_landed, 16)
            if not first:
                sp.dma_start(bias[0:1, :], b_src("b_gate_2")).then_inc(gate_landed, 16)
                sp.wait_ge(gu_ready, i)
            for j in range(2):
                slot_free(2 + j)
                if first and j == 1:
                    sp.dma_start(bias[0:1, :], b_src("b_gate_2")).then_inc(gate_landed, 16)
                sp.dma_start(moe_slot[2 + j].rearrange("p (k n) -> p k n", k=KC), cols_of(a["w_up_2"], e, j))\
                    .then_inc(up_landed, 16)
            sp.dma_start(bias[32:33, :], b_src("b_up_2")).then_inc(up_landed, 16)
            if not first:
                sp.wait_ge(gd_ready, i)
            for j in range(2):
                sp.dma_start(moe_slot[4 + j].rearrange("p (k n) -> p k n", k=4), rows_of(a["w_down_2"], e, j))\
                    .then_inc(down_landed, 16)
            sp.dma_start(bias[64:65, :], b_src("b_down_2")).then_inc(down_landed, 16)

        def far_item(eng, j):
            return eng.value_load(fari[0:1, bass.ds(j, 1)], min_val=0, max_val=E - 1)

        def further(eng, body, before=None):
            n = eng.value_load(nfar[0:1, 0:1], min_val=0, max_val=ITEMS)
            with eng.If(n > 0):
                if before is not None:
                    before()
                with eng.Fori(0, n) as j:
                    body(j)

        def moe_sync(sp):
            sp.wait_ge(psum_ready, group[("turn", "ob2", 1, 1)] + 1)
            sp.dma_start(rw[:, :, :], a["router_w_2"][0].rearrange("(k p) n -> p k n", p=P)).then_inc(rw_landed, 16)
            expert_units(sp, 0, 0, first=True)
            with sp.Fori(1, E) as e:
                expert_units(sp, e, e)
            sp.wait_ge(rank_ready, 1)
            further(sp, lambda j: expert_units(sp, far_item(sp, j), j + E))
            sp.wait_ge(out_ready, 1)
            sp.dma_start(out[0].rearrange("(t p) d -> p t d", p=P), xr[:, 0:XT, :]).then_inc(stored, 16)
            sp.wait_ge(stored, 16)

        def low_part(eng, l, fc, g, then):
            s = slot_of[unit_no[("up", l, fc // 2)]]
            raw = ring[:, s, :].rearrange("p (k g i c) -> p k g i c", k=KC, g=2, i=2)[:, :, g, fc % 2, :]
            w = w_split[fc % 2]
            then(eng.tensor_tensor(w[:, 1, :, g, :], raw, w[:, 0, :, g, :].bitcast(F32), ALU.subtract))

        @block.gpsimd
        def _(pool):
            for l in range(2):
                for fc in range(FC):
                    pool.wait_ge(w_high, 2 * (l * FC + fc) + 1)
                    low_part(pool, l, fc, 0, lambda ins: ins.then_inc(w_low, 1))

        @block.sync
        def _(sp):
            sp.dma_start(cols[:, :], a["cols"]).then_inc(params_landed, 16)
            sp.dma_start(const[:, :], a["const"]).then_inc(params_landed, 16)
            sp.dma_start(rows[:, :], a["rows"].partition_broadcast(P)).then_inc(params_landed, 16)
            sp.dma_start(xr[:, 0:XT, :], a["x"][0].rearrange("(t p) d -> p t d", p=P)).then_inc(params_landed, 16)
            sp.dma_start(xr[:, XT:NT, :], a["ctx"][0].rearrange("(t p) d -> p t d", p=P)).then_inc(params_landed, 16)
            sp.dma_start(mask_in, a["masks"]).then_inc(params_landed, 16)
            for g in range(2):
                sec = a["ada_b"][0][(2 + 3 * g) * D:(3 + 3 * g) * D]
                for row in (2 * g, 2 * g + 1):
                    sp.dma_start(gb[:, row, :], sec.partition_broadcast(P)).then_inc(rows_landed, 16)
            upto = unit_no[{'att0': ('wo0', 1), 'l0': ('down', 0, 5), 'h1': ('wo1', 1), 'l1': ('down', 1, 5),
                            'mix2': ('wo2', 1), None: ('wo2', 1)}[stop]] + 1
            for n, pieces in enumerate(units[:upto]):
                if before_load[n]:
                    sp.wait_ge(SEM[before_load[n][0]], before_load[n][1])
                    if before_load[n][0] == "w_low":
                        sp.wait_ge(w_low, before_load[n][1])
                if n == unit_no[("w2", 3)]:
                    for i, name in enumerate(("ln1_g_2", "ln1_b_2", "ln2_g_2", "ln2_b_2")):
                        sp.dma_start(gb[:, i, :], a[name][0].partition_broadcast(P)).then_inc(ln_landed, 16)
                for dst, src in pieces:
                    sp.dma_start(dst(slot_of[n]), src).then_inc(unit_landed[slot_of[n]], 16)
                if n == unit_no[("wo0", 1)] + 3:
                    sp.wait_ge(gates_read, 1)
                    for g, row in ((0, 0), (1, 1)):
                        sec = a["ada_b"][1][(2 + 3 * g) * D:(3 + 3 * g) * D]
                        sp.dma_start(gb[:, row, :], sec.partition_broadcast(P)).then_inc(rows_landed, 16)
            if stop is None:
                moe_sync(sp)
            if stop is not None:
                sp.wait_ge(stored, 1)
                for dst, src in dbg:
                    sp.dma_start(dst, {'xr': xr, 'hT': hT, 'arena': arena}[src][:, :, :]).then_inc(stored, 16)
                sp.wait_ge(stored, 1 + 16 * len(dbg))

        @block.tensor
        def _(pe):
            got = {}

            def await_next(s, n=1):
                got[s.name] = got.get(s.name, 0) + n
                pe.wait_ge(s, got[s.name])

            def bank(key):
                g = group[key]
                if g >= BANKS:
                    pe.wait_ge(freed[reader[g - BANKS]], nth[g - BANKS])
                return PS[g % BANKS]

            closed = [0]

            def close(ins, key):
                assert group[key] == closed[0], (key, group[key], closed[0])
                closed[0] += 1
                ins.then_inc(psum_ready, 1)

            used = [0]

            def unit(key):
                n = unit_no[key]
                assert n == used[0], (key, n, used[0])
                s, count = landed[n]
                pe.wait_ge(unit_landed[s], count)
                return s

            def release(ins):
                if unit_done[used[0]][0] == "units_used":
                    ins.then_inc(units_used, 1)
                used[0] += 1

            def mm(o, l, r, start, stop):
                return pe.matmul(o, l, r, start=start, stop=stop)

            def ada(l, blk):
                s = unit(("ada", l, blk))
                ps = bank(("adap", l, blk))
                for k in range(KC):
                    j = k % 4
                    m = mm(ps[32 * j:32 * j + 32, :], cT[:, k, :], ring_col(s, 0, 512)[:, k, :], k < 4, k >= 4)
                close(m, ("adap", l, blk))
                release(m)

            def ada2(l, blk):
                await_next(modp_ready)
                key = ("adat", l, blk)
                ps = bank(key)
                for i in range(4):
                    m = mm(ps[:, 2 * i:2 * i + 2], modp[:, ada_turn[l, blk], i * P:(i + 1) * P], C("sel2"), True, True)
                close(m, key)
                for row, v in gate_slots(l, blk):
                    key = ("adag", l, blk, row)
                    close(mm(bank(key)[:, :], C("selb", v * P, P), modp[:, ada_turn[l, blk], :], True, True), key)

            def turn(tag, tiles, src, ready, chunks=KC):
                for t in tiles:
                    ready(t)
                    for h in range((chunks + 3) // 4):
                        key = ("turn", tag, t, h)
                        ps = bank(key)
                        n = min(4, chunks - 4 * h)
                        for i in range(n):
                            k = 4 * h + i
                            m = pe.transpose(ps[:, i * P:(i + 1) * P], src(t)[:, k * P:(k + 1) * P], ident)
                        close(m, key)

            def stay(key, s, lo, n, t, rel=False, first=True, last=True):
                ps = bank(key)
                for k in range(KC):
                    m = mm(ps[:, 0:n], hT[:, k, t * P:(t + 1) * P], ring_col(s, lo, n)[:, k, :], k == 0, k == KC - 1)
                close(m, key)
                return m

            def move(key, s, lo, n, T, t0=0, o=0, close_it=True):
                ps = bank(key)
                for k in range(KC):
                    m = mm(ps[o:o + n, 0:T], ring_col(s, lo, n)[:, k, :], hT[:, k, t0:t0 + T], k == 0, k == KC - 1)
                if close_it:
                    close(m, key)
                return m

            def attention(us, between):
                for i in range(len(us) + 1):
                    if i < len(us):
                        u = us[i]
                        for r in range(nrows(u)):
                            key = ("score", u["tag"], r)
                            close(mm(bank(key)[:, 0:u["n"]], u["q"](r), u["k"](r), True, True), key)
                    if i == 0:
                        continue
                    u = us[i - 1]
                    n, nr, c = u["n"], nrows(u), u["n"] // P
                    await_next(p_ready)
                    pr = SB[:, (i - 1) % 2, :]
                    pv = None
                    for r in range(nr + 1):
                        if r < nr:
                            key = ("probt", u["tag"], r)
                            ps = bank(key)
                            for j in range(c):
                                m = pe.transpose(ps[:, j * P:(j + 1) * P], pr[:, r * n + j * P:r * n + (j + 1) * P],
                                                 ident)
                            close(m, key)
                        if r:
                            await_next(pt_ready)
                            if pv is None:
                                pv = bank(("pv", u["tag"]))
                            q = r - 1
                            lo = q * HD if u["heads"] == 4 else 0
                            many = u["heads"] == 4
                            for j in range(c):
                                m = mm(pv[:, lo:lo + HD], PT[:, q % 2, j * P:(j + 1) * P], u["v"](q, j),
                                       j == 0 and (many or q == 0), j == c - 1 and (many or q == nr - 1))
                    close(m, ("pv", u["tag"]))
                    between(i - 1)

            def project(name, tiles):
                for b in range(2):
                    s = unit((name, b))
                    for t in tiles:
                        m = stay((name, b, t), s, 0, 512, t)
                    release(m)

            def ffn(l, T):
                turn(("f", l), range(T), lambda t: xn[:, t % 2, :], lambda t: await_next(xn_ready))
                await_next(x_low, 2 * T)
                for j in range(FC // 2):
                    assert unit_no[("up", l, j)] == used[0]
                    for i in range(2):
                        w = w_split[i]
                        for g, (name, low) in enumerate((("gate", w_low), ("val", w_low_v))):
                            await_next(low)
                            key = (name, l, 2 * j + i)
                            ps = bank(key)
                            parts = [(k, *p) for k in range(KC) for p in ((0, hT_high), (0, hT_low), (1, hT_high))]
                            for n, (k, part, x) in enumerate(parts):
                                m = mm(ps[:, 0:T * P], w[:, part, k, g, :], x[:, k, 0:T * P], n == 0,
                                       n == len(parts) - 1)
                            close(m, key)
                    release(m)
                    if l == 0 and j < 4:
                        ada(1, ADA_LATE[j])
                        ada2(1, ADA_LATE[j])
                for u in range((FC + 3) // 4):
                    s = unit(("down", l, u))
                    n = min(4, FC - 4 * u)
                    await_next(hid_ready, n)
                    for t in range(T):
                        for h in range(2):
                            key = ("down", l, t, h)
                            ps = bank(key)
                            for i in range(n):
                                k = 4 * u + i
                                m = mm(ps[:, :], hid[:, k, t * P:(t + 1) * P], ring_row(s, n)[:, i, h * 512:(h + 1) * 512],
                                       k == 0, k == FC - 1)
                            if 4 * u + n == FC:
                                close(m, key)
                    release(m)

            pe.wait_ge(params_landed, 96)
            await_next(silu_c)
            for blk in range(4):
                ada(0, blk)
                ada2(0, blk)
            turn("a0", ALL, lambda t: xn[:, t % 2, :], lambda t: await_next(xn_ready))
            await_next(hT_ready)
            for b in range(3):
                s = unit(("qkv", b))
                for t in ALL:
                    m = stay(("qkv", b, t), s, 0, 512, t)
                release(m)
            for t in ALL:
                await_next(qk_ready)
                sbt = SB[:, t % 2, :]
                q = (sbt if t < XT else qkv[:, t, :])
                for j in range(3):
                    key = ("qkt", t, j)
                    ps = bank(key)
                    for i in range(4):
                        src = q[:, (4 * j + i) * P:(4 * j + i + 1) * P] if j < 2 else \
                            sbt[:, 1280 + i * P:1280 + (i + 1) * P]
                        m = pe.transpose(ps[:, i * P:(i + 1) * P], src, ident)
                    close(m, key)
            await_next(qT_ready)

            def with_ada(i):
                ada(*ADA_BETWEEN[i])
                ada2(*ADA_BETWEEN[i])

            attention(ATT0, with_ada)
            await_next(o_ready)
            turn("o0", ALL, lambda t: qkv[:, t, 0:D], lambda t: None)
            await_next(hT_ready)
            project("wo0", ALL)
            if stop == "att0":
                return
            ffn(0, NT)
            if stop == "l0":
                return

            turn("h1", ALL, lambda t: xn[:, t % 2, :], lambda t: await_next(xn_ready))
            await_next(hT_ready)
            for b in range(2):
                s = unit(("hq", b))
                for i in range(4):
                    m = move(("hq", 4 * b + i), s, i * P, P, SEQ)
                release(m)
            for name, tiles in (("hv", ALL), ("hg", XS)):
                project(name, tiles)
            def forget(d, b, i):
                s = unit(("hf", d, b)) if i == 0 else slot_of[unit_no[("hf", d, b)]]
                m = move(("hf", d, b, i), s, i * P, P, TOK)
                if i == 3:
                    release(m)

            for i in range(4):
                forget(0, 0, i)
            for d in range(2):
                late = 1 - d
                for b in range(2):
                    rk = rks[b]
                    for i in range(4):
                        if i == 0:
                            await_next(kdec_ready)
                        key = ("kt", d, b, i)
                        ps = bank(key)
                        for t in range(2):
                            m = pe.transpose(ps[:, t * P:(t + 1) * P], rE[:, i, t * P:(t + 1) * P], ident)
                        close(m, key)
                        await_next(kd_turned)
                        key = ("st", d, b, i)
                        ps = bank(key)
                        h = 4 * b + i
                        for t in range(2):
                            m = mm(ps[:, 0:P], rD[:, i % 2, t, :], rv[:, XT + t, h * P:(h + 1) * P], t == 0, t == 1)
                        close(m, key)
                    for n in range(-1, NL + 1):
                        if n >= 0:
                            await_next(qk_scaled)
                        for t in ([late] if n == NL else XS):
                            key = ("lev", d, b, n, 0 if n == NL else t)
                            ps = bank(key)
                            for i in range(4):
                                if n < 0:
                                    l, r = rk[:, i, t * P:(t + 1) * P], rq[:, 4 * b + i, t * P:(t + 1) * P]
                                else:
                                    st = 1 - t if n == NL else t
                                    l, r = KL[n % 2][:, i, st * P:(st + 1) * P], QL[n % 2][:, i, t * P:(t + 1) * P]
                                m = mm(ps[:, i * P:(i + 1) * P], l, r, True, True)
                            close(m, key)
                        if n >= 0 and n % 2 == 0 and after(d, b):
                            forget(*after(d, b), n // 2)
                    await_next(qk_scaled)
                    await_next(o_ready)
                    for t in XS:
                        key = ("ro", d, b, t)
                        ps = bank(key)
                        for i in range(4):
                            h = 4 * b + i
                            o = ps[:, i * P:(i + 1) * P]
                            mm(o, QL[(NL + 1) % 2][:, i, t * P:(t + 1) * P], rS[:, i, :], True, False)
                            if t == late:
                                mm(o, rC[:, i, :], rv[:, 1 - late, h * P:(h + 1) * P], False, False)
                            m = mm(o, rA[:, t, i, :], rv[:, t, h * P:(h + 1) * P], False, True)
                        close(m, key)
            await_next(o_ready)
            turn("o1", XS, lambda t: ro[:, t, :], lambda t: None)
            await_next(hT_ready)
            project("wo1", XS)
            if stop == "h1":
                return
            ffn(1, XT)
            if stop == "l1":
                return
            await_next(x2_ready)
            turn("x2", XS, lambda t: xr[:, t, :], lambda t: None)
            await_next(hT_ready)
            at, s = -1, None
            for u, kind, c, dst in W2:
                if u != at:
                    if at >= 0:
                        release(m)
                    at, s = u, unit(("w2", u))
                if kind == "T":
                    m = move(("w2", dst), s, c, P, SEQ)
                elif kind == "K":
                    for o in (0, 64):
                        m = move(("w2", dst), s, c, 64, SEQ, o=o, close_it=o == 64)
                else:
                    for t in XS:
                        m = stay(("w2", dst, t), s, c[0], c[1], t)
            release(m)
            await_next(qT_ready)
            attention(ATT2, lambda i: None)
            await_next(o_ready)
            turn("oa2", XS, lambda t: oA[:, t, :], lambda t: None, chunks=2)
            turn("ob2", XS, lambda t: oB[:, t, :], lambda t: None)
            await_next(hT_ready)
            sa, sbs = unit(("pa", 0)), None
            release(None)
            for b in range(2):
                s = unit(("pb", b))
                for t in XS:
                    ps = bank(("pa", b, t))
                    for k in range(2):
                        m = mm(ps[:, :], hT[:, k, SEQ + t * P:SEQ + (t + 1) * P],
                               ring_row(sa, 2)[:, k, b * 512:(b + 1) * 512], k == 0, k == 1)
                    close(m, ("pa", b, t))
                    m = stay(("pb", b, t), s, 0, 512, t)
                release(m)
            await_next(merged_ready)
            turn("m2", XS, lambda t: ga[:, t, :], lambda t: None)
            await_next(hT_ready)
            project("wo2", XS)
            if stop == "mix2":
                return
            await_next(y_ready)
            turn("y2", XS, lambda t: xr[:, t, :], lambda t: None)
            await_next(hT_ready)
            pe.wait_ge(rw_landed, 16)
            ps = bank(("route",))
            for t in XS:
                for k in range(KC):
                    m = mm(ps[:, t * E:(t + 1) * E], hT[:, k, t * P:(t + 1) * P], rw[:, k, :], k == 0, k == KC - 1)
            close(m, ("route",))
            await_next(route_ready)
            ps = bank(("rank",))
            mm(ps[:, 0:E], C("before"), chosen[:, 0, :], True, True)
            mm(ps[:, E:2 * E], C("ones"), chosen[:, 0, :], True, False)
            mm(ps[:, E:2 * E], C("before"), chosen[:, 1, :], False, True)
            mm(ps[:, 2 * E:3 * E], C("ones"), chosen[:, 0, :], True, False)
            close(mm(ps[:, 2 * E:3 * E], C("ones"), chosen[:, 1, :], False, True), ("rank",))
            pe.wait_ge(freed["dve"], nth[-1])
            BG, BU, BX, BS, BH, BD = PS[:6]

            def gather():
                for k in range(KC):
                    for t in XS:
                        m = mm(BX[:, k * SLOTS:(k + 1) * SLOTS], xr[:, t, k * P:(k + 1) * P], sel[:, t, 0:SLOTS],
                               t == 0, t == 1)
                m.then_inc(gx_ready, 1)

            def turn_sel():
                for t in XS:
                    m = pe.transpose(BS[:, t * P:(t + 1) * P], selg[:, t, :], ident)
                m.then_inc(gt_ready, 1)

            def item(i, ahead):
                def halves(out, slots, row, done):
                    for k in range(KC):
                        for f in range(2):
                            mm(out[64 * f:64 * f + 64, :], xg[:, k, :],
                               moe_slot[slots + f].rearrange("p (k n) -> p k n", k=KC)[:, k, :], k == 0, False)
                    for f in range(2):
                        m = mm(out[64 * f:64 * f + 64, :], C("ones")[row:row + 1, 0:64],
                               bias[row:row + 1, f * 512:(f + 1) * 512], False, True)
                    m.then_inc(done, 1)

                pe.wait_ge(gate_landed, 48 * (i + 1))
                pe.wait_ge(xg_ready, i + 1 + ahead)
                halves(BG, 0, 0, gg_ready)
                pe.wait_ge(up_landed, 48 * (i + 1))
                halves(BU, 2, 32, gu_ready)
                pe.wait_ge(sel_ready, i + 2 + 2 * ahead)
                gather()
                pe.wait_ge(hh_ready, i + 1)
                for c in range(4):
                    m = pe.transpose(BH[:, c * P:(c + 1) * P], hh[:, c * P:(c + 1) * P], ident)
                m.then_inc(ht_ready, 1)
                pe.wait_ge(down_landed, 48 * (i + 1))
                pe.wait_ge(hhT_ready, i + 1)
                for k in range(KC):
                    for h in range(2):
                        mm(BD[64 * h:64 * h + 64, :], hhT[:, k % 4, 64 * (k // 4):64 * (k // 4) + 64],
                           moe_slot[4 + k // 4].rearrange("p (k n) -> p k n", k=4)[:, k % 4, h * 512:(h + 1) * 512],
                           k == 0, False)
                for h in range(2):
                    m = mm(BD[64 * h:64 * h + 64, :], C("ones")[64:65, 0:64], bias[64:65, h * 512:(h + 1) * 512],
                           False, True)
                m.then_inc(gd_ready, 1)
                pe.wait_ge(yg_ready, i + 1)
                pe.wait_ge(selgT_ready, i + 1 + ahead)
                for j in range(4):
                    h, t = j // 2, j % 2
                    pe.wait_ge(c_added, 4 * i + 1 + max(j - 1, 0))
                    mm(PS[6 + t][:, :], selgT[64 * h:64 * h + 64, t, :], yg[64 * h:64 * h + 64, :], True, True)\
                        .then_inc(c_ready, 1)
                turn_sel()

            pe.wait_ge(sel_ready, 1)
            gather()
            turn_sel()
            with pe.Fori(0, E) as i:
                item(i, 0)

            pe.wait_ge(rank_ready, 1)

            def first_further():
                pe.wait_ge(sel_ready, E + 3)
                pe.wait_ge(xg_ready, E + 1)
                gather()
                pe.wait_ge(selgT_ready, E + 1)
                turn_sel()

            further(pe, lambda j: item(j + E, 1), first_further)

        @block.scalar
        def _(act):
            do, signal, await_next, take, pe_past = helpers(act, act_step, "act")
            F = freed["act"]

            def ada(l, blk):
                ps = take(("adap", l, blk))
                do(act.activation(modp[:, ada_turn[l, blk], :], ps[:, :], ACT.Copy), F)
                signal(modp_ready)

            def std(n, width, eps="eps6"):
                await_next(ss_ready)
                do(act.activation(stat[:, n:n + width], stat[:, n:n + width], ACT.Sqrt, bias=C(eps)[:, 0:1],
                                  scale=1.0 / {1: D, 20: HD, 8: P}[width]), std_ready)

            def norm_turn(tag, tiles, l, i, split=False):
                for t in tiles:
                    std(t, 1)
                await_next(coef_ready)
                for t in tiles:
                    v = 0 if t < XT else 1
                    for h in range(2):
                        ps = take(("turn", tag, t, h))
                        if split:
                            split_no[0] += 1
                            if split_no[0] > 2:
                                act.wait_ge(x_low, split_no[0] - 2)
                        for j in range(4):
                            k = 4 * h + j
                            o = modp[:, h, j * P:(j + 1) * P] if split else hT[:, k, t * P:(t + 1) * P]
                            do(act.activation(o, ps[:, j * P:(j + 1) * P], ACT.Identity,
                                              bias=modT[:, l, 24 * i + k, v:v + 1], scale=coef[:, l, i, k, v:v + 1]),
                               F if j == 3 else act_step)
                        if split:
                            do(act.activation(hT_high[:, 4 * h:4 * h + 4, t * P:(t + 1) * P],
                                              modp[:, h, :].rearrange("p (k c) -> p k c", k=4), ACT.Copy), x_high)
                if not split:
                    signal(hT_ready)

            def plain_turn(tag, tiles, chunks=KC, tell=True, at=0, shift=0):
                for t in tiles:
                    for h in range((chunks + 3) // 4):
                        ps = take(("turn", tag, t, h))
                        n = min(4, chunks - 4 * h)
                        do(act.activation(hT[:, at + 4 * h:at + 4 * h + n, shift + t * P:shift + (t + 1) * P],
                                          ps[:, 0:n * P].rearrange("p (k q) -> p k q", k=n), ACT.Copy), F)
                if tell:
                    signal(hT_ready)

            def attention(us, between):
                for i in range(len(us) + 1):
                    if i:
                        u = us[i - 1]
                        for r in range(nrows(u)):
                            ps = take(("probt", u["tag"], r))
                            do(act.activation(PT[:, r % 2, 0:u["n"]], ps[:, 0:u["n"]], ACT.Copy), F)
                            signal(pt_ready)
                        between(i - 1)
                    if i == len(us):
                        continue
                    u = us[i]
                    n, hs = u["n"], u["heads"]
                    w = n if hs == 4 else 3 * n
                    st = stat[:, 64 + 32 * (i % 2):96 + 32 * (i % 2)]
                    await_next(max_ready)
                    for r in range(hs):
                        pr = SB[:, i % 2, r * w:(r + 1) * w]
                        do(act.activation(pr, pr, ACT.Exp, bias=st[:, 4 + r:5 + r], accum_out=st[:, 12 + r:13 + r]))
                    signal(p_ready)
                    if u["sink"] is not None:
                        do(act.activation(st[:, 8:12], st[:, 8:12], ACT.Exp))
                    signal(sum_ready)

            def ffn(l, T):
                norm_turn(("f", l), range(T), l, 1, split=True)
                n = T * P

                def weights_high(fc):
                    s, count = landed[unit_no[("up", l, fc // 2)]]
                    act.wait_ge(unit_landed[s], count)
                    if fc >= 2:
                        pe_past(("val", l, fc - 2))
                    raw = ring[:, s, :].rearrange("p (k g i c) -> p k g i c", k=KC, g=2, i=2)
                    for g in range(2):
                        do(act.activation(w_split[fc % 2][:, 0, :, g, :], raw[:, :, g, fc % 2, :], ACT.Copy), w_high)

                weights_high(0)
                weights_high(1)
                for fc in range(FC):
                    ps = take(("gate", l, fc))
                    t1 = ft[:, fc % 2, 0:n]
                    if fc >= 2:
                        act.wait_ge(silu_used, (FC if l else 0) + fc - 1)
                    do(act.activation(t1, ps[:, 0:n], ACT.Identity, bias=COL("cb", l * FC + fc, 1),
                                      scale=COL("cw", (l * 3 + 1) * FC + fc, 1)), conv1)
                    await_next(conv2)
                    do(act.activation(ft[:, 2 + fc % 2, 0:n], t1, ACT.Silu), silu_ready)
                    signal(F)
                    if fc + 2 < FC:
                        weights_high(fc + 2)
                    if l == 0 and fc % 2 and fc < 8:
                        ada(1, ADA_LATE[fc // 2])

            silu_used = hid_ready
            split_no = [0]
            act.wait_ge(params_landed, 96)
            await_next(zeros_ready)
            do(act.activation(cT[:, :, 0:2], COL("c").rearrange("p (k v) -> p k v", v=2), ACT.Silu), silu_c)
            for blk in range(4):
                ada(0, blk)
            norm_turn("a0", ALL, 0, 0)
            for b in range(3):
                for t in ALL:
                    ps = take(("qkv", b, t))
                    do(act.activation(qkv[:, t, b * 512:(b + 1) * 512], ps[:, :], ACT.Copy), F)
                    if b == 2:
                        signal(qkv_ready)
            for t in ALL:
                std(t * 20, 20)
                for j in range(3):
                    ps = take(("qkt", t, j))[:, :].rearrange("p (k q) -> p k q", k=4)
                    if j < 2:
                        do(act.activation(qT[:, 4 * j:4 * j + 4, t * P:(t + 1) * P], ps, ACT.Copy), F)
                    else:
                        for z in range(2):
                            o = kT[64 * z:64 * z + 64, z::2, t * P:(t + 1) * P]
                            do(act.activation(o, ps[64 * z:64 * z + 64, :, :], ACT.Copy), F if z else act_step)
            signal(qT_ready)

            def with_ada(i):
                ada(*ADA_BETWEEN[i])

            attention(ATT0, with_ada)
            plain_turn("o0", ALL)
            if stop == "att0":
                return
            ffn(0, NT)
            if stop == "l0":
                return

            norm_turn("h1", ALL, 1, 0)
            await_next(lb_ready)
            do(act.activation(stat[:, 176:192], stat[:, 176:192], ACT.Exp), exp_lb)
            for i in range(HG):
                ps = take(("hq", i))
                do(act.activation(rq[:, i, :], ps[:, 0:SEQ], ACT.Silu), F)
            for b in range(2):
                for t in ALL:
                    ps = take(("hv", b, t))
                    do(act.activation(rv[:, t, b * 512:(b + 1) * 512], ps[:, :], ACT.Copy), F)
            for b in range(2):
                for t in XS:
                    ps = take(("hg", b, t))
                    do(act.activation(rg[:, t, b * 512:(b + 1) * 512], ps[:, :], ACT.Silu), F)
            def forget(d, b, i):
                ps = take(("hf", d, b, i))
                do(act.activation(rks[b][:, i, :], ps[:, :], ACT.Copy), F)

            for i in range(4):
                forget(0, 0, i)
            for d in range(2):
                for b in range(2):
                    rk = rks[b]
                    do(act.activation(rk[:, :, :], rk[:, :, :], ACT.Sigmoid), sig_ready)
                    await_next(forget_ready)
                    do(act.activation(rlog[:, :, :], rk[:, :, :], ACT.Ln), state_k)
                    await_next(diff_ready)
                    last = TOK - 1 if d == 0 else SEQ
                    for i in range(4):
                        do(act.activation(rE[:, i, :], rb[:, i, SEQ:TOK], ACT.Exp, bias=rb[:, i, last:last + 1],
                                          scale=-1.0), exp_ready if i == 3 else act_step)
                    for i in range(4):
                        ps = take(("kt", d, b, i))
                        do(act.activation(rD[:, i % 2, :, :], ps[:, 0:SEQ].rearrange("p (t c) -> p t c", t=2),
                                          ACT.Copy), F)
                        signal(kd_turned)
                        ps = take(("st", d, b, i))
                        do(act.activation(rS[:, i, :], ps[:, 0:P], ACT.Copy), F)
                    for n in range(NL + 1):
                        await_next(diff_ready)
                        h = LEVELS[n] if n < NL else P
                        n_late, n_early = late_early(EL[n % 2], h, d)
                        do(act.activation(n_late, n_late, ACT.Exp))
                        do(act.activation(n_early, n_early, ACT.Exp, scale=-1.0), exp_ready)
                        if n % 2 and after(d, b):
                            forget(*after(d, b), n // 2)
                    await_next(diff_ready)
                    do(act.activation(EL[(NL + 1) % 2], rb[:, :, 0:SEQ], ACT.Exp), exp_ready)
            for t in XS:
                std(t * 8, 8)
            plain_turn("o1", XS)
            if stop == "h1":
                return
            ffn(1, XT)
            if stop == "l1":
                return
            plain_turn("x2", XS)
            for u, kind, c, dst in W2:
                name, j = dst
                if kind == "N":
                    for t in XS:
                        ps = take(("w2", dst, t))
                        o = {"av": lambda: av[:, t, j:j + c[1]], "bv": lambda: bv[:, t, :],
                             "g": lambda: (ga if j < 2 else gb2)[:, t, j % 2 * 512:j % 2 * 512 + 512]}[name]()
                        do(act.activation(o, ps[:, 0:c[1]], ACT.Sigmoid if name == "g" else ACT.Copy), F)
                else:
                    ps = take(("w2", dst))
                    if j < (6 if name == "aT" else 8):
                        do(act.activation((aT if name == "aT" else bT)[:, j, :], ps[:, 0:SEQ], ACT.Copy,
                                          scale=HD ** -0.5), F)
                    else:
                        if (name, j) == ("aT", 6):
                            await_next(zeros_ready)
                        for z in range(2):
                            o = aK[:, 2 * (j - 6) + z, :] if name == "aT" else bK[:, 2 * (j - 8) + z, :]
                            do(act.activation(o[64 * z:64 * z + 64, :], ps[64 * z:64 * z + 64, 0:SEQ], ACT.Copy),
                               F if z else act_step)
            signal(qT_ready)
            attention(ATT2, lambda i: None)
            plain_turn("oa2", XS, chunks=2, tell=False, shift=SEQ)
            plain_turn("ob2", XS)
            plain_turn("m2", XS)
            for t in XS:
                std(t, 1, "eps5")
            if stop == "mix2":
                return
            plain_turn("y2", XS)
            await_next(route_max)
            for t in XS:
                do(act.activation(gate[:, t, :], lgx[:, t, 0:E], ACT.Exp, bias=tst[:, t:t + 1]),
                   gate_exp if t else act_step)

            def take_gather():
                act.activation(xg[:, :, :], PS[2][:, :].rearrange("p (k s) -> p k s", k=KC), ACT.Copy)\
                    .then_inc(xg_ready, 1)

            def take_sel():
                act.activation(selgT[:, :, :], PS[3][:, 0:2 * P].rearrange("p (t c) -> p t c", t=2), ACT.Copy)\
                    .then_inc(selgT_ready, 1)

            def item(i, ahead):
                act.wait_ge(hm_ready, i + 1)
                act.activation(sg[:, :], hm[:, :], ACT.Sigmoid, scale=1.702).then_inc(sg_ready, 1)
                act.wait_ge(gx_ready, i + 2 + ahead)
                take_gather()
                act.wait_ge(ht_ready, i + 1)
                act.activation(hhT[:, :, :], PS[4][:, :].rearrange("p (c s) -> p c s", c=4), ACT.Copy)\
                    .then_inc(hhT_ready, 1)
                act.wait_ge(gd_ready, i + 1)
                act.activation(yg[:, :], PS[5][:, :], ACT.Copy).then_inc(yg_ready, 1)
                act.wait_ge(gt_ready, i + 2 + ahead)
                take_sel()

            act.wait_ge(gx_ready, 1)
            take_gather()
            act.wait_ge(gt_ready, 1)
            take_sel()
            with act.Fori(0, E) as i:
                item(i, 0)
            act.wait_ge(rank_ready, 1)

            def first_further():
                act.wait_ge(gx_ready, E + 2)
                take_gather()
                act.wait_ge(gt_ready, E + 2)
                take_sel()

            further(act, lambda j: item(j + E, 1), first_further)
            for t in XS:
                std(t, 1, "eps5")

        @block.vector
        def _(dve):
            do, signal, await_next, take, pe_past = helpers(dve, dve_step, "dve")
            F = freed["dve"]
            TT, STT = dve.tensor_tensor, dve.scalar_tensor_tensor

            def rms(tag, tiles, before):
                for t in tiles:
                    if t >= 2:
                        pe_past(("turn", tag, t - 2, 1))
                    do(dve.tensor_tensor_reduce(out=xn[:, t % 2, :], in0=xr[:, t, :], in1=xr[:, t, :], scale=1.0,
                                                scalar=0.0, op0=ALU.mult, op1=ALU.add,
                                                accum_out=stat[:, t:t + 1]), ss_ready)
                    await_next(std_ready)
                    do(dve.reciprocal(stat[:, t:t + 1], stat[:, t:t + 1]))
                    do(dve.tensor_scalar(xn[:, t % 2, :], xr[:, t, :], stat[:, t:t + 1], None, ALU.mult), xn_ready)

            def ada2(l, blk):
                ps = take(("adat", l, blk))
                o = modT[:, l, 4 * blk:4 * blk + 4, :]
                do(TT(o, ps[:, 0:8].rearrange("p (k v) -> p k v", v=2),
                      COL("adab", l * 48 + 4 * blk, 4).unsqueeze(2).broadcast_to((P, 4, 2)), ALU.add), F)
                for row, v in gate_slots(l, blk):
                    ps = take(("adag", l, blk, row))
                    h = G_BLOCKS[blk][1]
                    if l == 0 and blk == 4 and row == 0:
                        dve.wait_ge(rows_landed, 64)
                    if l == 1 and blk == 4 and row == 0:
                        dve.wait_ge(rows_landed, 96)
                    o = gb[:, row, h * 512:(h + 1) * 512]
                    do(TT(o, o, ps[:, :], ALU.add), F)

            def coefs(l, i):
                sc = modT[:, l, 24 * i + 8:24 * i + 16, :]
                g = COL("n1" if i == 0 else "n2", l * 8, 8).unsqueeze(2).broadcast_to((P, 8, 2))
                do(STT(out=coef[:, l, i, :, :], in0=sc, scalar=1.0, in1=g, op0=ALU.add, op1=ALU.mult), coef_ready)

            def attention(us, between):
                for i in range(len(us) + 1):
                    if i < len(us):
                        u = us[i]
                        n, hs = u["n"], u["heads"]
                        st = stat[:, 64 + 32 * (i % 2):96 + 32 * (i % 2)]
                        for r in range(nrows(u)):
                            ps = take(("score", u["tag"], r))
                            o = SB[:, i % 2, r * n:(r + 1) * n]
                            if u["slope"]:
                                sl, diff = u["slope"][r]
                                do(STT(out=o, in0=diff, scalar=-sl, in1=ps[:, 0:n], op0=ALU.mult, op1=ALU.add), F)
                            elif u["mask"] is not None:
                                do(TT(o, ps[:, 0:n], u["mask"], ALU.add), F)
                            else:
                                do(dve.tensor_copy(o, ps[:, 0:n]), F)
                        w = n if hs == 4 else 3 * n
                        do(dve.tensor_reduce(st[:, 0:hs], SB[:, i % 2, 0:hs * w].rearrange("p (h w) -> p h w", h=hs),
                                             AX, ALU.max))
                        if u["sink"] is not None:
                            do(TT(st[:, 0:4], st[:, 0:4], u["sink"], ALU.max))
                            do(TT(st[:, 8:12], u["sink"], st[:, 0:4], ALU.subtract))
                        do(dve.tensor_scalar(st[:, 4:4 + hs], st[:, 0:hs], -1.0, None, ALU.mult), max_ready)
                    if i:
                        u = us[i - 1]
                        hs = u["heads"]
                        st = stat[:, 64 + 32 * ((i - 1) % 2):96 + 32 * ((i - 1) % 2)]
                        await_next(sum_ready)
                        if u["sink"] is not None:
                            do(TT(st[:, 12:16], st[:, 12:16], st[:, 8:12], ALU.add))
                        do(dve.reciprocal(st[:, 16:16 + hs], st[:, 12:12 + hs]))
                        ps = take(("pv", u["tag"]))
                        do(TT(u["out"].rearrange("p (h c) -> p h c", h=hs),
                              ps[:, 0:hs * HD].rearrange("p (h c) -> p h c", h=hs),
                              st[:, 16:16 + hs].unsqueeze(2).broadcast_to((P, hs, HD)), ALU.mult), F)
                        between(i - 1)
                signal(o_ready)

            def residual(key, tiles, gates):
                for b in range(2):
                    for t in tiles:
                        gated_add((key, b, t), b, t, gates)

            def gated_add(key, b, t, gates):
                ps = take(key)
                tmp = xn[:, 0, 0:512]
                o = xr[:, t, b * 512:(b + 1) * 512]
                do(TT(tmp, ps[:, :], gb[:, gates[0 if t < XT else 1], b * 512:(b + 1) * 512], ALU.mult), F)
                do(TT(o, o, tmp, ALU.add))

            def ffn(l, T):
                coefs(l, 1)
                rms(("f", l), range(T), None)
                for t in range(T):
                    for h in range(2):
                        await_next(x_high)
                        cut = (slice(None), slice(4 * h, 4 * h + 4), slice(t * P, (t + 1) * P))
                        do(TT(hT_low[cut], modp[:, h, :].rearrange("p (k c) -> p k c", k=4),
                              hT_high[cut].bitcast(F32), ALU.subtract), x_low)
                n = T * P

                def weights_low(fc):
                    await_next(w_high, 2)
                    low_part(dve, l, fc, 1, lambda ins: do(ins, w_low_v))

                weights_low(0)
                weights_low(1)
                seg = T // 2
                for fc in range(FC):
                    await_next(conv1)
                    g = PS[group[("gate", l, fc)] % BANKS][:, 0:n].rearrange("p (s t) -> p s t", s=seg)
                    t1 = ft[:, fc % 2, 0:n].rearrange("p (s t) -> p s t", s=seg)
                    cw = lambda i: COL("cw", (l * 3 + i) * FC + fc, 1)
                    do(STT(out=t1[:, :, 1:SEQ], in0=g[:, :, 0:SEQ - 1], scalar=cw(0), in1=t1[:, :, 1:SEQ],
                           op0=ALU.mult, op1=ALU.add))
                    do(STT(out=t1[:, :, 0:SEQ - 1], in0=g[:, :, 1:SEQ], scalar=cw(2), in1=t1[:, :, 0:SEQ - 1],
                           op0=ALU.mult, op1=ALU.add), conv2)
                    await_next(silu_ready)
                    ps = take(("val", l, fc))
                    do(TT(hid[:, fc, 0:n], ft[:, 2 + fc % 2, 0:n], ps[:, 0:n], ALU.mult), F)
                    signal(hid_ready)
                    if fc + 2 < FC:
                        weights_low(fc + 2)
                    if l == 0 and fc % 2 and fc < 8:
                        ada2(1, ADA_LATE[fc // 2])
                for t in range(T):
                    for h in range(2):
                        gated_add(("down", l, t, h), h, t, GATE[(l, 1)])

            do(dve.memset(cT[:, :, :], 0.0), zeros_ready)
            dve.wait_ge(params_landed, 96)
            do(dve.tensor_copy(masks[:, :], mask_in))
            do(dve.tensor_scalar(ROW("qg"), ROW("qg"), HD ** -0.5, None, ALU.mult))
            for blk in range(4):
                ada2(0, blk)
            coefs(0, 0)
            rms("a0", ALL, None)
            for z in range(2):
                do(dve.memset(kT[64 * z:64 * z + 64, 1 - z::2, :], 0.0))
            for t in ALL:
                await_next(qkv_ready)
                if t >= 2:
                    pe_past(("qkt", t - 2, 2))
                sbt = SB[:, t % 2, :]
                qk = qkv[:, t, 0:1280].rearrange("p (h c) -> p h c", h=20)
                sq = sbt[:, 0:1280].rearrange("p (h c) -> p h c", h=20)
                st = stat[:, t * 20:t * 20 + 20]
                do(TT(sq, qk, qk, ALU.mult))
                do(dve.tensor_reduce(st, sq, AX, ALU.add), ss_ready)
                await_next(std_ready)
                do(dve.reciprocal(st, st))
                do(TT(qk, qk, st.unsqueeze(2).broadcast_to((P, 20, HD)), ALU.mult))
                for lo, n, g in ((0, NH, "qg"), (NH, NKV, "kg")):
                    o = qk[:, lo:lo + n, :]
                    do(TT(o, o, ROW(g).unsqueeze(1).broadcast_to((P, n, HD)), ALU.mult))
                kn = qk[:, NH:20, :]
                if t < XT:
                    half = lambda v, j: v.rearrange("p h (r z c) -> p h r z c", r=2, z=2)[:, :, :, j, :]
                    x1, x2, o1, o2 = half(qk, 0), half(qk, 1), half(sq, 0), half(sq, 1)
                    tab = lambda f: C(f, t * 32, 32).rearrange("p (r c) -> p r c", r=2)
                    for r in range(2):
                        cs = [tab(f)[:, r, :].unsqueeze(1).broadcast_to((P, 20, 16)) for f in ("cos", "sin")]
                        tmp = PT[:, 0, 0:320].rearrange("p (h c) -> p h c", h=20)
                        do(TT(o1[:, :, r, :], x1[:, :, r, :], cs[0], ALU.mult))
                        do(TT(tmp, x2[:, :, r, :], cs[1], ALU.mult))
                        do(TT(o1[:, :, r, :], o1[:, :, r, :], tmp, ALU.subtract))
                        do(TT(o2[:, :, r, :], x1[:, :, r, :], cs[1], ALU.mult))
                        do(TT(tmp, x2[:, :, r, :], cs[0], ALU.mult))
                        do(TT(o2[:, :, r, :], o2[:, :, r, :], tmp, ALU.add))
                    kn = sq[:, NH:20, :]
                kd = sbt[:, 1280:1792].rearrange("p (g z c) -> p g z c", g=NKV, z=2)
                do(dve.tensor_copy(kd[:, :, 0, :], kn))
                do(dve.tensor_copy(kd[:, :, 1, :], kn), qk_ready)

            attention(ATT0, lambda i: ada2(*ADA_BETWEEN[i]))
            residual("wo0", ALL, GATE[(0, 0)])
            signal(gates_read)
            if stop == "att0":
                signal(stored)
                return
            ffn(0, NT)
            if stop == "l0":
                signal(stored)
                return

            coefs(1, 0)
            rms("h1", ALL, None)
            lbs, oml, ex = stat[:, 160:168], stat[:, 168:176], stat[:, 176:192]
            l2 = COL("lb").rearrange("p (l k) -> p l k", l=2)
            do(TT(lbs, l2[:, 0, :], l2[:, 1, :], ALU.max))
            do(TT(ex.rearrange("p (l k) -> p l k", l=2), l2, lbs.unsqueeze(1).broadcast_to((P, 2, 8)), ALU.subtract),
               lb_ready)
            await_next(exp_lb)
            do(TT(oml, ex[:, 0:8], ex[:, 8:16], ALU.add))
            do(dve.reciprocal(oml, oml))
            do(TT(lbs, ex[:, 8:16], oml, ALU.mult))
            do(dve.tensor_scalar(oml, lbs, -1.0, 1.0, ALU.mult, ALU.add))
            for v in (rQ, rK):
                do(dve.memset(v[:, :, :], 0.0))
            for d in range(2):
                late = 1 - d
                for b in range(2):
                    rk = rks[b]
                    await_next(sig_ready)
                    for i in range(4):
                        h = 4 * b + i
                        do(dve.tensor_scalar(rk[:, i, :], rk[:, i, :], oml[:, h:h + 1], lbs[:, h:h + 1], ALU.mult,
                                             ALU.add), forget_ready if i == 3 else dve_step)
                    await_next(state_k)
                    do(dve.tensor_scalar(rk[:, :, :], rk[:, :, :], -1.0, 1.0, ALU.mult, ALU.add))
                    for i in range(4):
                        for lo in (0, SEQ):
                            v = (lambda x: x[:, i, lo:lo + SEQ]) if d == 0 else \
                                (lambda x: x[:, i, lo:lo + SEQ][:, ::-1])
                            do(dve.tensor_tensor_scan(v(rb), C("ones", 0, 1).broadcast_to((P, SEQ)), v(rlog), 0.0,
                                                      ALU.mult, ALU.add), diff_ready if (i, lo) == (3, SEQ) else dve_step)
                    await_next(exp_ready)
                    do(TT(rE[:, :, :], rE[:, :, :], rk[:, :, SEQ:TOK], ALU.mult), kdec_ready)
                    bx, kx, qx = rb[:, :, 0:SEQ], rk[:, :, 0:SEQ], rq[:, 4 * b:4 * b + 4, :]

                    def sub(n):
                        h = LEVELS[n] if n < NL else P
                        if n < 2:
                            pe_past(("kt", d, b, 3) if n == 0 else ("lev", d, b, -1, 1))
                        ref = h - 1 if d == 0 else h
                        v = bx.rearrange("p i (n c) -> p i n c", c=2 * h)
                        o = EL[n % 2].rearrange("p i (n c) -> p i n c", c=2 * h)
                        do(TT(o, v, v[:, :, :, ref:ref + 1].broadcast_to((P, 4, SEQ // (2 * h), 2 * h)), ALU.subtract),
                           diff_ready)

                    def scale(n):
                        h = LEVELS[n] if n < NL else P
                        await_next(exp_ready)
                        if n >= 2:
                            pe_past(("lev", d, b, n - 2, 1))
                        le = [late_early(v, h, d) for v in (EL[n % 2], QL[n % 2], KL[n % 2], qx, kx)]
                        do(TT(le[1][0], le[3][0], le[0][0], ALU.mult))
                        do(TT(le[2][1], le[4][1], le[0][1], ALU.mult), qk_scaled)

                    def keep(n):
                        for t in ([0] if n == NL else XS):
                            ps = take(("lev", d, b, n, t))[:, :].rearrange("p (i c) -> p i c", i=4)
                            if n == NL:
                                do(dve.tensor_copy(rC[:, :, :], ps), F)
                            elif n < 0:
                                do(TT(rA[:, t, :, :], ps, ident.unsqueeze(1).broadcast_to((P, 4, P)), ALU.mult), F)
                            else:
                                at = (d * NL + n) * P
                                m = masks[:, at:at + P].unsqueeze(1).broadcast_to((P, 4, P))
                                do(dve.copy_predicated(rA[:, t, :, :], m, ps), F)

                    sub(0)
                    for n in range(NL + 1):
                        if n < NL:
                            sub(n + 1)
                        scale(n)
                        keep(n - 1)
                    signal(diff_ready)
                    await_next(exp_ready)
                    n = NL + 1
                    pe_past(("lev", d, b, n - 2, 1))
                    do(TT(QL[n % 2], qx, EL[n % 2], ALU.mult), qk_scaled)
                    keep(NL)
                    signal(o_ready)
                    for t in XS:
                        ps = take(("ro", d, b, t))
                        o = ro[:, t, b * 512:(b + 1) * 512]
                        if d == 0:
                            do(dve.tensor_copy(o, ps[:, :]), F)
                        else:
                            do(TT(o, o, ps[:, :], ALU.add), F)
            for t in XS:
                o = ro[:, t, :].rearrange("p (h c) -> p h c", h=HG)
                sq = xn[:, t, :].rearrange("p (h c) -> p h c", h=HG)
                st = stat[:, t * 8:t * 8 + 8]
                do(TT(sq, o, o, ALU.mult))
                do(dve.tensor_reduce(st, sq, AX, ALU.add), ss_ready)
                await_next(std_ready)
                do(dve.reciprocal(st, st))
                do(TT(o, o, st.unsqueeze(2).broadcast_to((P, HG, P)), ALU.mult))
                do(TT(o, o, ROW("og").unsqueeze(1).broadcast_to((P, HG, P)), ALU.mult))
                do(TT(ro[:, t, :], ro[:, t, :], rg[:, t, :], ALU.mult))
            signal(o_ready)
            residual("wo1", XS, GATE[(1, 0)])
            if stop == "h1":
                signal(stored)
                return
            ffn(1, XT)
            signal(x2_ready)
            pe_past(("down", 1, XT - 1, 1))
            for v, n in ((aK, 6), (bK, 2)):
                for z in range(2):
                    do(dve.memset(v[64 * z:64 * z + 64, 1 - z::2, :], 0.0),
                       zeros_ready if (n, z) == (2, 1) else dve_step)
            if stop == "l1":
                signal(stored)
                return
            attention(ATT2, lambda i: None)
            for b in range(2):
                for t in XS:
                    tmp = xn[:, 0, 0:512]
                    o, o2 = (v[:, t, b * 512:(b + 1) * 512] for v in (ga, gb2))
                    do(TT(o, o, take(("pa", b, t))[:, :], ALU.mult), F)
                    do(TT(tmp, o2, take(("pb", b, t))[:, :], ALU.mult), F)
                    do(TT(o, o, tmp, ALU.add))
            signal(merged_ready)
            for b in range(2):
                for t in XS:
                    ps = take(("wo2", b, t))
                    o = xr[:, t, b * 512:(b + 1) * 512]
                    do(STT(out=o, in0=o, scalar=ALPHA, in1=ps[:, :], op0=ALU.mult, op1=ALU.add), F)

            def layer_norm(src, g, after):
                for t in XS:
                    v, o, st = src[:, t, :], xr[:, t, :], stat[:, t:t + 1]
                    do(dve.tensor_reduce(st, v, AX, ALU.add))
                    do(dve.tensor_scalar(st, st, -1.0 / D, None, ALU.mult))
                    do(dve.tensor_scalar(o, v, st, None, ALU.add))
                    do(dve.tensor_tensor_reduce(out=xn[:, 0, :], in0=o, in1=o, scale=1.0, scalar=0.0, op0=ALU.mult,
                                                op1=ALU.add, accum_out=st), ss_ready)
                    await_next(std_ready)
                    do(dve.reciprocal(st, st))
                    do(STT(out=o, in0=o, scalar=st, in1=gb[:, g, :], op0=ALU.mult, op1=ALU.mult))
                    do(TT(o, o, gb[:, g + 1, :], ALU.add))
                signal(after)

            dve.wait_ge(ln_landed, 64)
            layer_norm(xr, 0, y_ready)
            if stop == "mix2":
                signal(stored)
                return
            do(dve.memset(lgx[:, :, :], -3e38))
            for t in XS:
                do(dve.tensor_scalar(acc[:, t, :], xr[:, t, :], ALPHA, None, ALU.mult))
            do(dve.memset(table[:, :, :], 0.0))
            ps = take(("route",))
            do(TT(lgx[:, :, 0:E], ps[:, 0:2 * E].rearrange("p (t e) -> p t e", t=2),
                  ROW("rb").unsqueeze(1).broadcast_to((P, 2, E)), ALU.add), F)
            for t in XS:
                do(dve.max(out=top[:, t, :], in_=lgx[:, t, :]))
            do(dve.tensor_scalar(tst[:, 0:2], top[:, :, 0], -1.0, None, ALU.mult), route_max)
            do(dve.memset(top[:, :, 4:8], -3e38))
            for t in XS:
                do(dve.match_replace(out=pick[:, t, :], in_to_replace=top[:, t, :], in_values=lgx[:, t, :],
                                     imm_value=3e38))
            do(dve.tensor_scalar(chosen[:, :, :], pick[:, :, 0:E], 3e38, None, ALU.is_equal), route_ready)
            await_next(gate_exp)
            do(TT(gate[:, :, :], gate[:, :, :], chosen[:, :, :], ALU.mult))
            do(dve.tensor_reduce(tst[:, 2:4], gate[:, :, :], AX, ALU.add))
            do(dve.reciprocal(tst[:, 2:4], tst[:, 2:4]))
            do(TT(gate[:, :, :], gate[:, :, :], tst[:, 2:4].unsqueeze(2).broadcast_to((P, 2, E)), ALU.mult))
            ps = take(("rank",))
            do(dve.tensor_copy(rank[:, :, :], ps[:, 0:3 * E].rearrange("p (t e) -> p t e", t=3)), F)
            for j, v in enumerate((rank, chosen, gate)):
                do(dve.tensor_copy(table[:, 0:E, 2 * j:2 * j + 2], v[:, 0:2, :].rearrange("p t e -> p e t")))
            LINKS = 7

            def chain(at):
                n = [0]

                def link(ins):
                    n[0] += 1
                    ins.then_inc(dve_link, 1)
                    dve.wait_ge(dve_link, at + n[0])

                return link, n

            def select(e, link, first=None):
                link(dve.tensor_copy(cur[:, 0:6], table[:, bass.ds(e, 1), :].rearrange("p e c -> p (e c)")))
                if first is None:
                    link(dve.tensor_copy(cur[:, 6:8], cur[:, 0:2]))
                else:
                    link(dve.tensor_scalar(cur[:, 6:8], cur[:, 0:2], first, None, ALU.subtract))
                for t in XS:
                    for dst, c in ((sel, 2 + t), (selg, 4 + t)):
                        ins = dve.tensor_scalar(dst[:, t, :], C("slot"), cur[:, 6 + t:7 + t], cur[:, c:c + 1],
                                                ALU.is_equal, ALU.mult)
                        if t == 0:
                            link(ins)
                        elif dst is sel:
                            link(ins)
                        else:
                            ins.then_inc(sel_ready, 1)

            def item(i, ahead, select_next):
                link, n = chain(LINK0 + i * LINKS + ahead * 2 * 5)
                dve.wait_ge(gg_ready, i + 1)
                dve.tensor_scalar(hm[:, :], PS[0][:, :], 7.0, None, ALU.min).then_inc(hm_ready, 1)
                dve.wait_ge(gu_ready, i + 1)
                link(dve.tensor_scalar(um[:, :], PS[1][:, :], 7.0, -7.0, ALU.min, ALU.max))
                dve.wait_ge(sg_ready, i + 1)
                link(TT(hm[:, :], hm[:, :], sg[:, :], ALU.mult))
                STT(out=hh[:, :], in0=um[:, :], scalar=1.0, in1=hm[:, :], op0=ALU.add, op1=ALU.mult)\
                    .then_inc(hh_ready, 1)
                for j in range(4):
                    h, t = j // 2, j % 2
                    dve.wait_ge(c_ready, 4 * i + j + 1)
                    o = acc[:, t, h * 512:(h + 1) * 512]
                    TT(o, o, PS[6 + t][:, :], ALU.add).then_inc(c_added, 1)
                dve.wait_ge(c_added, 4 * i + 5)
                dve.wait_ge(gx_ready, i + 2 + ahead)
                dve.wait_ge(gt_ready, i + 2 + ahead)
                select_next(link)
                assert n[0] == LINKS

            signal(c_added)
            for e in range(2):
                if e:
                    dve.wait_ge(gx_ready, 1)
                    dve.wait_ge(gt_ready, 1)
                link, n = chain(5 * e)
                select(e, link)
                assert n[0] == 5
            do(dve.tensor_scalar(extra[:, 0, :], rank[:, 2, :], float(SLOTS), None, ALU.is_gt))
            for k in range(2, PASSES):
                do(STT(out=extra[:, 0, :], in0=rank[:, 2, :], scalar=float(k * SLOTS), in1=extra[:, 0, :],
                       op0=ALU.is_gt, op1=ALU.add))
            do(dve.tensor_tensor_scan(extra[:, 1, :], C("ones", 0, E), extra[:, 0, :], 0.0, ALU.mult, ALU.add))
            bc = lambda v: v.unsqueeze(1).broadcast_to((P, ITEMS + 2, E))
            it = C("item")
            do(TT(wide, bc(extra[:, 1, :]), it.unsqueeze(2).broadcast_to((P, ITEMS + 2, E)), ALU.is_le))
            do(dve.tensor_reduce(far[:, 0, :], wide, AX, ALU.add))
            do(TT(wide, wide, bc(extra[:, 0, :]), ALU.mult))
            do(dve.tensor_reduce(far[:, 1, :], wide, AX, ALU.add))
            do(TT(far[:, 1, :], it, far[:, 1, :], ALU.subtract))
            do(dve.tensor_scalar(far[:, 1, :], far[:, 1, :], 1.0, float(SLOTS), ALU.add, ALU.mult))
            do(dve.tensor_scalar(fari, far[:, 0, :], float(E - 1), None, ALU.min))
            do(dve.tensor_copy(nfar, extra[:, 1, E - 1:E]), rank_ready)

            LINK0 = 10
            with dve.Fori(0, E) as i:
                item(i, 0, lambda link: select(i + 2, link))

            def far_select(j, link):
                select(far_item(dve, j), link, far[:, 1, bass.ds(j, 1)])

            def first_further():
                dve.wait_ge(sel_ready, E + 2)
                for j in range(2):
                    dve.wait_ge(gx_ready, E + 1 + j)
                    dve.wait_ge(gt_ready, E + 1 + j)
                    far_select(j, chain(LINK0 + E * LINKS + 5 * j)[0])

            further(dve, lambda j: item(j + E, 1, lambda link: far_select(j + 2, link)), first_further)
            layer_norm(acc, 2, out_ready)




def _rows(inputs):
    f = {k: np.asarray(v) for k, v in inputs.items()}

    def col(v):
        v = v.reshape(-1, P)
        return v.T

    cc = np.stack([f["c"][0].reshape(KC, P), f["c_ctx"].reshape(KC, P)], 1)
    cols = np.concatenate([col(f["norm1_g"]), col(f["norm2_g"]), col(f["ada_b"]), col(f["ffn_conv_w"]),
                           col(f["ffn_conv_b"]), col(f["hgrn_lb_logits"]), col(cc)], 1)
    rows = np.concatenate([f["attn_q_gain"][0], f["attn_k_gain"][0], f["attn_sink"][0], f["hgrn_o_gain"][0],
                           f["sinks_2"][0], f["router_b_2"][0]])
    const, masks = constants()
    big = {k: f[k] for k in BIG}
    return {"cols": np.ascontiguousarray(cols), "rows": np.ascontiguousarray(rows), "const": const, "masks": masks, **big}


BIG = ["x", "ctx", "ada_w", "ada_b", "attn_w_in", "attn_w_out", "hgrn_w_in", "hgrn_w_out", "ffn_w_up", "ffn_w_down",
       "w_in_2", "w_proj_a_2", "w_proj_b_2", "w_out_2", "ln1_g_2", "ln1_b_2", "router_w_2", "w_gate_2", "b_gate_2",
       "w_up_2", "b_up_2", "w_down_2", "b_down_2", "ln2_g_2", "ln2_b_2"]


def kernel(**inputs):
    import concourse.bacc as bacc
    from concourse.bass_utils import run_bass_kernel_spmd as run

    nc = bacc.Bacc("TRN2", target_bir_lowering=False, num_devices=1)
    arrays, args = {}, {}
    for name, v in _rows(inputs).items():
        v = np.ascontiguousarray(v)
        arrays["in_" + name] = v
        args[name] = nc.dram_tensor("in_" + name, v.shape, mybir.dt.from_np(v.dtype), kind="ExternalInput").ap()
    out = nc.dram_tensor("out", (1, SEQ, D), F32, kind="ExternalOutput").ap()
    program(nc, args, out)
    r = run(nc, [arrays], core_ids=[0])
    return r.results[0]["out"]
```

```python
from contextlib import ExitStack

import numpy as np
import concourse.bass as bass
from concourse import mybir

ALU = mybir.AluOpType
ACT = mybir.ActivationFunctionType
AX = mybir.AxisListType.X
F32 = mybir.dt.float32
F32R = mybir.dt.float32r
I32 = mybir.dt.int32
U8 = mybir.dt.uint8

P = 128
D = 1024
KC = D // P
SEQ, CTX = 256, 256
TOK = SEQ + CTX
NT, XT = TOK // P, SEQ // P
HD = 64
FF = 2816
FC = FF // P
NH, NKV = 16, 4
HG = 8
LEVELS = [64, 32, 16, 8, 4, 2, 1]
E = 32
SLOTS = 64
UNIT = 4096
RING = 3
PASSES = -(-SEQ // SLOTS)
ITEMS = E * (PASSES - 1)
ALPHA = 2.0 ** 0.25
BANKS = 8

CONST = {}


def _lay():
    at = 0
    for name, n in (("ident", 128), ("cos", 64), ("sin", 64), ("mask0", 1024), ("diff", 1024), ("sel2", 2),
                    ("selb", 256), ("before", 128), ("slot", 128), ("ones", 128), ("eps6", 1), ("eps5", 1),
                    ("item", ITEMS + 2)):
        CONST[name] = (at, n)
        at += n
    return at


NCONST = _lay()

COLS = {"n1": (0, 16), "n2": (16, 16), "adab": (32, 96), "cw": (128, 132), "cb": (260, 44), "lb": (304, 16),
        "c": (320, 16)}
NCOLS = 336
ROWS = {"qg": (0, 64), "kg": (64, 64), "sink": (128, 16), "og": (144, 128), "sink2": (272, 16), "rb": (288, 32)}
NROWS = 320


def slopes():
    h = np.arange(1, 29, dtype=np.float32)
    return [float(v) for v in np.exp2(np.float32(-8.0) * h / np.float32(28))]


def constants():
    c = np.zeros((P, NCONST), np.float32)

    def put(name, v):
        at, n = CONST[name]
        c[:, at:at + n] = np.asarray(v, np.float32).reshape(-1, n) if np.ndim(v) else v

    p = np.arange(P)
    put("ident", np.eye(P))
    inv = (np.float32(10000.0) ** (-np.arange(16, dtype=np.float32) / np.float32(16))).astype(np.float32)
    t = np.arange(SEQ)
    ang = np.stack([(t // 64).astype(np.float32)[:, None] * inv, (t % 64).astype(np.float32)[:, None] * inv], 1)
    for name, f in (("cos", np.cos), ("sin", np.sin)):
        put(name, f(ang.astype(np.float32)).reshape(2, P, 32).transpose(1, 0, 2).reshape(P, 64))
    m = np.zeros((P, 2, 512), np.float32)
    for i in range(2):
        m[:, i, :SEQ] = np.where(np.abs((i * P + p)[:, None] - np.arange(SEQ)) <= 128, 0.0, -1e30)
    put("mask0", m.reshape(P, 1024))
    diff = P + p[:, None] - np.arange(SEQ)
    far = np.float32(1e33)
    d = np.stack([np.where((diff >= 0) & (diff <= lim) & (diff % dil == 0), diff, far)
                  for lim, dil in ((127, 1), (128, 1), (512, 4), (2048, 16))], 1)
    put("diff", d.reshape(P, 1024))
    q, v = p % 32, np.arange(2)
    put("sel2", (q[:, None] == v).astype(np.float32))
    put("selb", np.repeat((q[:, None] == v).astype(np.float32), P, axis=1))
    put("before", (p[:, None] < p).astype(np.float32))
    put("slot", np.tile(np.arange(SLOTS, dtype=np.float32), (P, 2)))
    put("ones", np.ones((P, P)))
    put("eps6", 1e-6)
    put("eps5", 1e-5)
    put("item", np.tile(np.arange(ITEMS + 2, dtype=np.float32), (P, 1)))
    masks = np.zeros((P, 2, len(LEVELS), P), np.float32)
    s, tt = p[:, None], p[None, :]
    for n, h in enumerate(LEVELS):
        fw = (s // (2 * h) == tt // (2 * h)) & (s % (2 * h) < h) & (tt % (2 * h) >= h)
        masks[:, 0, n], masks[:, 1, n] = fw, fw.T
    return c, masks.reshape(P, -1)


def program(nc, a, out):
    with ExitStack() as ctx:
        def sb(name, shape, dt=F32):
            return ctx.enter_context(nc.sbuf_tensor(name, shape, dt))

        def sem(name):
            return ctx.enter_context(nc.semaphore(name))

        PS = [ctx.enter_context(nc.psum_tensor(f"bank{i}", [P, 512], F32)) for i in range(BANKS)]
        ring_at = -(-nc.sbuf_base // 32) * 32
        ring = sb("ring", [P, RING, UNIT])
        arena_at = -(-nc.sbuf_base // 32) * 32
        arena = sb("arena", [P, 80 * 256])
        xr = sb("xr", [P, NT, D])
        hT_at = -(-nc.sbuf_base // 32) * 32
        hT = sb("hT", [P, KC, TOK])
        gb = sb("gb", [P, 4, D])
        modp = sb("modp", [P, 2, 512])
        xn_at = -(-nc.sbuf_base // 32) * 32
        xn = sb("xn", [P, 2, D])
        const = sb("const", [P, NCONST])
        mask_in = xn[:, :, :].rearrange("p a b -> p (a b)")[:, 0:2 * len(LEVELS) * P]
        masks = sb("masks", [P, 2 * len(LEVELS) * P], U8)
        cols = sb("cols", [P, NCOLS])
        rows = sb("rows", [P, NROWS])
        cT = sb("cT", [P, KC, 32])
        modT = sb("modT", [P, 2, 48, 2])
        coef = sb("coef", [P, 2, 2, KC, 2])
        stat = sb("stat", [P, 256])

        def C(name, lo=0, n=None):
            at, w = CONST[name]
            return const[:, at + lo:at + lo + (w if n is None else n)]

        def COL(name, lo=0, n=None):
            at, w = COLS[name]
            return cols[:, at + lo:at + lo + (w if n is None else n)]

        def ROW(name, lo=0, n=None):
            at, w = ROWS[name]
            return rows[:, at + lo:at + lo + (w if n is None else n)]

        ident = C("ident")

        def region(at, *shape):
            n = int(np.prod(shape))
            assert at + n <= 80 * 256, (at, n)
            v = arena[:, at:at + n]
            if len(shape) == 1:
                return v
            names = "abcd"[:len(shape)]
            return v.rearrange(f"p ({' '.join(names)}) -> p {' '.join(names)}",
                               **{k: s for k, s in zip(names, shape)})

        qkv = region(0, NT, 1536)
        qT = region(6144, 8, TOK)
        kT = region(10240, 8, TOK)
        SB = region(14336, 2, 2048)
        PT = region(18432, 2, 512)
        hid = region(0, FC, TOK)
        ft = xn[:, :, :].rearrange("p a (b n) -> p (a b) n", n=512)
        def high_low(name, shape, at):
            return nc.alloc_sbuf_tensor_at(name, shape, F32R, offset=at)

        hT_high = high_low("hT_high", [P, KC, TOK], hT_at)
        hT_low = high_low("hT_low", [P, KC, TOK], arena_at + 4 * FC * TOK)
        w_split = [high_low("w_split0", [P, 2, KC, 2, P], arena_at + 4 * (FC * TOK + KC * TOK)),
                   high_low("w_split1", [P, 2, KC, 2, P], ring_at + 4 * UNIT * (RING - 1))]
        hid_high = high_low("hid_high", [P, 2, 4, TOK], hT_at)
        hid_low = high_low("hid_low", [P, FC, TOK], arena_at)
        down_high = [high_low(f"down_high{i}", [P, 4, D], arena_at + 4 * (FC * TOK + i * KC * TOK)) for i in range(2)]
        down_low = high_low("down_low", [P, RING, 4, D], ring_at)
        hx_high = high_low("hx_high", [P, KC, TOK], arena_at + 4 * 10240)
        hx_low = high_low("hx_low", [P, KC, TOK], arena_at + 4 * (10240 + KC * TOK))
        hw_high = [high_low("hw_high0", [P, KC, 256], arena_at + 4 * (10240 + 2 * KC * TOK)),
                   high_low("hw_high1", [P, KC, 256], xn_at)]
        hw_low = high_low("hw_low", [P, RING, KC, 512], ring_at)
        HALVES = [(key, z) for key in (("hq", 1), ("hv", 0), ("hv", 1), ("hg", 0), ("hg", 1), ("hf", 0, 0))
                  for z in range(2)]
        qx_high = high_low("qx_high", [P, KC, TOK], arena_at + 4 * 6144)
        qx_low = high_low("qx_low", [P, KC, TOK], arena_at + 4 * (6144 + KC * TOK))
        qw_high = [high_low(f"qw_high{j}", [P, KC, 256], arena_at + 4 * (6144 + 2 * KC * TOK + 2048 * j))
                   for j in range(3)] + [hw_high[1]]
        Q_HALVES = [(("qkv", b), z) for b in (1, 2) for z in range(2)]
        x2_high = hT_high[:, :, SEQ:TOK]
        x2_low = high_low("x2_low", [P, KC, SEQ], xn_at)
        w2_high = [high_low(f"w2_high{j}", [P, KC, 256], arena_at + 4 * (14336 + 2048 * j)) for j in range(3)]
        W_HALVES = [(u, z) for u in range(1, 11) for z in range(2) if (u, z) != (6, 1)]
        rq = region(0, HG, SEQ)
        rv = region(2048, NT, D)
        rg = region(6144, XT, D)
        rk = region(8192, 4, TOK)
        rb = region(10240, 4, TOK)
        rE = region(12288, 4, SEQ)
        rQ = region(13312, 4, SEQ)
        rK = region(14336, 4, SEQ)
        rA = region(15360, 2, 4, P)
        rC = region(16384, 4, P)
        rS = region(16896, 4, P)
        rD = region(17408, 2, 2, P)
        ro = region(17920, XT, D)
        aT = region(0, 6, SEQ)
        aK = region(1536, 12, SEQ)
        bT = region(4608, 8, SEQ)
        bK = region(6656, 4, SEQ)
        av = region(7680, XT, 768)
        bv = region(9216, XT, P)
        ga = region(9472, XT, D)
        gb2 = region(11520, XT, D)
        oA = region(13568, XT, 256)
        oB = xn
        moe_slot = [ring[:, i, :] for i in range(RING)] + [region(i * UNIT, UNIT) for i in range(6 - RING)]
        M0 = (6 - RING) * UNIT
        xg = region(M0, KC, SLOTS)
        hm = region(M0 + 512, 512)
        um = region(M0 + 1024, 512)
        sg = region(M0 + 1536, 512)
        hh = region(M0 + 2048, 512)
        hhT = region(M0 + 2560, 4, P)
        yg = region(M0 + 3072, 512)
        bias = region(M0 + 3584, D)
        rw = region(M0 + 4608, KC, E)
        sel = region(M0 + 4864, 2, P)
        selg = region(M0 + 5120, 2, P)
        selgT = region(M0 + 5376, 2, P)
        table = region(M0 + 5632, E + 2, 6)
        cur = region(M0 + 5900, 8)
        lgx = region(M0 + 5908, 2, 40)
        top = region(M0 + 5988, 2, 8)
        pick = region(M0 + 6004, 2, 40)
        gate = region(M0 + 6084, 2, E)
        chosen = region(M0 + 6148, 2, E)
        rank = region(M0 + 6212, 3, E)
        extra = region(M0 + 6308, 2, E)
        far = region(M0 + 6372, 2, ITEMS + 2)
        fari = region(M0 + 6572, ITEMS + 2).bitcast(I32)
        nfar = region(M0 + 6670, 1).bitcast(I32)
        tst = region(M0 + 6672, 16)
        wide = hT[:, :, :].rearrange("p k t -> p (k t)")[:, 0:(ITEMS + 2) * E].rearrange("p (j e) -> p j e", e=E)
        acc = xr[:, XT:NT, :]

        NL = len(LEVELS)

        group, reader, nth = {}, [], []
        seen = {"act": 0, "dve": 0}

        def add(key, who):
            assert key not in group, key
            group[key] = len(reader)
            reader.append(who)
            seen[who] += 1
            nth.append(seen[who])

        units, unit_no = [], {}

        def stream(key, *pieces):
            unit_no[key] = len(units)
            units.append(pieces)

        def colblock(w, lo, n):
            return w.rearrange("(k p) n -> p k n", p=P)[:, :, lo:lo + n]

        def ring_col(s, lo, n):
            return ring[:, s, :].rearrange("p (k n) -> p k n", k=KC)[:, :, lo:lo + n]

        def ring_row(s, n):
            return ring[:, s, 0:n * D].rearrange("p (k n) -> p k n", k=n)

        def col_unit(key, w, lo, n=512):
            stream(key, (lambda s: ring_col(s, 0, n), colblock(w, lo, n)))

        def row_units(key, w, chunks):
            for j, k0 in enumerate(range(0, chunks, 4)):
                n = min(4, chunks - k0)
                stream((*key, j), (lambda s, n=n: ring_row(s, n),
                                   w[k0 * P:(k0 + n) * P, :].rearrange("(k p) n -> p k n", p=P)))

        G_BLOCKS = {4: (0, 0), 5: (0, 1), 10: (1, 0), 11: (1, 1)}

        def gate_slots(l, blk):
            if blk not in G_BLOCKS:
                return []
            g = G_BLOCKS[blk][0]
            return [(2 * g, 0), (2 * g + 1, 1)] if l == 0 else [(g, 0)]

        GATE = {(0, 0): (0, 1), (0, 1): (2, 3), (1, 0): (0,), (1, 1): (1,)}

        ada_turn = {}

        def plan_ada(l, blk):
            ada_turn[l, blk] = len(ada_turn) % 2
            col_unit(("ada", l, blk), a["ada_w"][l], blk * 512)
            add(("adap", l, blk), "act")
            add(("adat", l, blk), "dve")
            for row, v in gate_slots(l, blk):
                add(("adag", l, blk, row), "dve")

        def plan_turn(tag, tiles):
            for t in tiles:
                for h in range(2):
                    add(("turn", tag, t, h), "act")

        ALL, XS = range(NT), range(XT)
        for blk in range(4):
            plan_ada(0, blk)
        plan_turn("a0", ALL)
        for b in range(3):
            col_unit(("qkv", b), a["attn_w_in"][0], b * 512)
            for t in ALL:
                add(("qkv", b, t), "act")
        for t in ALL:
            for j in range(3):
                add(("qkt", t, j), "act")

        def att_units0():
            for t in ALL:
                for g in range(NKV):
                    w = TOK if t < XT else CTX
                    lo = 0 if t < XT else SEQ

                    def qa(r, t=t, g=g):
                        return qT[:, 2 * g + r // 2, t * P:(t + 1) * P]

                    def ka(r, g=g, lo=lo, w=w):
                        return kT[:, 2 * g + r % 2, lo:lo + w]

                    def va(r, c, g=g, t=t):
                        return qkv[:, c if t < XT else c + XT, 1280 + g * HD:1280 + (g + 1) * HD]

                    yield dict(tag=("x0", t, g), n=w, q=qa, k=ka, v=va, heads=4,
                               mask=C("mask0", t * 512, 512) if t < XT else None, slope=None,
                               sink=ROW("sink", 4 * g, 4), out=qkv[:, t, g * 256:(g + 1) * 256])

        def att_units2():
            sl = slopes()
            for t in XS:
                n = (t + 1) * P
                for g in range(4):
                    def qa(r, t=t, g=g):
                        return bT[:, 2 * g + r // 2, t * P:(t + 1) * P]

                    def ka(r, g=g, n=n):
                        return bK[:, 2 * (g // 2) + r % 2, 0:n]

                    def va(r, c, g=g):
                        return bv[:, c, (g // 2) * HD:(g // 2 + 1) * HD]

                    yield dict(tag=("b2", t, g), n=n, q=qa, k=ka, v=va, heads=4, mask=None,
                               slope=[(sl[4 * g + r], C("diff", SEQ - n, n)) for r in range(4)],
                               sink=ROW("sink2", 4 * g, 4), out=oB[:, t, g * 256:(g + 1) * 256])
            for t in XS:
                n = (t + 1) * P
                for h in range(4):
                    def qa(r, t=t, h=h):
                        return aT[:, 2 * r + h // 2, t * P:(t + 1) * P]

                    def ka(r, h=h, n=n):
                        return aK[:, 4 * r + h, 0:n]

                    def va(r, c, h=h):
                        return av[:, c, (r * 4 + h) * HD:(r * 4 + h + 1) * HD]

                    yield dict(tag=("a2", t, h), n=n, q=qa, k=ka, v=va, heads=1, mask=None,
                               slope=[(sl[16 + 4 * r + h], C("diff", (r + 1) * SEQ + SEQ - n, n)) for r in range(3)],
                               sink=None, out=oA[:, t, h * HD:(h + 1) * HD])

        rk2 = gb[:, 2:4, :].rearrange("p a b -> p (a b)").rearrange("p (i t) -> p i t", i=4)
        rks = (rk, rk2)
        rb2 = ring[:, RING - 1, 0:4 * TOK].rearrange("p (i t) -> p i t", i=4)
        rbs = (rb, rb2)
        rlog = ring[:, RING - 1, 4 * TOK:8 * TOK].rearrange("p (i t) -> p i t", i=4)
        kdec = rlog[:, :, 0:SEQ]
        EL = [rE, xn[:, 0, :].rearrange("p (h t) -> p h t", h=4)]
        QL = [rQ, xn[:, 1, :].rearrange("p (h t) -> p h t", h=4)]
        KL = [rK, modp[:, :, :].rearrange("p a b -> p (a b)").rearrange("p (h t) -> p h t", h=4)]

        def late_early(v, h, d):
            v = v.rearrange("p i (n z c) -> p i n z c", z=2, c=h)
            return v[:, :, :, 1 - d, :], v[:, :, :, d, :]

        def nrows(u):
            return 4 if u["heads"] == 4 else 3

        def plan_att(us, between):
            for i in range(len(us) + 1):
                if i < len(us):
                    for r in range(nrows(us[i])):
                        add(("score", us[i]["tag"], r), "dve")
                if i:
                    for r in range(nrows(us[i - 1])):
                        add(("probt", us[i - 1]["tag"], r), "act")
                    add(("pv", us[i - 1]["tag"]), "dve")
                    between(i - 1)

        ATT0, ATT2 = list(att_units0()), list(att_units2())
        ADA_BETWEEN = [(0, 4 + i // 2) if i % 2 == 0 else (1, (0, 1, 2, 3, 6, 7, 8, 9)[i // 2]) for i in range(16)]
        ADA_LATE = [4, 5, 10, 11]
        plan_att(ATT0, lambda i: plan_ada(*ADA_BETWEEN[i]))
        plan_turn("o0", ALL)
        for b in range(2):
            col_unit(("wo0", b), a["attn_w_out"][0], b * 512)
            for t in ALL:
                add(("wo0", b, t), "dve")

        def plan_ffn(l, T):
            plan_turn(("f", l), range(T))
            w = a["ffn_w_up"][l]
            for j in range(FC // 2):
                stream(("up", l, j), (lambda s: ring_col(s, 0, 256), colblock(w, j * 256, 256)),
                       (lambda s: ring_col(s, 256, 256), colblock(w, FF + j * 256, 256)))
                for i in range(2):
                    add(("gate", l, 2 * j + i), "act")
                    add(("val", l, 2 * j + i), "dve")
                if l == 0 and j < 4:
                    plan_ada(1, ADA_LATE[j])
            row_units(("down", l), a["ffn_w_down"][l], FC)
            for t in range(T):
                for h in range(2):
                    add(("down", l, t, h), "dve")

        plan_ffn(0, NT)
        plan_turn("h1", ALL)
        w = a["hgrn_w_in"][0]
        for b in range(2):
            col_unit(("hq", b), w, b * 512)
            for i in range(4):
                add(("hq", 4 * b + i), "act")
        for b in range(2):
            col_unit(("hv", b), w, 3072 + b * 512)
            for t in ALL:
                add(("hv", b, t), "act")
        for b in range(2):
            col_unit(("hg", b), w, 4096 + b * 512)
            for t in XS:
                add(("hg", b, t), "act")
        def after(d, b):
            return (d, 1) if b == 0 else (1, 0) if d == 0 else None

        def plan_hf(d, b, i):
            if i == 0:
                col_unit(("hf", d, b), w, 1024 + d * 1024 + b * 512)
            add(("hf", d, b, i), "act")

        for i in range(4):
            plan_hf(0, 0, i)
        for d in range(2):
            for b in range(2):
                for n in range(-1, NL + 1):
                    if n == NL:
                        add(("lev", d, b, n, 0), "dve")
                    else:
                        for t in XS:
                            add(("lev", d, b, n, t), "dve")
                    if 1 <= n <= 4:
                        add(("st", d, b, n - 1), "act")
                    if 0 <= n < 4:
                        add(("kt", d, b, n), "act")
                        if after(d, b):
                            plan_hf(*after(d, b), n)
                for t in XS:
                    add(("ro", d, b, t), "dve")
        plan_turn("o1", XS)
        for b in range(2):
            col_unit(("wo1", b), a["hgrn_w_out"][0], b * 512)
            for t in XS:
                add(("wo1", b, t), "dve")
        plan_ffn(1, XT)
        plan_turn("x2", XS)
        w = a["w_in_2"][0]
        W2 = []
        for c in range(12):
            W2.append((c * 128 // 512, "T", c * 128 % 512, ("aT", c)))
        W2 += [(3, "N", (0, 512), ("av", 0)), (4, "N", (0, 256), ("av", 512))]
        for c in range(8):
            at = 2304 + c * 128
            W2.append((at // 512, "T", at % 512, ("bT", c)))
        for g in range(2):
            W2.append((6, "K", 256 + 64 * g, ("bT", 8 + g)))
        W2.append((6, "N", (384, 128), ("bv", 0)))
        for j in range(4):
            W2.append((7 + j, "N", (0, 512), ("g", j)))
        for b in range(11):
            col_unit(("w2", b), w, b * 512)
        for u, kind, c, dst in W2:
            if kind == "N":
                for t in XS:
                    add(("w2", dst, t), "act")
            else:
                add(("w2", dst), "act")
        plan_att(ATT2, lambda i: None)
        for t in XS:
            add(("turn", "oa2", t, 0), "act")
        plan_turn("ob2", XS)
        row_units(("pa",), a["w_proj_a_2"][0], 2)
        for b in range(2):
            col_unit(("pb", b), a["w_proj_b_2"][0], b * 512)
        for b in range(2):
            for t in XS:
                add(("pa", b, t), "dve")
                add(("pb", b, t), "dve")
        plan_turn("m2", XS)
        for b in range(2):
            col_unit(("wo2", b), a["w_out_2"][0], b * 512)
            for t in XS:
                add(("wo2", b, t), "dve")
        plan_turn("y2", XS)
        add(("route",), "dve")
        add(("rank",), "dve")

        unit_end = {}
        for key in unit_no:
            if key[0] == "ada":
                unit_end[key] = ("adap", *key[1:])
            elif key[0] == "up":
                unit_end[key] = ("val", key[1], 2 * key[2] + 1)
            elif key[0] == "down":
                last = key[2] == (FC + 3) // 4 - 1
                unit_end[key] = ("down", key[1], NT - 1 if key[1] == 0 else XT - 1, 1) if last else None
            elif key[0] in ("qkv", "wo0", "hv"):
                unit_end[key] = (*key, NT - 1)
            elif key[0] == "hq":
                unit_end[key] = ("hq", 4 * key[1] + 3)
            elif key[0] == "hf":
                unit_end[key] = (*key, 3)
            elif key[0] == "pa":
                unit_end[key] = ("pa", 1, XT - 1)
            elif key[0] == "w2":
                dst, kind = [(d, k) for u, k, _, d in W2 if u == key[1]][-1]
                unit_end[key] = ("w2", dst, XT - 1) if kind == "N" else ("w2", dst)
            else:
                unit_end[key] = (*key, XT - 1)
        mid_units = 0
        splits = 0
        unit_done = []
        for key, n in unit_no.items():
            if key[0] == "up":
                splits += 2
                unit_done.append(("w_low", splits))
            elif unit_end[key] is None:
                mid_units += 1
                unit_done.append(("units_used", mid_units))
            else:
                unit_done.append(("psum_ready", group[unit_end[key]] + 1))

        slot_of, before_load, landed = [], [], []
        cnt, owner, order = [0] * RING, [None] * RING, list(range(RING))
        names = list(unit_no)
        for n, (key, pieces) in enumerate(zip(names, units)):
            narrow = key[0] in ("up", "hf") or key == ("wo1", 0) or (key[0] == "ada" and names[n - 1][0] == "up")
            s = [x for x in order if x < RING - 1 or not narrow][0]
            order.remove(s)
            order.append(s)
            slot_of.append(s)
            before_load.append(owner[s])
            owner[s] = unit_done[n]
            if key[0] == "up":
                owner[RING - 1] = ("psum_ready", group[unit_end[key]] + 1)
            if key[0] == "hf":
                owner[RING - 1] = ("psum_ready", group[("ro", 1, 1, 1)] + 1)
            cnt[s] += 16 * len(pieces)
            landed.append((s, cnt[s]))
        unit_landed = [sem(f"unit_landed{i}") for i in range(RING)]
        units_used = sem("units_used")
        psum_ready = sem("psum_ready")
        w_high, w_low, w_low_v = sem("weights_high"), sem("weights_low_gate"), sem("weights_low_value")
        down_w_high, down_hid_high, down_low_ready = sem("down_w_high"), sem("down_hid_high"), sem("down_low")
        qx_high_ready, qx_low_ready, qw_high_ready, qw_low_ready = (
            sem("qx_high"), sem("qx_low"), sem("qw_high"), sem("qw_low"))
        x2_high_ready, x2_low_ready, w2_high_ready, w2_low_ready, half2_used = (
            sem("x2_high"), sem("x2_low"), sem("w2_high"), sem("w2_low"), sem("half2_used"))
        hx_high_ready, hx_low_ready, hw_high_ready, hw_low_ready, half_used = (
            sem("hx_high"), sem("hx_low"), sem("hw_high"), sem("hw_low"), sem("half_used"))
        x_high, x_low = sem("input_high"), sem("input_low")
        SEM = {"psum_ready": psum_ready, "units_used": units_used, "w_low": w_low_v}
        freed = {"act": sem("freed_by_act"), "dve": sem("freed_by_dve")}
        cols_landed, params_landed, x_landed = sem("cols_landed"), sem("params_landed"), sem("x_landed")
        rows_landed = sem("gate_bias_landed")
        zeros_ready, silu_c = sem("zeros_ready"), sem("silu_c_ready")
        modp_ready = sem("modp_ready")
        coef_ready = sem("coef_ready")
        ss_ready, std_ready, xn_ready = sem("square_sum_ready"), sem("std_ready"), sem("normed_ready")
        hT_ready = sem("hT_ready")
        qkv_ready, qk_ready, qT_ready = sem("qkv_ready"), sem("qk_normed"), sem("qT_ready")
        max_ready, p_ready, sum_ready, pt_ready = sem("max_ready"), sem("p_ready"), sem("sum_ready"), sem("pt_ready")
        o_ready = sem("o_ready")
        state_k, kdec_ready, diff_ready, exp_ready, qk_scaled = (
            sem("gate_logs"), sem("kdec_ready"), sem("diff_ready"), sem("exp_ready"), sem("qk_scaled"))
        sums_ready, kexp_ready = sem("running_sums_ready"), sem("keys_decay_ready")
        sig_ready, forget_ready, kd_turned, lb_ready, exp_lb = (
            sem("sigmoid_ready"), sem("forget_ready"), sem("kdec_turned"), sem("lb_ready"), sem("lb_exp"))
        x2_ready, merged_ready, y_ready, route_ready, rank_ready = (
            sem("x2_ready"), sem("merged_ready"), sem("y_ready"), sem("chosen_ready"), sem("table_ready"))
        out_ready, route_max, gate_exp = sem("out_ready"), sem("route_max_ready"), sem("gate_exp_ready")
        ln_landed, rw_landed = sem("ln_landed"), sem("router_landed")
        gate_landed, up_landed, down_landed = sem("moe_gate_landed"), sem("moe_up_landed"), sem("moe_down_landed")
        sel_ready, gx_ready, xg_ready, gt_ready, selgT_ready = (
            sem("sel_ready"), sem("gather_closed"), sem("xg_ready"), sem("selt_closed"), sem("selgT_ready"))
        gg_ready, gu_ready, hm_ready, sg_ready, hh_ready = (
            sem("gate_closed"), sem("up_closed"), sem("hm_ready"), sem("sg_ready"), sem("hidden_ready"))
        ht_ready, hhT_ready, gd_ready, yg_ready, c_ready, c_added = (
            sem("hiddent_closed"), sem("hhT_ready"), sem("down_closed"), sem("yg_ready"), sem("combine_closed"),
            sem("combine_added"))
        gates_read = sem("gates_read")
        conv1, conv2, silu_ready, hid_ready = sem("gate_scaled"), sem("conv_done"), sem("silu_ready"), sem("hid_ready")
        act_step, dve_step, dve_link = sem("act_step"), sem("dve_step"), sem("dve_link")
        stored = sem("stored")

        def helpers(eng, own, name):
            count, got, last = {}, {}, [-1]

            def do(ins, s=own, n=1):
                count[s.name] = count.get(s.name, 0) + n
                ins.then_inc(s, n)
                eng.wait_ge(s, count[s.name])

            def signal(s):
                count[s.name] = count.get(s.name, 0) + 1
                eng.sem_inc(s, 1)

            def await_next(s, n=1):
                got[s.name] = got.get(s.name, 0) + n
                eng.wait_ge(s, got[s.name])

            def take(key):
                g = group[key]
                assert reader[g] == name and g > last[0], key
                last[0] = g
                eng.wait_ge(psum_ready, g + 1)
                return PS[g % BANKS]

            def pe_past(key):
                eng.wait_ge(psum_ready, group[key] + 1)

            return do, signal, await_next, take, pe_past

        block = ctx.enter_context(nc.Block())

        def expert_units(sp, e, i, first=False):
            def rows_of(w, e, j):
                return w[0][bass.ds(e, 1)].rearrange("e (k p) n -> p (e k) n", p=P)[:, 4 * j:4 * j + 4, :]

            def cols_of(w, e, j):
                return w[0][bass.ds(e, 1)].rearrange("e (k p) n -> p (e k) n", p=P)[:, :, 512 * j:512 * j + 512]

            def slot_free(n):
                if first and n < RING:
                    sp.wait_ge(SEM[owner[n][0]], owner[n][1])
                if first and n == RING:
                    sp.wait_ge(psum_ready, group[("turn", "m2", 1, 1)] + 1)

            b_src = lambda name: a[name][0][bass.ds(e, 1)]
            if not first:
                sp.wait_ge(gg_ready, i)
            for j in range(2):
                slot_free(j)
                sp.dma_start(moe_slot[j].rearrange("p (k n) -> p k n", k=KC), cols_of(a["w_gate_2"], e, j))\
                    .then_inc(gate_landed, 16)
            if not first:
                sp.dma_start(bias[0:1, :], b_src("b_gate_2")).then_inc(gate_landed, 16)
                sp.wait_ge(gu_ready, i)
            for j in range(2):
                slot_free(2 + j)
                if first and j == 1:
                    sp.dma_start(bias[0:1, :], b_src("b_gate_2")).then_inc(gate_landed, 16)
                sp.dma_start(moe_slot[2 + j].rearrange("p (k n) -> p k n", k=KC), cols_of(a["w_up_2"], e, j))\
                    .then_inc(up_landed, 16)
            sp.dma_start(bias[32:33, :], b_src("b_up_2")).then_inc(up_landed, 16)
            if not first:
                sp.wait_ge(gd_ready, i)
            for j in range(2):
                sp.dma_start(moe_slot[4 + j].rearrange("p (k n) -> p k n", k=4), rows_of(a["w_down_2"], e, j))\
                    .then_inc(down_landed, 16)
            sp.dma_start(bias[64:65, :], b_src("b_down_2")).then_inc(down_landed, 16)

        def far_item(eng, j):
            return eng.value_load(fari[0:1, bass.ds(j, 1)], min_val=0, max_val=E - 1)

        def further(eng, body, before=None):
            n = eng.value_load(nfar[0:1, 0:1], min_val=0, max_val=ITEMS)
            with eng.If(n > 0):
                if before is not None:
                    before()
                with eng.Fori(0, n) as j:
                    body(j)

        def moe_sync(sp):
            sp.wait_ge(psum_ready, group[("turn", "ob2", 1, 1)] + 1)
            sp.dma_start(rw[:, :, :], a["router_w_2"][0].rearrange("(k p) n -> p k n", p=P)).then_inc(rw_landed, 16)
            expert_units(sp, 0, 0, first=True)
            with sp.Fori(1, E) as e:
                expert_units(sp, e, e)
            sp.wait_ge(rank_ready, 1)
            further(sp, lambda j: expert_units(sp, far_item(sp, j), j + E))
            sp.wait_ge(out_ready, 1)
            sp.dma_start(out[0].rearrange("(t p) d -> p t d", p=P), xr[:, 0:XT, :]).then_inc(stored, 16)
            sp.wait_ge(stored, 16)

        def low_part(eng, l, fc, g, then):
            s = slot_of[unit_no[("up", l, fc // 2)]]
            raw = ring[:, s, :].rearrange("p (k g i c) -> p k g i c", k=KC, g=2, i=2)[:, :, g, fc % 2, :]
            w = w_split[fc % 2]
            then(eng.tensor_tensor(w[:, 1, :, g, :], raw, w[:, 0, :, g, :].bitcast(F32), ALU.subtract))

        @block.gpsimd
        def _(pool):
            for l in range(2):
                for fc in range(FC):
                    pool.wait_ge(w_high, 2 * (l * FC + fc) + 1)
                    low_part(pool, l, fc, 0, lambda ins: ins.then_inc(w_low, 1))

        @block.sync
        def _(sp):
            def tokens():
                sp.dma_start(xr[:, 0:XT, :], a["x"][0].rearrange("(t p) d -> p t d", p=P)).then_inc(x_landed, 16)
                sp.dma_start(xr[:, XT:NT, :], a["ctx"][0].rearrange("(t p) d -> p t d", p=P)).then_inc(x_landed, 16)
                sp.dma_start(mask_in, a["masks"]).then_inc(x_landed, 16)

            def constants():
                sp.dma_start(const[:, :], a["const"]).then_inc(params_landed, 16)
                sp.dma_start(rows[:, :], a["rows"].partition_broadcast(P)).then_inc(params_landed, 16)

            def gate_biases():
                for g in range(2):
                    sec = a["ada_b"][0][(2 + 3 * g) * D:(3 + 3 * g) * D]
                    for row in (2 * g, 2 * g + 1):
                        sp.dma_start(gb[:, row, :], sec.partition_broadcast(P)).then_inc(rows_landed, 16)

            early = {1: constants, 2: tokens, 5: gate_biases}
            sp.dma_start(cols[:, :], a["cols"]).then_inc(cols_landed, 16)
            for n, pieces in enumerate(units):
                if n in early:
                    early[n]()
                if before_load[n]:
                    sp.wait_ge(SEM[before_load[n][0]], before_load[n][1])
                    if before_load[n][0] == "w_low":
                        sp.wait_ge(w_low, before_load[n][1])
                if n == unit_no[("w2", 3)]:
                    for i, name in enumerate(("ln1_g_2", "ln1_b_2", "ln2_g_2", "ln2_b_2")):
                        sp.dma_start(gb[:, i, :], a[name][0].partition_broadcast(P)).then_inc(ln_landed, 16)
                for dst, src in pieces:
                    sp.dma_start(dst(slot_of[n]), src).then_inc(unit_landed[slot_of[n]], 16)
                if n == unit_no[("wo0", 1)] + 3:
                    sp.wait_ge(gates_read, 1)
                    for g, row in ((0, 0), (1, 1)):
                        sec = a["ada_b"][1][(2 + 3 * g) * D:(3 + 3 * g) * D]
                        sp.dma_start(gb[:, row, :], sec.partition_broadcast(P)).then_inc(rows_landed, 16)
            moe_sync(sp)

        @block.tensor
        def _(pe):
            got = {}

            def await_next(s, n=1):
                got[s.name] = got.get(s.name, 0) + n
                pe.wait_ge(s, got[s.name])

            def bank(key):
                g = group[key]
                if g >= BANKS:
                    pe.wait_ge(freed[reader[g - BANKS]], nth[g - BANKS])
                return PS[g % BANKS]

            closed = [0]

            def close(ins, key):
                assert group[key] == closed[0], (key, group[key], closed[0])
                closed[0] += 1
                ins.then_inc(psum_ready, 1)

            used = [0]

            def unit(key):
                n = unit_no[key]
                assert n == used[0], (key, n, used[0])
                s, count = landed[n]
                pe.wait_ge(unit_landed[s], count)
                return s

            def release(ins):
                if unit_done[used[0]][0] == "units_used":
                    ins.then_inc(units_used, 1)
                used[0] += 1

            def mm(o, l, r, start, stop):
                return pe.matmul(o, l, r, start=start, stop=stop)

            def ada(l, blk):
                s = unit(("ada", l, blk))
                ps = bank(("adap", l, blk))
                for k in range(KC):
                    j = k % 4
                    m = mm(ps[32 * j:32 * j + 32, :], cT[:, k, :], ring_col(s, 0, 512)[:, k, :], k < 4, k >= 4)
                close(m, ("adap", l, blk))
                release(m)

            def ada2(l, blk):
                await_next(modp_ready)
                key = ("adat", l, blk)
                ps = bank(key)
                for i in range(4):
                    m = mm(ps[:, 2 * i:2 * i + 2], modp[:, ada_turn[l, blk], i * P:(i + 1) * P], C("sel2"), True, True)
                close(m, key)
                for row, v in gate_slots(l, blk):
                    key = ("adag", l, blk, row)
                    close(mm(bank(key)[:, :], C("selb", v * P, P), modp[:, ada_turn[l, blk], :], True, True), key)

            def turn(tag, tiles, src, ready, chunks=KC):
                for t in tiles:
                    ready(t)
                    for h in range((chunks + 3) // 4):
                        key = ("turn", tag, t, h)
                        ps = bank(key)
                        n = min(4, chunks - 4 * h)
                        for i in range(n):
                            k = 4 * h + i
                            m = pe.transpose(ps[:, i * P:(i + 1) * P], src(t)[:, k * P:(k + 1) * P], ident)
                        close(m, key)

            def stay(key, s, lo, n, t, rel=False, first=True, last=True):
                ps = bank(key)
                for k in range(KC):
                    m = mm(ps[:, 0:n], hT[:, k, t * P:(t + 1) * P], ring_col(s, lo, n)[:, k, :], k == 0, k == KC - 1)
                close(m, key)
                return m

            def move(key, s, lo, n, T, t0=0, o=0, close_it=True):
                ps = bank(key)
                for k in range(KC):
                    m = mm(ps[o:o + n, 0:T], ring_col(s, lo, n)[:, k, :], hT[:, k, t0:t0 + T], k == 0, k == KC - 1)
                if close_it:
                    close(m, key)
                return m

            def attention(us, between):
                for i in range(len(us) + 1):
                    if i < len(us):
                        u = us[i]
                        for r in range(nrows(u)):
                            key = ("score", u["tag"], r)
                            close(mm(bank(key)[:, 0:u["n"]], u["q"](r), u["k"](r), True, True), key)
                    if i == 0:
                        continue
                    u = us[i - 1]
                    n, nr, c = u["n"], nrows(u), u["n"] // P
                    await_next(p_ready)
                    pr = SB[:, (i - 1) % 2, :]
                    pv = None
                    for r in range(nr + 1):
                        if r < nr:
                            key = ("probt", u["tag"], r)
                            ps = bank(key)
                            for j in range(c):
                                m = pe.transpose(ps[:, j * P:(j + 1) * P], pr[:, r * n + j * P:r * n + (j + 1) * P],
                                                 ident)
                            close(m, key)
                        if r:
                            await_next(pt_ready)
                            if pv is None:
                                pv = bank(("pv", u["tag"]))
                            q = r - 1
                            lo = q * HD if u["heads"] == 4 else 0
                            many = u["heads"] == 4
                            for j in range(c):
                                m = mm(pv[:, lo:lo + HD], PT[:, q % 2, j * P:(j + 1) * P], u["v"](q, j),
                                       j == 0 and (many or q == 0), j == c - 1 and (many or q == nr - 1))
                    close(m, ("pv", u["tag"]))
                    between(i - 1)

            def project(name, tiles):
                for b in range(2):
                    s = unit((name, b))
                    for t in tiles:
                        m = stay((name, b, t), s, 0, 512, t)
                    release(m)

            def ffn(l, T):
                turn(("f", l), range(T), lambda t: xn[:, t % 2, :], lambda t: await_next(xn_ready))
                await_next(x_low, 2 * T)
                for j in range(FC // 2):
                    assert unit_no[("up", l, j)] == used[0]
                    for i in range(2):
                        w = w_split[i]
                        for g, (name, low) in enumerate((("gate", w_low), ("val", w_low_v))):
                            await_next(low)
                            key = (name, l, 2 * j + i)
                            ps = bank(key)
                            parts = [(k, *p) for k in range(KC) for p in ((0, hT_high), (0, hT_low), (1, hT_high))]
                            for n, (k, part, x) in enumerate(parts):
                                m = mm(ps[:, 0:T * P], w[:, part, k, g, :], x[:, k, 0:T * P], n == 0,
                                       n == len(parts) - 1)
                            close(m, key)
                    release(m)
                    if l == 0 and j < 4:
                        ada(1, ADA_LATE[j])
                        ada2(1, ADA_LATE[j])
                for u in range((FC + 3) // 4):
                    s = unit(("down", l, u))
                    n = min(4, FC - 4 * u)
                    await_next(hid_ready, n)
                    if u:
                        await_next(down_low_ready, 2)
                    for t in range(T):
                        for h in range(2):
                            key = ("down", l, t, h)
                            ps = bank(key)
                            for i in range(n):
                                k = 4 * u + i
                                tok, col = slice(t * P, (t + 1) * P), slice(h * 512, (h + 1) * 512)
                                if u == 0:
                                    m = mm(ps[:, :], hid[:, k, tok], ring_row(s, n)[:, i, col], k == 0, False)
                                    continue
                                x_hi, w_hi = hid_high[:, u % 2, i, tok], down_high[u % 2][:, i, col]
                                mm(ps[:, :], x_hi, w_hi, False, False)
                                mm(ps[:, :], hid_low[:, k, tok], w_hi, False, False)
                                m = mm(ps[:, :], x_hi, down_low[:, s, i, col], False, k == FC - 1)
                            if 4 * u + n == FC:
                                close(m, key)
                    release(m)

            await_next(silu_c)
            for blk in range(4):
                ada(0, blk)
                if blk == 0:
                    pe.wait_ge(params_landed, 32)
                ada2(0, blk)
            turn("a0", ALL, lambda t: xn[:, t % 2, :], lambda t: await_next(xn_ready))
            await_next(hT_ready)
            s = unit(("qkv", 0))
            for t in ALL:
                m = stay(("qkv", 0, t), s, 0, 512, t)
            release(m)
            await_next(qx_low_ready)
            for j, (key, z) in enumerate(Q_HALVES):
                s = unit(key) if z == 0 else slot_of[unit_no[key]]
                await_next(qw_low_ready)
                hi, lo = qw_high[j], hw_low[:, s, :, 256 * z:256 * z + 256]
                parts = [(k, *p) for k in range(KC) for p in ((hi, qx_high), (hi, qx_low), (lo, qx_high))]
                for t in ALL:
                    ps = bank((*key, t))
                    for n, (k, wt, x) in enumerate(parts):
                        m = mm(ps[:, 256 * z:256 * z + 256], x[:, k, t * P:(t + 1) * P], wt[:, k, :], n == 0,
                               n == len(parts) - 1)
                    if z:
                        close(m, (*key, t))
                if z:
                    release(m)
            for t in ALL:
                await_next(qk_ready)
                sbt = SB[:, t % 2, :]
                q = (sbt if t < XT else qkv[:, t, :])
                for j in range(3):
                    key = ("qkt", t, j)
                    ps = bank(key)
                    for i in range(4):
                        src = q[:, (4 * j + i) * P:(4 * j + i + 1) * P] if j < 2 else \
                            sbt[:, 1280 + i * P:1280 + (i + 1) * P]
                        m = pe.transpose(ps[:, i * P:(i + 1) * P], src, ident)
                    close(m, key)
            await_next(qT_ready)

            def with_ada(i):
                ada(*ADA_BETWEEN[i])
                ada2(*ADA_BETWEEN[i])

            attention(ATT0, with_ada)
            await_next(o_ready)
            turn("o0", ALL, lambda t: qkv[:, t, 0:D], lambda t: None)
            await_next(hT_ready)
            project("wo0", ALL)
            ffn(0, NT)

            turn("h1", ALL, lambda t: xn[:, t % 2, :], lambda t: await_next(xn_ready))
            await_next(hT_ready)
            s = unit(("hq", 0))
            for i in range(4):
                m = move(("hq", i), s, i * P, P, SEQ)
            release(m)
            await_next(hx_low_ready)
            for j, (key, z) in enumerate(HALVES):
                s = unit(key) if z == 0 else slot_of[unit_no[key]]
                await_next(hw_low_ready)
                hi, lo = hw_high[j % 2], hw_low[:, s, :, 256 * z:256 * z + 256]
                parts = [(k, *p) for k in range(KC) for p in ((hi, hx_high), (hi, hx_low), (lo, hx_high))]
                if key[0] in ("hq", "hf"):
                    for i in range(2):
                        g, T = (("hq", 4 + 2 * z + i), SEQ) if key[0] == "hq" else ((*key, 2 * z + i), TOK)
                        ps = bank(g)
                        for n, (k, wt, x) in enumerate(parts):
                            m = mm(ps[:, 0:T], wt[:, k, i * P:(i + 1) * P], x[:, k, 0:T], n == 0,
                                   n == len(parts) - 1)
                        close(m, g)
                else:
                    for t in (ALL if key[0] == "hv" else XS):
                        ps = bank((*key, t))
                        for n, (k, wt, x) in enumerate(parts):
                            m = mm(ps[:, 256 * z:256 * z + 256], x[:, k, t * P:(t + 1) * P], wt[:, k, :], n == 0,
                                   n == len(parts) - 1)
                        if z:
                            close(m, (*key, t))
                    if z == 0:
                        m.then_inc(half_used, 1)
                if z:
                    release(m)

            def forget(d, b, i):
                s = unit(("hf", d, b)) if i == 0 else slot_of[unit_no[("hf", d, b)]]
                m = move(("hf", d, b, i), s, i * P, P, TOK)
                if i == 3:
                    release(m)

            def turn_keys(d, b, i):
                ps = bank(("kt", d, b, i))
                for t in range(2):
                    m = pe.transpose(ps[:, t * P:(t + 1) * P], kdec[:, i, t * P:(t + 1) * P], ident)
                close(m, ("kt", d, b, i))

            def context_state(d, b, i):
                await_next(kd_turned)
                ps = bank(("st", d, b, i))
                h = 4 * b + i
                for t in range(2):
                    m = mm(ps[:, 0:P], rD[:, i % 2, t, :], rv[:, XT + t, h * P:(h + 1) * P], t == 0, t == 1)
                close(m, ("st", d, b, i))

            for d in range(2):
                late = 1 - d
                for b in range(2):
                    rk = rks[b]
                    await_next(kdec_ready)
                    for n in range(-1, NL + 1):
                        if n >= 0:
                            await_next(qk_scaled)
                        for t in ([late] if n == NL else XS):
                            key = ("lev", d, b, n, 0 if n == NL else t)
                            ps = bank(key)
                            for i in range(4):
                                if n < 0:
                                    l, r = rk[:, i, t * P:(t + 1) * P], rq[:, 4 * b + i, t * P:(t + 1) * P]
                                else:
                                    st = 1 - t if n == NL else t
                                    l, r = KL[n % 2][:, i, st * P:(st + 1) * P], QL[n % 2][:, i, t * P:(t + 1) * P]
                                m = mm(ps[:, i * P:(i + 1) * P], l, r, True, True)
                            close(m, key)
                        if 1 <= n <= 4:
                            context_state(d, b, n - 1)
                        if 0 <= n < 4:
                            turn_keys(d, b, n)
                            if after(d, b):
                                forget(*after(d, b), n)
                    await_next(qk_scaled)
                    pe.wait_ge(freed["act"], nth[group["st", d, b, 3]])
                    await_next(o_ready)
                    for t in XS:
                        key = ("ro", d, b, t)
                        ps = bank(key)
                        for i in range(4):
                            h = 4 * b + i
                            o = ps[:, i * P:(i + 1) * P]
                            mm(o, QL[(NL + 1) % 2][:, i, t * P:(t + 1) * P], rS[:, i, :], True, False)
                            if t == late:
                                mm(o, rC[:, i, :], rv[:, 1 - late, h * P:(h + 1) * P], False, False)
                            m = mm(o, rA[:, t, i, :], rv[:, t, h * P:(h + 1) * P], False, True)
                        close(m, key)
            await_next(o_ready)
            turn("o1", XS, lambda t: ro[:, t, :], lambda t: None)
            await_next(hT_ready)
            project("wo1", XS)
            ffn(1, XT)
            await_next(x2_ready)
            turn("x2", XS, lambda t: xr[:, t, :], lambda t: None)
            await_next(hT_ready)
            at, s = -1, None
            split_to = -1

            def w2_parts(u, z):
                nonlocal split_to
                j = W_HALVES.index((u, z))
                if j > split_to:
                    if j == 0:
                        await_next(x2_low_ready)
                    await_next(w2_low_ready)
                    split_to = j
                hi, lo = w2_high[j % 3], hw_low[:, s, :, 256 * z:256 * z + 256]
                return [(k, *p) for k in range(KC) for p in ((hi, x2_high), (hi, x2_low), (lo, x2_high))]

            for u, kind, c, dst in W2:
                if u != at:
                    if at >= 0:
                        release(m)
                    at, s = u, unit(("w2", u))
                at_half = (u, (c[0] if kind == "N" else c) // 256)
                if at_half not in W_HALVES:
                    if kind == "T":
                        m = move(("w2", dst), s, c, P, SEQ)
                    elif kind == "K":
                        for o in (0, 64):
                            m = move(("w2", dst), s, c, 64, SEQ, o=o, close_it=o == 64)
                    else:
                        for t in XS:
                            m = stay(("w2", dst, t), s, c[0], c[1], t)
                elif kind == "T":
                    parts = w2_parts(*at_half)
                    ps = bank(("w2", dst))
                    for n, (k, wt, x) in enumerate(parts):
                        m = mm(ps[:, 0:SEQ], wt[:, k, c % 256:c % 256 + P], x[:, k, :], n == 0, n == len(parts) - 1)
                    close(m, ("w2", dst))
                else:
                    for z in range(c[1] // 256):
                        parts = w2_parts(u, z)
                        for t in XS:
                            ps = bank(("w2", dst, t))
                            for n, (k, wt, x) in enumerate(parts):
                                m = mm(ps[:, 256 * z:256 * z + 256], x[:, k, t * P:(t + 1) * P], wt[:, k, :], n == 0,
                                       n == len(parts) - 1)
                            if 256 * (z + 1) == c[1]:
                                close(m, ("w2", dst, t))
                        if 256 * (z + 1) < c[1]:
                            m.then_inc(half2_used, 1)
            release(m)
            await_next(qT_ready)
            attention(ATT2, lambda i: None)
            await_next(o_ready)
            turn("oa2", XS, lambda t: oA[:, t, :], lambda t: None, chunks=2)
            turn("ob2", XS, lambda t: oB[:, t, :], lambda t: None)
            await_next(hT_ready)
            sa = unit(("pa", 0))
            release(None)
            for b in range(2):
                s = unit(("pb", b))
                for t in XS:
                    ps = bank(("pa", b, t))
                    for k in range(2):
                        m = mm(ps[:, :], hT[:, k, SEQ + t * P:SEQ + (t + 1) * P],
                               ring_row(sa, 2)[:, k, b * 512:(b + 1) * 512], k == 0, k == 1)
                    close(m, ("pa", b, t))
                    m = stay(("pb", b, t), s, 0, 512, t)
                release(m)
            await_next(merged_ready)
            turn("m2", XS, lambda t: ga[:, t, :], lambda t: None)
            await_next(hT_ready)
            project("wo2", XS)
            await_next(y_ready)
            turn("y2", XS, lambda t: xr[:, t, :], lambda t: None)
            await_next(hT_ready)
            pe.wait_ge(rw_landed, 16)
            ps = bank(("route",))
            for t in XS:
                for k in range(KC):
                    m = mm(ps[:, t * E:(t + 1) * E], hT[:, k, t * P:(t + 1) * P], rw[:, k, :], k == 0, k == KC - 1)
            close(m, ("route",))
            await_next(route_ready)
            ps = bank(("rank",))
            mm(ps[:, 0:E], C("before"), chosen[:, 0, :], True, True)
            mm(ps[:, E:2 * E], C("ones"), chosen[:, 0, :], True, False)
            mm(ps[:, E:2 * E], C("before"), chosen[:, 1, :], False, True)
            mm(ps[:, 2 * E:3 * E], C("ones"), chosen[:, 0, :], True, False)
            close(mm(ps[:, 2 * E:3 * E], C("ones"), chosen[:, 1, :], False, True), ("rank",))
            pe.wait_ge(freed["dve"], nth[-1])
            BG, BU, BX, BS, BH, BD = PS[:6]

            def gather():
                for k in range(KC):
                    for t in XS:
                        m = mm(BX[:, k * SLOTS:(k + 1) * SLOTS], xr[:, t, k * P:(k + 1) * P], sel[:, t, 0:SLOTS],
                               t == 0, t == 1)
                m.then_inc(gx_ready, 1)

            def turn_sel():
                for t in XS:
                    m = pe.transpose(BS[:, t * P:(t + 1) * P], selg[:, t, :], ident)
                m.then_inc(gt_ready, 1)

            def item(i, ahead):
                def halves(out, slots, row, done):
                    for k in range(KC):
                        for f in range(2):
                            mm(out[64 * f:64 * f + 64, :], xg[:, k, :],
                               moe_slot[slots + f].rearrange("p (k n) -> p k n", k=KC)[:, k, :], k == 0, False)
                    for f in range(2):
                        m = mm(out[64 * f:64 * f + 64, :], C("ones")[row:row + 1, 0:64],
                               bias[row:row + 1, f * 512:(f + 1) * 512], False, True)
                    m.then_inc(done, 1)

                pe.wait_ge(gate_landed, 48 * (i + 1))
                pe.wait_ge(xg_ready, i + 1 + ahead)
                halves(BG, 0, 0, gg_ready)
                pe.wait_ge(up_landed, 48 * (i + 1))
                halves(BU, 2, 32, gu_ready)
                pe.wait_ge(sel_ready, i + 2 + 2 * ahead)
                gather()
                pe.wait_ge(hh_ready, i + 1)
                for c in range(4):
                    m = pe.transpose(BH[:, c * P:(c + 1) * P], hh[:, c * P:(c + 1) * P], ident)
                m.then_inc(ht_ready, 1)
                pe.wait_ge(down_landed, 48 * (i + 1))
                pe.wait_ge(hhT_ready, i + 1)
                for k in range(KC):
                    for h in range(2):
                        mm(BD[64 * h:64 * h + 64, :], hhT[:, k % 4, 64 * (k // 4):64 * (k // 4) + 64],
                           moe_slot[4 + k // 4].rearrange("p (k n) -> p k n", k=4)[:, k % 4, h * 512:(h + 1) * 512],
                           k == 0, False)
                for h in range(2):
                    m = mm(BD[64 * h:64 * h + 64, :], C("ones")[64:65, 0:64], bias[64:65, h * 512:(h + 1) * 512],
                           False, True)
                m.then_inc(gd_ready, 1)
                pe.wait_ge(yg_ready, i + 1)
                pe.wait_ge(selgT_ready, i + 1 + ahead)
                for j in range(4):
                    h, t = j // 2, j % 2
                    pe.wait_ge(c_added, 4 * i + 1 + max(j - 1, 0))
                    mm(PS[6 + t][:, :], selgT[64 * h:64 * h + 64, t, :], yg[64 * h:64 * h + 64, :], True, True)\
                        .then_inc(c_ready, 1)
                turn_sel()

            pe.wait_ge(sel_ready, 1)
            gather()
            turn_sel()
            with pe.Fori(0, E) as i:
                item(i, 0)

            pe.wait_ge(rank_ready, 1)

            def first_further():
                pe.wait_ge(sel_ready, E + 3)
                pe.wait_ge(xg_ready, E + 1)
                gather()
                pe.wait_ge(selgT_ready, E + 1)
                turn_sel()

            further(pe, lambda j: item(j + E, 1), first_further)

        @block.scalar
        def _(act):
            do, signal, await_next, take, pe_past = helpers(act, act_step, "act")
            F = freed["act"]

            def ada(l, blk):
                ps = take(("adap", l, blk))
                do(act.activation(modp[:, ada_turn[l, blk], :], ps[:, :], ACT.Copy), F)
                signal(modp_ready)

            def std(n, width, eps="eps6"):
                await_next(ss_ready)
                do(act.activation(stat[:, n:n + width], stat[:, n:n + width], ACT.Sqrt, bias=C(eps)[:, 0:1],
                                  scale=1.0 / {1: D, 20: HD, 8: P}[width]), std_ready)

            def norm_turn(tag, tiles, l, i, split=False):
                for t in tiles:
                    std(t, 1)
                await_next(coef_ready)
                for t in tiles:
                    v = 0 if t < XT else 1
                    for h in range(2):
                        ps = take(("turn", tag, t, h))
                        if split:
                            split_no[0] += 1
                            if split_no[0] > 2:
                                act.wait_ge(x_low, split_no[0] - 2)
                        for j in range(4):
                            k = 4 * h + j
                            o = modp[:, h, j * P:(j + 1) * P] if split else hT[:, k, t * P:(t + 1) * P]
                            do(act.activation(o, ps[:, j * P:(j + 1) * P], ACT.Identity,
                                              bias=modT[:, l, 24 * i + k, v:v + 1], scale=coef[:, l, i, k, v:v + 1]),
                               F if j == 3 else act_step)
                        if split:
                            do(act.activation(hT_high[:, 4 * h:4 * h + 4, t * P:(t + 1) * P],
                                              modp[:, h, :].rearrange("p (k c) -> p k c", k=4), ACT.Copy), x_high)
                if not split:
                    signal(hT_ready)

            def plain_turn(tag, tiles, chunks=KC, tell=True, at=0, shift=0):
                for t in tiles:
                    for h in range((chunks + 3) // 4):
                        ps = take(("turn", tag, t, h))
                        n = min(4, chunks - 4 * h)
                        do(act.activation(hT[:, at + 4 * h:at + 4 * h + n, shift + t * P:shift + (t + 1) * P],
                                          ps[:, 0:n * P].rearrange("p (k q) -> p k q", k=n), ACT.Copy), F)
                if tell:
                    signal(hT_ready)

            def attention(us, between):
                for i in range(len(us) + 1):
                    if i:
                        u = us[i - 1]
                        for r in range(nrows(u)):
                            ps = take(("probt", u["tag"], r))
                            do(act.activation(PT[:, r % 2, 0:u["n"]], ps[:, 0:u["n"]], ACT.Copy), F)
                            signal(pt_ready)
                        between(i - 1)
                    if i == len(us):
                        continue
                    u = us[i]
                    n, hs = u["n"], u["heads"]
                    w = n if hs == 4 else 3 * n
                    st = stat[:, 64 + 32 * (i % 2):96 + 32 * (i % 2)]
                    await_next(max_ready)
                    for r in range(hs):
                        pr = SB[:, i % 2, r * w:(r + 1) * w]
                        do(act.activation(pr, pr, ACT.Exp, bias=st[:, 4 + r:5 + r], accum_out=st[:, 12 + r:13 + r]))
                    signal(p_ready)
                    if u["sink"] is not None:
                        do(act.activation(st[:, 8:12], st[:, 8:12], ACT.Exp))
                    signal(sum_ready)

            def ffn(l, T):
                norm_turn(("f", l), range(T), l, 1, split=True)
                n = T * P

                def weights_high(fc):
                    s, count = landed[unit_no[("up", l, fc // 2)]]
                    act.wait_ge(unit_landed[s], count)
                    if fc >= 2:
                        pe_past(("val", l, fc - 2))
                    raw = ring[:, s, :].rearrange("p (k g i c) -> p k g i c", k=KC, g=2, i=2)
                    for g in range(2):
                        do(act.activation(w_split[fc % 2][:, 0, :, g, :], raw[:, :, g, fc % 2, :], ACT.Copy), w_high)

                weights_high(0)
                weights_high(1)
                for fc in range(FC):
                    ps = take(("gate", l, fc))
                    t1 = ft[:, fc % 2, 0:n]
                    if fc >= 2:
                        act.wait_ge(silu_used, (FC if l else 0) + fc - 1)
                    do(act.activation(t1, ps[:, 0:n], ACT.Identity, bias=COL("cb", l * FC + fc, 1),
                                      scale=COL("cw", (l * 3 + 1) * FC + fc, 1)), conv1)
                    await_next(conv2)
                    do(act.activation(ft[:, 2 + fc % 2, 0:n], t1, ACT.Silu), silu_ready)
                    signal(F)
                    if fc + 2 < FC:
                        weights_high(fc + 2)
                    if l == 0 and fc % 2 and fc < 8:
                        ada(1, ADA_LATE[fc // 2])

                act.wait_ge(hid_ready, (l + 1) * FC)
                pe_past(("val", l, FC - 1))
                for u in range(1, (FC + 3) // 4):
                    m = min(4, FC - 4 * u)
                    if u >= 3:
                        act.wait_ge(units_used, unit_done[unit_no[("down", l, u - 2)]][1])
                    s, count = landed[unit_no[("down", l, u)]]
                    do(act.activation(hid_high[:, u % 2, 0:m, 0:n], hid[:, 4 * u:4 * u + m, 0:n], ACT.Copy),
                       down_hid_high)
                    act.wait_ge(unit_landed[s], count)
                    do(act.activation(down_high[u % 2][:, 0:m, :], ring_row(s, m), ACT.Copy), down_w_high)

            silu_used = hid_ready
            split_no = [0]
            act.wait_ge(cols_landed, 16)
            await_next(zeros_ready)
            do(act.activation(cT[:, :, 0:2], COL("c").rearrange("p (k v) -> p k v", v=2), ACT.Silu), silu_c)
            for blk in range(4):
                ada(0, blk)
            act.wait_ge(params_landed, 32)
            norm_turn("a0", ALL, 0, 0)
            do(act.activation(qx_high[:, :, :], hT[:, :, :], ACT.Copy), qx_high_ready)
            for j, (key, z) in enumerate(Q_HALVES):
                s, count = landed[unit_no[key]]
                act.wait_ge(unit_landed[s], count)
                do(act.activation(qw_high[j][:, :, :], ring_col(s, 256 * z, 256), ACT.Copy), qw_high_ready)
            for b in range(3):
                for t in ALL:
                    ps = take(("qkv", b, t))
                    do(act.activation(qkv[:, t, b * 512:(b + 1) * 512], ps[:, :], ACT.Copy), F)
                    if b == 2:
                        signal(qkv_ready)
            for t in ALL:
                std(t * 20, 20)
                for j in range(3):
                    ps = take(("qkt", t, j))[:, :].rearrange("p (k q) -> p k q", k=4)
                    if j < 2:
                        do(act.activation(qT[:, 4 * j:4 * j + 4, t * P:(t + 1) * P], ps, ACT.Copy), F)
                    else:
                        for z in range(2):
                            o = kT[64 * z:64 * z + 64, z::2, t * P:(t + 1) * P]
                            do(act.activation(o, ps[64 * z:64 * z + 64, :, :], ACT.Copy), F if z else act_step)
            signal(qT_ready)

            def with_ada(i):
                ada(*ADA_BETWEEN[i])

            attention(ATT0, with_ada)
            plain_turn("o0", ALL)
            ffn(0, NT)

            norm_turn("h1", ALL, 1, 0)
            do(act.activation(hx_high[:, :, :], hT[:, :, :], ACT.Copy), hx_high_ready)
            await_next(lb_ready)
            do(act.activation(stat[:, 176:192], stat[:, 176:192], ACT.Exp), exp_lb)

            def take_queries(lo, hi):
                for i in range(lo, hi):
                    ps = take(("hq", i))
                    do(act.activation(rq[:, i, :], ps[:, 0:SEQ], ACT.Silu), F)

            def half_high(j):
                key, z = HALVES[j]
                s, count = landed[unit_no[key]]
                act.wait_ge(unit_landed[s], count)
                if j >= 2:
                    before, z2 = HALVES[j - 2]
                    if before[0] == "hq":
                        pe_past(("hq", 5 + 2 * z2))
                    elif z2:
                        pe_past(unit_end[before])
                    else:
                        act.wait_ge(half_used, (j - 2) // 2)
                do(act.activation(hw_high[j % 2][:, :, :], ring_col(s, 256 * z, 256), ACT.Copy), hw_high_ready)

            half_high(0)
            half_high(1)
            take_queries(0, 6)
            half_high(2)
            take_queries(6, 8)
            half_high(3)
            for j, (name, b) in ((4, ("hv", 0)), (6, ("hv", 1)), (8, ("hg", 0)), (10, ("hg", 1))):
                if j < len(HALVES):
                    half_high(j)
                for t in (ALL if name == "hv" else XS):
                    ps = take((name, b, t))
                    cut = (slice(None), t, slice(b * 512, (b + 1) * 512))
                    if name == "hv":
                        do(act.activation(rv[cut], ps[:, :], ACT.Copy), F)
                    else:
                        do(act.activation(rg[cut], ps[:, :], ACT.Silu), F)
                if j < len(HALVES):
                    half_high(j + 1)

            def forget(d, b, i):
                ps = take(("hf", d, b, i))
                do(act.activation(rks[b][:, i, :], ps[:, :], ACT.Copy), F)

            def sigmoid(d, b):
                do(act.activation(rks[b][:, :, :], rks[b][:, :, :], ACT.Sigmoid), sig_ready)

            def log_forget(d, b):
                await_next(forget_ready)
                do(act.activation(rlog[:, :, :], rks[b][:, :, :], ACT.Ln), state_k)

            def context_decay(d, b):
                await_next(sums_ready)
                last = TOK - 1 if d == 0 else SEQ
                for i in range(4):
                    do(act.activation(kdec[:, i, :], rbs[b][:, i, SEQ:TOK], ACT.Exp,
                                      bias=rbs[b][:, i, last:last + 1], scale=-1.0),
                       kexp_ready if i == 3 else act_step)

            def take_keys(d, b, i):
                ps = take(("kt", d, b, i))
                do(act.activation(rD[:, i % 2, :, :], ps[:, 0:SEQ].rearrange("p (t c) -> p t c", t=2),
                                  ACT.Copy), F)
                signal(kd_turned)

            def take_state(d, b, i):
                ps = take(("st", d, b, i))
                do(act.activation(rS[:, i, :], ps[:, 0:P], ACT.Copy), F)

            for i in range(4):
                forget(0, 0, i)
            for step in (sigmoid, log_forget, context_decay):
                step(0, 0)
            for d in range(2):
                for b in range(2):
                    for n in range(NL + 1):
                        await_next(diff_ready)
                        h = LEVELS[n] if n < NL else P
                        back, seen_half = late_early(EL[n % 2], h, d)
                        do(act.activation(back, back, ACT.Exp))
                        do(act.activation(seen_half, seen_half, ACT.Exp, scale=-1.0), exp_ready)
                        if 2 <= n <= 5:
                            take_state(d, b, n - 2)
                        if 1 <= n <= 4:
                            take_keys(d, b, n - 1)
                            if after(d, b):
                                forget(*after(d, b), n - 1)
                        if after(d, b) and n == 4:
                            sigmoid(*after(d, b))
                        if after(d, b) and n == 5:
                            log_forget(*after(d, b))
                    await_next(diff_ready)
                    do(act.activation(EL[(NL + 1) % 2], rbs[b][:, :, 0:SEQ], ACT.Exp), exp_ready)
                    if after(d, b):
                        context_decay(*after(d, b))
            for t in XS:
                std(t * 8, 8)
            plain_turn("o1", XS)
            ffn(1, XT)
            plain_turn("x2", XS)
            do(act.activation(x2_high, hT[:, :, 0:SEQ], ACT.Copy), x2_high_ready)

            def w2_half_high(i):
                if i < len(W_HALVES):
                    u, z = W_HALVES[i]
                    slot, count = landed[unit_no[("w2", u)]]
                    act.wait_ge(unit_landed[slot], count)
                    do(act.activation(w2_high[i % 3][:, :, :], ring_col(slot, 256 * z, 256), ACT.Copy), w2_high_ready)

            for i in range(3):
                w2_half_high(i)
            wide_ones = 0
            for entry, (u, kind, c, dst) in enumerate(W2):
                name, j = dst
                if kind == "N" and c[1] == 512:
                    wide_ones += 1
                    act.wait_ge(half2_used, wide_ones)
                    w2_half_high(W_HALVES.index((u, 0)) + 3)
                if kind == "N":
                    for t in XS:
                        ps = take(("w2", dst, t))
                        o = {"av": lambda: av[:, t, j:j + c[1]], "bv": lambda: bv[:, t, :],
                             "g": lambda: (ga if j < 2 else gb2)[:, t, j % 2 * 512:j % 2 * 512 + 512]}[name]()
                        do(act.activation(o, ps[:, 0:c[1]], ACT.Sigmoid if name == "g" else ACT.Copy), F)
                else:
                    ps = take(("w2", dst))
                    if j < (6 if name == "aT" else 8):
                        do(act.activation((aT if name == "aT" else bT)[:, j, :], ps[:, 0:SEQ], ACT.Copy,
                                          scale=HD ** -0.5), F)
                    else:
                        if (name, j) == ("aT", 6):
                            await_next(zeros_ready)
                        for z in range(2):
                            o = aK[:, 2 * (j - 6) + z, :] if name == "aT" else bK[:, 2 * (j - 8) + z, :]
                            do(act.activation(o[64 * z:64 * z + 64, :], ps[64 * z:64 * z + 64, 0:SEQ], ACT.Copy),
                               F if z else act_step)
                z = ((c[0] + c[1] if kind == "N" else c + P) - 1) // 256
                after_it = W2[entry + 1] if entry + 1 < len(W2) else None
                if (u, z) in W_HALVES and (after_it is None or after_it[0] != u or
                                           (after_it[2][0] if after_it[1] == "N" else after_it[2]) >= 256 * (z + 1)):
                    w2_half_high(W_HALVES.index((u, z)) + 3)
            signal(qT_ready)
            attention(ATT2, lambda i: None)
            plain_turn("oa2", XS, chunks=2, tell=False, shift=SEQ)
            plain_turn("ob2", XS)
            plain_turn("m2", XS)
            for t in XS:
                std(t, 1, "eps5")
            plain_turn("y2", XS)
            await_next(route_max)
            for t in XS:
                do(act.activation(gate[:, t, :], lgx[:, t, 0:E], ACT.Exp, bias=tst[:, t:t + 1]),
                   gate_exp if t else act_step)

            def take_gather():
                act.activation(xg[:, :, :], PS[2][:, :].rearrange("p (k s) -> p k s", k=KC), ACT.Copy)\
                    .then_inc(xg_ready, 1)

            def take_sel():
                act.activation(selgT[:, :, :], PS[3][:, 0:2 * P].rearrange("p (t c) -> p t c", t=2), ACT.Copy)\
                    .then_inc(selgT_ready, 1)

            def item(i, ahead):
                act.wait_ge(hm_ready, i + 1)
                act.activation(sg[:, :], hm[:, :], ACT.Sigmoid, scale=1.702).then_inc(sg_ready, 1)
                act.wait_ge(gx_ready, i + 2 + ahead)
                take_gather()
                act.wait_ge(ht_ready, i + 1)
                act.activation(hhT[:, :, :], PS[4][:, :].rearrange("p (c s) -> p c s", c=4), ACT.Copy)\
                    .then_inc(hhT_ready, 1)
                act.wait_ge(gd_ready, i + 1)
                act.activation(yg[:, :], PS[5][:, :], ACT.Copy).then_inc(yg_ready, 1)
                act.wait_ge(gt_ready, i + 2 + ahead)
                take_sel()

            act.wait_ge(gx_ready, 1)
            take_gather()
            act.wait_ge(gt_ready, 1)
            take_sel()
            with act.Fori(0, E) as i:
                item(i, 0)
            act.wait_ge(rank_ready, 1)

            def first_further():
                act.wait_ge(gx_ready, E + 2)
                take_gather()
                act.wait_ge(gt_ready, E + 2)
                take_sel()

            further(act, lambda j: item(j + E, 1), first_further)
            for t in XS:
                std(t, 1, "eps5")

        @block.vector
        def _(dve):
            do, signal, await_next, take, pe_past = helpers(dve, dve_step, "dve")
            F = freed["dve"]
            TT, STT = dve.tensor_tensor, dve.scalar_tensor_tensor

            def rms(tag, tiles):
                for t in tiles:
                    if t >= 2:
                        pe_past(("turn", tag, t - 2, 1))
                    do(dve.tensor_tensor_reduce(out=xn[:, t % 2, :], in0=xr[:, t, :], in1=xr[:, t, :], scale=1.0,
                                                scalar=0.0, op0=ALU.mult, op1=ALU.add,
                                                accum_out=stat[:, t:t + 1]), ss_ready)
                    await_next(std_ready)
                    do(dve.reciprocal(stat[:, t:t + 1], stat[:, t:t + 1]))
                    do(dve.tensor_scalar(xn[:, t % 2, :], xr[:, t, :], stat[:, t:t + 1], None, ALU.mult), xn_ready)

            def ada2(l, blk):
                ps = take(("adat", l, blk))
                o = modT[:, l, 4 * blk:4 * blk + 4, :]
                do(TT(o, ps[:, 0:8].rearrange("p (k v) -> p k v", v=2),
                      COL("adab", l * 48 + 4 * blk, 4).unsqueeze(2).broadcast_to((P, 4, 2)), ALU.add), F)
                for row, v in gate_slots(l, blk):
                    ps = take(("adag", l, blk, row))
                    h = G_BLOCKS[blk][1]
                    if l == 0 and blk == 4 and row == 0:
                        dve.wait_ge(rows_landed, 64)
                    if l == 1 and blk == 4 and row == 0:
                        dve.wait_ge(rows_landed, 96)
                    o = gb[:, row, h * 512:(h + 1) * 512]
                    do(TT(o, o, ps[:, :], ALU.add), F)

            def coefs(l, i):
                sc = modT[:, l, 24 * i + 8:24 * i + 16, :]
                g = COL("n1" if i == 0 else "n2", l * 8, 8).unsqueeze(2).broadcast_to((P, 8, 2))
                do(STT(out=coef[:, l, i, :, :], in0=sc, scalar=1.0, in1=g, op0=ALU.add, op1=ALU.mult), coef_ready)

            def attention(us, between):
                for i in range(len(us) + 1):
                    if i < len(us):
                        u = us[i]
                        n, hs = u["n"], u["heads"]
                        st = stat[:, 64 + 32 * (i % 2):96 + 32 * (i % 2)]
                        for r in range(nrows(u)):
                            ps = take(("score", u["tag"], r))
                            o = SB[:, i % 2, r * n:(r + 1) * n]
                            if u["slope"]:
                                sl, diff = u["slope"][r]
                                do(STT(out=o, in0=diff, scalar=-sl, in1=ps[:, 0:n], op0=ALU.mult, op1=ALU.add), F)
                            elif u["mask"] is not None:
                                do(TT(o, ps[:, 0:n], u["mask"], ALU.add), F)
                            else:
                                do(dve.tensor_copy(o, ps[:, 0:n]), F)
                        w = n if hs == 4 else 3 * n
                        do(dve.tensor_reduce(st[:, 0:hs], SB[:, i % 2, 0:hs * w].rearrange("p (h w) -> p h w", h=hs),
                                             AX, ALU.max))
                        if u["sink"] is not None:
                            do(TT(st[:, 0:4], st[:, 0:4], u["sink"], ALU.max))
                            do(TT(st[:, 8:12], u["sink"], st[:, 0:4], ALU.subtract))
                        do(dve.tensor_scalar(st[:, 4:4 + hs], st[:, 0:hs], -1.0, None, ALU.mult), max_ready)
                    if i:
                        u = us[i - 1]
                        hs = u["heads"]
                        st = stat[:, 64 + 32 * ((i - 1) % 2):96 + 32 * ((i - 1) % 2)]
                        await_next(sum_ready)
                        if u["sink"] is not None:
                            do(TT(st[:, 12:16], st[:, 12:16], st[:, 8:12], ALU.add))
                        do(dve.reciprocal(st[:, 16:16 + hs], st[:, 12:12 + hs]))
                        ps = take(("pv", u["tag"]))
                        do(TT(u["out"].rearrange("p (h c) -> p h c", h=hs),
                              ps[:, 0:hs * HD].rearrange("p (h c) -> p h c", h=hs),
                              st[:, 16:16 + hs].unsqueeze(2).broadcast_to((P, hs, HD)), ALU.mult), F)
                        between(i - 1)
                signal(o_ready)

            def residual(key, tiles, gates):
                for b in range(2):
                    for t in tiles:
                        gated_add((key, b, t), b, t, gates)

            def gated_add(key, b, t, gates):
                ps = take(key)
                tmp = xn[:, 0, 0:512]
                o = xr[:, t, b * 512:(b + 1) * 512]
                do(TT(tmp, ps[:, :], gb[:, gates[0 if t < XT else 1], b * 512:(b + 1) * 512], ALU.mult), F)
                do(TT(o, o, tmp, ALU.add))

            def ffn(l, T):
                coefs(l, 1)
                rms(("f", l), range(T))
                for t in range(T):
                    for h in range(2):
                        await_next(x_high)
                        cut = (slice(None), slice(4 * h, 4 * h + 4), slice(t * P, (t + 1) * P))
                        do(TT(hT_low[cut], modp[:, h, :].rearrange("p (k c) -> p k c", k=4),
                              hT_high[cut].bitcast(F32), ALU.subtract), x_low)
                n = T * P

                def weights_low(fc):
                    await_next(w_high, 2)
                    low_part(dve, l, fc, 1, lambda ins: do(ins, w_low_v))

                weights_low(0)
                weights_low(1)
                seg = T // 2
                for fc in range(FC):
                    await_next(conv1)
                    g = PS[group[("gate", l, fc)] % BANKS][:, 0:n].rearrange("p (s t) -> p s t", s=seg)
                    t1 = ft[:, fc % 2, 0:n].rearrange("p (s t) -> p s t", s=seg)
                    cw = lambda i: COL("cw", (l * 3 + i) * FC + fc, 1)
                    do(STT(out=t1[:, :, 1:SEQ], in0=g[:, :, 0:SEQ - 1], scalar=cw(0), in1=t1[:, :, 1:SEQ],
                           op0=ALU.mult, op1=ALU.add))
                    do(STT(out=t1[:, :, 0:SEQ - 1], in0=g[:, :, 1:SEQ], scalar=cw(2), in1=t1[:, :, 0:SEQ - 1],
                           op0=ALU.mult, op1=ALU.add), conv2)
                    await_next(silu_ready)
                    ps = take(("val", l, fc))
                    do(TT(hid[:, fc, 0:n], ft[:, 2 + fc % 2, 0:n], ps[:, 0:n], ALU.mult), F)
                    signal(hid_ready)
                    if fc + 2 < FC:
                        weights_low(fc + 2)
                    if l == 0 and fc % 2 and fc < 8:
                        ada2(1, ADA_LATE[fc // 2])
                for u in range(1, (FC + 3) // 4):
                    m = min(4, FC - 4 * u)
                    s = slot_of[unit_no[("down", l, u)]]
                    await_next(down_hid_high)
                    do(TT(hid_low[:, 4 * u:4 * u + m, 0:n], hid[:, 4 * u:4 * u + m, 0:n],
                          hid_high[:, u % 2, 0:m, 0:n].bitcast(F32), ALU.subtract), down_low_ready)
                    await_next(down_w_high)
                    do(TT(down_low[:, s, 0:m, :], ring_row(s, m), down_high[u % 2][:, 0:m, :].bitcast(F32),
                          ALU.subtract), down_low_ready)
                for t in range(T):
                    for h in range(2):
                        gated_add(("down", l, t, h), h, t, GATE[(l, 1)])

            do(dve.memset(cT[:, :, :], 0.0), zeros_ready)
            dve.wait_ge(cols_landed, 16)
            dve.wait_ge(params_landed, 32)
            do(dve.tensor_scalar(ROW("qg"), ROW("qg"), HD ** -0.5, None, ALU.mult))
            for blk in range(4):
                ada2(0, blk)
            dve.wait_ge(x_landed, 48)
            do(dve.tensor_copy(masks[:, :], mask_in))
            coefs(0, 0)
            rms("a0", ALL)
            await_next(qx_high_ready)
            do(TT(qx_low[:, :, :], hT[:, :, :], qx_high[:, :, :].bitcast(F32), ALU.subtract), qx_low_ready)
            for j, (key, z) in enumerate(Q_HALVES):
                s = slot_of[unit_no[key]]
                await_next(qw_high_ready)
                do(TT(hw_low[:, s, :, 256 * z:256 * z + 256], ring_col(s, 256 * z, 256),
                      qw_high[j][:, :, :].bitcast(F32), ALU.subtract), qw_low_ready)
            for t in ALL:
                await_next(qkv_ready)
                if t == NT - 1:
                    pe_past(("qkv", 2, NT - 1))
                    for z in range(2):
                        do(dve.memset(kT[64 * z:64 * z + 64, 1 - z::2, :], 0.0))
                if t >= 2:
                    pe_past(("qkt", t - 2, 2))
                sbt = SB[:, t % 2, :]
                qk = qkv[:, t, 0:1280].rearrange("p (h c) -> p h c", h=20)
                sq = sbt[:, 0:1280].rearrange("p (h c) -> p h c", h=20)
                st = stat[:, t * 20:t * 20 + 20]
                do(TT(sq, qk, qk, ALU.mult))
                do(dve.tensor_reduce(st, sq, AX, ALU.add), ss_ready)
                await_next(std_ready)
                do(dve.reciprocal(st, st))
                do(TT(qk, qk, st.unsqueeze(2).broadcast_to((P, 20, HD)), ALU.mult))
                for lo, n, g in ((0, NH, "qg"), (NH, NKV, "kg")):
                    o = qk[:, lo:lo + n, :]
                    do(TT(o, o, ROW(g).unsqueeze(1).broadcast_to((P, n, HD)), ALU.mult))
                kn = qk[:, NH:20, :]
                if t < XT:
                    half = lambda v, j: v.rearrange("p h (r z c) -> p h r z c", r=2, z=2)[:, :, :, j, :]
                    x1, x2, o1, o2 = half(qk, 0), half(qk, 1), half(sq, 0), half(sq, 1)
                    tab = lambda f: C(f, t * 32, 32).rearrange("p (r c) -> p r c", r=2)
                    for r in range(2):
                        cs = [tab(f)[:, r, :].unsqueeze(1).broadcast_to((P, 20, 16)) for f in ("cos", "sin")]
                        tmp = PT[:, 0, 0:320].rearrange("p (h c) -> p h c", h=20)
                        do(TT(o1[:, :, r, :], x1[:, :, r, :], cs[0], ALU.mult))
                        do(TT(tmp, x2[:, :, r, :], cs[1], ALU.mult))
                        do(TT(o1[:, :, r, :], o1[:, :, r, :], tmp, ALU.subtract))
                        do(TT(o2[:, :, r, :], x1[:, :, r, :], cs[1], ALU.mult))
                        do(TT(tmp, x2[:, :, r, :], cs[0], ALU.mult))
                        do(TT(o2[:, :, r, :], o2[:, :, r, :], tmp, ALU.add))
                    kn = sq[:, NH:20, :]
                kd = sbt[:, 1280:1792].rearrange("p (g z c) -> p g z c", g=NKV, z=2)
                do(dve.tensor_copy(kd[:, :, 0, :], kn))
                do(dve.tensor_copy(kd[:, :, 1, :], kn), qk_ready)

            attention(ATT0, lambda i: ada2(*ADA_BETWEEN[i]))
            residual("wo0", ALL, GATE[(0, 0)])
            signal(gates_read)
            ffn(0, NT)

            coefs(1, 0)
            rms("h1", ALL)
            lbs, oml, ex = stat[:, 160:168], stat[:, 168:176], stat[:, 176:192]
            l2 = COL("lb").rearrange("p (l k) -> p l k", l=2)
            do(TT(lbs, l2[:, 0, :], l2[:, 1, :], ALU.max))
            do(TT(ex.rearrange("p (l k) -> p l k", l=2), l2, lbs.unsqueeze(1).broadcast_to((P, 2, 8)), ALU.subtract),
               lb_ready)
            await_next(exp_lb)
            do(TT(oml, ex[:, 0:8], ex[:, 8:16], ALU.add))
            do(dve.reciprocal(oml, oml))
            do(TT(lbs, ex[:, 8:16], oml, ALU.mult))
            do(dve.tensor_scalar(oml, lbs, -1.0, 1.0, ALU.mult, ALU.add))
            await_next(hx_high_ready)
            do(TT(hx_low[:, :, :], hT[:, :, :], hx_high[:, :, :].bitcast(F32), ALU.subtract), hx_low_ready)
            for j, (key, z) in enumerate(HALVES):
                raw = ring_col(slot_of[unit_no[key]], 256 * z, 256)
                await_next(hw_high_ready)
                do(TT(hw_low[:, slot_of[unit_no[key]], :, 256 * z:256 * z + 256], raw,
                      hw_high[j % 2][:, :, :].bitcast(F32), ALU.subtract), hw_low_ready)
            pe_past(("hf", 0, 0, 3))
            for v in (*QL, rK):
                do(dve.memset(v[:, :, :], 0.0))
            def scale_forget(d, b):
                await_next(sig_ready)
                for i in range(4):
                    h = 4 * b + i
                    do(dve.tensor_scalar(rks[b][:, i, :], rks[b][:, i, :], oml[:, h:h + 1], lbs[:, h:h + 1],
                                         ALU.mult, ALU.add), forget_ready if i == 3 else dve_step)

            def running_sums(d, b):
                await_next(state_k)
                do(dve.tensor_scalar(rks[b][:, :, :], rks[b][:, :, :], -1.0, 1.0, ALU.mult, ALU.add))
                for i in range(4):
                    for lo in (0, SEQ):
                        v = (lambda x: x[:, i, lo:lo + SEQ]) if d == 0 else \
                            (lambda x: x[:, i, lo:lo + SEQ][:, ::-1])
                        do(dve.tensor_tensor_scan(v(rbs[b]), C("ones", 0, 1).broadcast_to((P, SEQ)), v(rlog), 0.0,
                                                  ALU.mult, ALU.add), sums_ready if (i, lo) == (3, SEQ) else dve_step)

            def decay_keys(d, b):
                await_next(kexp_ready)
                do(TT(kdec, kdec, rks[b][:, :, SEQ:TOK], ALU.mult), kdec_ready)

            def sub(d, b, n):
                h = LEVELS[n] if n < NL else P
                ref = h - 1 if d == 0 else h
                v = rbs[b][:, :, 0:SEQ].rearrange("p i (n c) -> p i n c", c=2 * h)
                o = EL[n % 2].rearrange("p i (n c) -> p i n c", c=2 * h)
                do(TT(o, v, v[:, :, :, ref:ref + 1].broadcast_to((P, 4, SEQ // (2 * h), 2 * h)), ALU.subtract),
                   diff_ready)

            for step in (scale_forget, running_sums, decay_keys):
                step(0, 0)
            sub(0, 0, 0)
            for d in range(2):
                for b in range(2):
                    kx, qx = rks[b][:, :, 0:SEQ], rq[:, 4 * b:4 * b + 4, :]

                    def scale(n):
                        h = LEVELS[n] if n < NL else P
                        await_next(exp_ready)
                        if n >= 2:
                            pe_past(("lev", d, b, n - 2, 1))
                        le = [late_early(v, h, d) for v in (EL[n % 2], QL[n % 2], KL[n % 2], qx, kx)]
                        do(TT(le[1][0], le[3][0], le[0][0], ALU.mult))
                        do(TT(le[2][1], le[4][1], le[0][1], ALU.mult), qk_scaled)

                    def keep(n):
                        for t in ([0] if n == NL else XS):
                            ps = take(("lev", d, b, n, t))[:, :].rearrange("p (i c) -> p i c", i=4)
                            if n == NL:
                                do(dve.tensor_copy(rC[:, :, :], ps), F)
                            elif n < 0:
                                do(TT(rA[:, t, :, :], ps, ident.unsqueeze(1).broadcast_to((P, 4, P)), ALU.mult), F)
                            else:
                                at = (d * NL + n) * P
                                m = masks[:, at:at + P].unsqueeze(1).broadcast_to((P, 4, P))
                                do(dve.copy_predicated(rA[:, t, :, :], m, ps), F)

                    for n in range(NL + 1):
                        if n < NL:
                            sub(d, b, n + 1)
                        if after(d, b) and n == 5:
                            scale_forget(*after(d, b))
                        scale(n)
                        keep(n - 1)
                        if after(d, b) and n == 6:
                            running_sums(*after(d, b))
                    signal(diff_ready)
                    await_next(exp_ready)
                    n = NL + 1
                    pe_past(("lev", d, b, n - 2, 1))
                    do(TT(QL[n % 2], qx, EL[n % 2], ALU.mult), qk_scaled)
                    keep(NL)
                    signal(o_ready)
                    if after(d, b):
                        sub(*after(d, b), 0)
                        decay_keys(*after(d, b))
                    for t in XS:
                        ps = take(("ro", d, b, t))
                        o = ro[:, t, b * 512:(b + 1) * 512]
                        if d == 0:
                            do(dve.tensor_copy(o, ps[:, :]), F)
                        else:
                            do(TT(o, o, ps[:, :], ALU.add), F)
            for t in XS:
                o = ro[:, t, :].rearrange("p (h c) -> p h c", h=HG)
                sq = xn[:, t, :].rearrange("p (h c) -> p h c", h=HG)
                st = stat[:, t * 8:t * 8 + 8]
                do(TT(sq, o, o, ALU.mult))
                do(dve.tensor_reduce(st, sq, AX, ALU.add), ss_ready)
                await_next(std_ready)
                do(dve.reciprocal(st, st))
                do(TT(o, o, st.unsqueeze(2).broadcast_to((P, HG, P)), ALU.mult))
                do(TT(o, o, ROW("og").unsqueeze(1).broadcast_to((P, HG, P)), ALU.mult))
                do(TT(ro[:, t, :], ro[:, t, :], rg[:, t, :], ALU.mult))
            signal(o_ready)
            residual("wo1", XS, GATE[(1, 0)])
            ffn(1, XT)
            signal(x2_ready)
            pe_past(("down", 1, XT - 1, 1))
            for v, n in ((aK, 6), (bK, 2)):
                for z in range(2):
                    do(dve.memset(v[64 * z:64 * z + 64, 1 - z::2, :], 0.0),
                       zeros_ready if (n, z) == (2, 1) else dve_step)
            await_next(x2_high_ready)
            do(TT(x2_low[:, :, :], hT[:, :, 0:SEQ], x2_high.bitcast(F32), ALU.subtract), x2_low_ready)
            for j, (u, z) in enumerate(W_HALVES):
                slot = slot_of[unit_no[("w2", u)]]
                await_next(w2_high_ready)
                do(TT(hw_low[:, slot, :, 256 * z:256 * z + 256], ring_col(slot, 256 * z, 256),
                      w2_high[j % 3][:, :, :].bitcast(F32), ALU.subtract), w2_low_ready)
            attention(ATT2, lambda i: None)
            for b in range(2):
                for t in XS:
                    tmp = xn[:, 0, 0:512]
                    o, o2 = (v[:, t, b * 512:(b + 1) * 512] for v in (ga, gb2))
                    do(TT(o, o, take(("pa", b, t))[:, :], ALU.mult), F)
                    do(TT(tmp, o2, take(("pb", b, t))[:, :], ALU.mult), F)
                    do(TT(o, o, tmp, ALU.add))
            signal(merged_ready)
            for b in range(2):
                for t in XS:
                    ps = take(("wo2", b, t))
                    o = xr[:, t, b * 512:(b + 1) * 512]
                    do(STT(out=o, in0=o, scalar=ALPHA, in1=ps[:, :], op0=ALU.mult, op1=ALU.add), F)

            def layer_norm(src, g, after):
                for t in XS:
                    v, o, st = src[:, t, :], xr[:, t, :], stat[:, t:t + 1]
                    do(dve.tensor_reduce(st, v, AX, ALU.add))
                    do(dve.tensor_scalar(st, st, -1.0 / D, None, ALU.mult))
                    do(dve.tensor_scalar(o, v, st, None, ALU.add))
                    do(dve.tensor_tensor_reduce(out=xn[:, 0, :], in0=o, in1=o, scale=1.0, scalar=0.0, op0=ALU.mult,
                                                op1=ALU.add, accum_out=st), ss_ready)
                    await_next(std_ready)
                    do(dve.reciprocal(st, st))
                    do(STT(out=o, in0=o, scalar=st, in1=gb[:, g, :], op0=ALU.mult, op1=ALU.mult))
                    do(TT(o, o, gb[:, g + 1, :], ALU.add))
                signal(after)

            dve.wait_ge(ln_landed, 64)
            layer_norm(xr, 0, y_ready)
            do(dve.memset(lgx[:, :, :], -3e38))
            for t in XS:
                do(dve.tensor_scalar(acc[:, t, :], xr[:, t, :], ALPHA, None, ALU.mult))
            do(dve.memset(table[:, :, :], 0.0))
            ps = take(("route",))
            do(TT(lgx[:, :, 0:E], ps[:, 0:2 * E].rearrange("p (t e) -> p t e", t=2),
                  ROW("rb").unsqueeze(1).broadcast_to((P, 2, E)), ALU.add), F)
            for t in XS:
                do(dve.max(out=top[:, t, :], in_=lgx[:, t, :]))
            do(dve.tensor_scalar(tst[:, 0:2], top[:, :, 0], -1.0, None, ALU.mult), route_max)
            do(dve.memset(top[:, :, 4:8], -3e38))
            for t in XS:
                do(dve.match_replace(out=pick[:, t, :], in_to_replace=top[:, t, :], in_values=lgx[:, t, :],
                                     imm_value=3e38))
            do(dve.tensor_scalar(chosen[:, :, :], pick[:, :, 0:E], 3e38, None, ALU.is_equal), route_ready)
            await_next(gate_exp)
            do(TT(gate[:, :, :], gate[:, :, :], chosen[:, :, :], ALU.mult))
            do(dve.tensor_reduce(tst[:, 2:4], gate[:, :, :], AX, ALU.add))
            do(dve.reciprocal(tst[:, 2:4], tst[:, 2:4]))
            do(TT(gate[:, :, :], gate[:, :, :], tst[:, 2:4].unsqueeze(2).broadcast_to((P, 2, E)), ALU.mult))
            ps = take(("rank",))
            do(dve.tensor_copy(rank[:, :, :], ps[:, 0:3 * E].rearrange("p (t e) -> p t e", t=3)), F)
            for j, v in enumerate((rank, chosen, gate)):
                do(dve.tensor_copy(table[:, 0:E, 2 * j:2 * j + 2], v[:, 0:2, :].rearrange("p t e -> p e t")))
            LINKS = 7

            def chain(at):
                n = [0]

                def link(ins):
                    n[0] += 1
                    ins.then_inc(dve_link, 1)
                    dve.wait_ge(dve_link, at + n[0])

                return link, n

            def select(e, link, first=None):
                link(dve.tensor_copy(cur[:, 0:6], table[:, bass.ds(e, 1), :].rearrange("p e c -> p (e c)")))
                if first is None:
                    link(dve.tensor_copy(cur[:, 6:8], cur[:, 0:2]))
                else:
                    link(dve.tensor_scalar(cur[:, 6:8], cur[:, 0:2], first, None, ALU.subtract))
                for t in XS:
                    for dst, c in ((sel, 2 + t), (selg, 4 + t)):
                        ins = dve.tensor_scalar(dst[:, t, :], C("slot"), cur[:, 6 + t:7 + t], cur[:, c:c + 1],
                                                ALU.is_equal, ALU.mult)
                        if t == 0:
                            link(ins)
                        elif dst is sel:
                            link(ins)
                        else:
                            ins.then_inc(sel_ready, 1)

            def item(i, ahead, select_next):
                link, n = chain(LINK0 + i * LINKS + ahead * 2 * 5)
                dve.wait_ge(gg_ready, i + 1)
                dve.tensor_scalar(hm[:, :], PS[0][:, :], 7.0, None, ALU.min).then_inc(hm_ready, 1)
                dve.wait_ge(gu_ready, i + 1)
                link(dve.tensor_scalar(um[:, :], PS[1][:, :], 7.0, -7.0, ALU.min, ALU.max))
                dve.wait_ge(sg_ready, i + 1)
                link(TT(hm[:, :], hm[:, :], sg[:, :], ALU.mult))
                STT(out=hh[:, :], in0=um[:, :], scalar=1.0, in1=hm[:, :], op0=ALU.add, op1=ALU.mult)\
                    .then_inc(hh_ready, 1)
                for j in range(4):
                    h, t = j // 2, j % 2
                    dve.wait_ge(c_ready, 4 * i + j + 1)
                    o = acc[:, t, h * 512:(h + 1) * 512]
                    TT(o, o, PS[6 + t][:, :], ALU.add).then_inc(c_added, 1)
                dve.wait_ge(c_added, 4 * i + 5)
                dve.wait_ge(gx_ready, i + 2 + ahead)
                dve.wait_ge(gt_ready, i + 2 + ahead)
                select_next(link)
                assert n[0] == LINKS

            signal(c_added)
            for e in range(2):
                if e:
                    dve.wait_ge(gx_ready, 1)
                    dve.wait_ge(gt_ready, 1)
                link, n = chain(5 * e)
                select(e, link)
                assert n[0] == 5
            do(dve.tensor_scalar(extra[:, 0, :], rank[:, 2, :], float(SLOTS), None, ALU.is_gt))
            for k in range(2, PASSES):
                do(STT(out=extra[:, 0, :], in0=rank[:, 2, :], scalar=float(k * SLOTS), in1=extra[:, 0, :],
                       op0=ALU.is_gt, op1=ALU.add))
            do(dve.tensor_tensor_scan(extra[:, 1, :], C("ones", 0, E), extra[:, 0, :], 0.0, ALU.mult, ALU.add))
            bc = lambda v: v.unsqueeze(1).broadcast_to((P, ITEMS + 2, E))
            it = C("item")
            do(TT(wide, bc(extra[:, 1, :]), it.unsqueeze(2).broadcast_to((P, ITEMS + 2, E)), ALU.is_le))
            do(dve.tensor_reduce(far[:, 0, :], wide, AX, ALU.add))
            do(TT(wide, wide, bc(extra[:, 0, :]), ALU.mult))
            do(dve.tensor_reduce(far[:, 1, :], wide, AX, ALU.add))
            do(TT(far[:, 1, :], it, far[:, 1, :], ALU.subtract))
            do(dve.tensor_scalar(far[:, 1, :], far[:, 1, :], 1.0, float(SLOTS), ALU.add, ALU.mult))
            do(dve.tensor_scalar(fari, far[:, 0, :], float(E - 1), None, ALU.min))
            do(dve.tensor_copy(nfar, extra[:, 1, E - 1:E]), rank_ready)

            LINK0 = 10
            with dve.Fori(0, E) as i:
                item(i, 0, lambda link: select(i + 2, link))

            def far_select(j, link):
                select(far_item(dve, j), link, far[:, 1, bass.ds(j, 1)])

            def first_further():
                dve.wait_ge(sel_ready, E + 2)
                for j in range(2):
                    dve.wait_ge(gx_ready, E + 1 + j)
                    dve.wait_ge(gt_ready, E + 1 + j)
                    far_select(j, chain(LINK0 + E * LINKS + 5 * j)[0])

            further(dve, lambda j: item(j + E, 1, lambda link: far_select(j + 2, link)), first_further)
            layer_norm(acc, 2, out_ready)




def _rows(inputs):
    f = {k: np.asarray(v) for k, v in inputs.items()}

    def col(v):
        v = v.reshape(-1, P)
        return v.T

    cc = np.stack([f["c"][0].reshape(KC, P), f["c_ctx"].reshape(KC, P)], 1)
    cols = np.concatenate([col(f["norm1_g"]), col(f["norm2_g"]), col(f["ada_b"]), col(f["ffn_conv_w"]),
                           col(f["ffn_conv_b"]), col(f["hgrn_lb_logits"]), col(cc)], 1)
    rows = np.concatenate([f["attn_q_gain"][0], f["attn_k_gain"][0], f["attn_sink"][0], f["hgrn_o_gain"][0],
                           f["sinks_2"][0], f["router_b_2"][0]])
    const, masks = constants()
    big = {k: f[k] for k in BIG}
    return {"cols": np.ascontiguousarray(cols), "rows": np.ascontiguousarray(rows), "const": const, "masks": masks, **big}


BIG = ["x", "ctx", "ada_w", "ada_b", "attn_w_in", "attn_w_out", "hgrn_w_in", "hgrn_w_out", "ffn_w_up", "ffn_w_down",
       "w_in_2", "w_proj_a_2", "w_proj_b_2", "w_out_2", "ln1_g_2", "ln1_b_2", "router_w_2", "w_gate_2", "b_gate_2",
       "w_up_2", "b_up_2", "w_down_2", "b_down_2", "ln2_g_2", "ln2_b_2"]


def kernel(**inputs):
    import concourse.bacc as bacc
    from concourse.bass_utils import run_bass_kernel_spmd as run

    nc = bacc.Bacc("TRN2", target_bir_lowering=False, num_devices=1)
    arrays, args = {}, {}
    for name, v in _rows(inputs).items():
        v = np.ascontiguousarray(v)
        arrays["in_" + name] = v
        args[name] = nc.dram_tensor("in_" + name, v.shape, mybir.dt.from_np(v.dtype), kind="ExternalInput").ap()
    out = nc.dram_tensor("out", (1, SEQ, D), F32, kind="ExternalOutput").ap()
    program(nc, args, out)
    r = run(nc, [arrays], core_ids=[0])
    return r.results[0]["out"]
```
